# Optimizing a Trainium2 kernel written in Bass

```python
import math
import jax, jax.numpy as jnp
from jax import lax
import numpy as np

D_MODEL = 1024
BATCH = 1
SEQ = 512
DEPTH = 1

HEAD_DIM = 64
SB_HEADS = (D_MODEL // 2) // HEAD_DIM
DIFF_HEADS = (D_MODEL // 2) // (2 * HEAD_DIM)
SB_WIDTH = SB_HEADS * HEAD_DIM
DIFF_WIDTH = DIFF_HEADS * 2 * HEAD_DIM
MIX_WIDTH = SB_WIDTH + DIFF_WIDTH
IN_WIDTH = 3 * MIX_WIDTH
D_FF = -(-8 * D_MODEL // (3 * 256)) * 256
Q_BLOCK = 128
ROPE_THETA = 10000.0
NORM_EPS = 1e-6
SUBLN_EPS = 1e-5


def rmsnorm(x, g, eps=NORM_EPS):
    xf = x.astype(jnp.float32)
    y = xf * lax.rsqrt(jnp.mean(xf * xf, axis=-1, keepdims=True) + eps) * g.astype(jnp.float32)
    return y.astype(x.dtype)

def rope(x, pos):
    half = HEAD_DIM // 2
    inv_freq = ROPE_THETA ** (-jnp.arange(half, dtype=jnp.float32) / half)
    ang = pos.astype(jnp.float32)[:, None] * inv_freq[None, :]
    cos, sin = jnp.cos(ang), jnp.sin(ang)
    xf = x.astype(jnp.float32)
    x1, x2 = xf[..., :half], xf[..., half:]
    return jnp.concatenate([x1 * cos - x2 * sin, x1 * sin + x2 * cos], axis=-1).astype(x.dtype)

def stick_breaking_attention(q, k, v):
    S = q.shape[2]
    scale = HEAD_DIM ** -0.5
    outs = []
    for start in range(0, S, Q_BLOCK):
        end = start + Q_BLOCK
        z = jnp.einsum('bhqd,bhkd->bhqk', q[:, :, start:end], k[:, :, :end]).astype(jnp.float32) * scale
        past = jnp.arange(end)[None, :] < jnp.arange(start, end)[:, None]
        log_beta = jax.nn.log_sigmoid(z)
        log_1m = jnp.where(past, jax.nn.log_sigmoid(-z), 0.0)
        acc = lax.cumsum(log_1m, axis=3, reverse=True) - log_1m
        w = jnp.where(past, jnp.exp(log_beta + acc), 0.0)
        outs.append(jnp.einsum('bhqk,bhkd->bhqd', w.astype(v.dtype), v[:, :, :end]))
    return jnp.concatenate(outs, axis=2)

def differential_attention(q, k, v, lam):
    S = q.shape[3]
    scale = HEAD_DIM ** -0.5
    outs = []
    for start in range(0, S, Q_BLOCK):
        end = start + Q_BLOCK
        s = jnp.einsum('bhcqd,bhckd->bhcqk', q[:, :, :, start:end], k[:, :, :, :end]).astype(jnp.float32) * scale
        causal = jnp.arange(end)[None, :] <= jnp.arange(start, end)[:, None]
        p = jax.nn.softmax(jnp.where(causal, s, -jnp.inf), axis=-1)
        a = p[:, :, 0] - lam * p[:, :, 1]
        outs.append(jnp.einsum('bhqk,bhkd->bhqd', a.astype(v.dtype), v[:, :, :end]))
    return jnp.concatenate(outs, axis=2)

def first_inputs(seed: int = 0) -> dict:
    key = jax.random.key(seed)
    ks = jax.random.split(key, 16)
    f32 = jnp.float32
    nrm = lambda k, shape, s: jax.random.normal(k, shape, f32) * s
    return {
        "x": nrm(ks[0], (BATCH, SEQ, D_MODEL), 1.0),
        "attn_norm_g": 1.0 + nrm(ks[1], (DEPTH, D_MODEL), 0.02),
        "w_in": nrm(ks[2], (DEPTH, D_MODEL, IN_WIDTH), D_MODEL ** -0.5),
        "diff_q_norm_g": 1.0 + nrm(ks[3], (DEPTH, HEAD_DIM), 0.02),
        "diff_k_norm_g": 1.0 + nrm(ks[4], (DEPTH, HEAD_DIM), 0.02),
        "lambda_q1": nrm(ks[5], (DEPTH, HEAD_DIM), 0.1),
        "lambda_k1": nrm(ks[6], (DEPTH, HEAD_DIM), 0.1),
        "lambda_q2": nrm(ks[7], (DEPTH, HEAD_DIM), 0.1),
        "lambda_k2": nrm(ks[8], (DEPTH, HEAD_DIM), 0.1),
        "diff_subln_g": 1.0 + nrm(ks[9], (DEPTH, 2 * HEAD_DIM), 0.02),
        "w_o": nrm(ks[10], (DEPTH, MIX_WIDTH, D_MODEL), MIX_WIDTH ** -0.5),
        "ffn_norm_g": 1.0 + nrm(ks[11], (DEPTH, D_MODEL), 0.02),
        "w_gate": nrm(ks[12], (DEPTH, D_MODEL, D_FF), D_MODEL ** -0.5),
        "w_up": nrm(ks[13], (DEPTH, D_MODEL, D_FF), D_MODEL ** -0.5),
        "w_down": nrm(ks[14], (DEPTH, D_FF, D_MODEL), D_FF ** -0.5),
    }

def first_block(x, attn_norm_g, w_in, diff_q_norm_g, diff_k_norm_g, lambda_q1, lambda_k1,
              lambda_q2, lambda_k2, diff_subln_g, w_o, ffn_norm_g, w_gate, w_up, w_down):
    B, S, _ = x.shape
    pos = jnp.arange(S, dtype=jnp.int32)
    for layer in range(DEPTH):
        lambda_init = 0.8 - 0.6 * math.exp(-0.3 * layer)
        h = rmsnorm(x, attn_norm_g[layer])
        proj = h @ w_in[layer]
        sb_q, sb_k, sb_v, d_q, d_k, d_v = jnp.split(
            proj, [SB_WIDTH, 2 * SB_WIDTH, 3 * SB_WIDTH,
                   3 * SB_WIDTH + DIFF_WIDTH, 3 * SB_WIDTH + 2 * DIFF_WIDTH], axis=-1)

        to_heads = lambda t: t.reshape(B, S, SB_HEADS, HEAD_DIM).transpose(0, 2, 1, 3)
        sb_out = stick_breaking_attention(to_heads(sb_q), to_heads(sb_k), to_heads(sb_v))
        sb_out = sb_out.transpose(0, 2, 1, 3).reshape(B, S, SB_WIDTH)

        to_pair = lambda t: t.reshape(B, S, DIFF_HEADS, 2, HEAD_DIM).transpose(0, 2, 3, 1, 4)
        dq = rope(rmsnorm(to_pair(d_q), diff_q_norm_g[layer]), pos)
        dk = rope(rmsnorm(to_pair(d_k), diff_k_norm_g[layer]), pos)
        dv = d_v.reshape(B, S, DIFF_HEADS, 2 * HEAD_DIM).transpose(0, 2, 1, 3)
        lam = (jnp.exp(jnp.sum(lambda_q1[layer].astype(jnp.float32) * lambda_k1[layer].astype(jnp.float32)))
               - jnp.exp(jnp.sum(lambda_q2[layer].astype(jnp.float32) * lambda_k2[layer].astype(jnp.float32)))
               + lambda_init)
        d_out = differential_attention(dq, dk, dv, lam)
        d_out = rmsnorm(d_out, diff_subln_g[layer], SUBLN_EPS) * (1.0 - lambda_init)
        d_out = d_out.transpose(0, 2, 1, 3).reshape(B, S, DIFF_WIDTH)

        mix = jnp.concatenate([sb_out, d_out.astype(sb_out.dtype)], axis=-1)
        x = x + mix @ w_o[layer]

        h2 = rmsnorm(x, ffn_norm_g[layer])
        x = x + (jax.nn.silu(h2 @ w_gate[layer]) * (h2 @ w_up[layer])) @ w_down[layer]
    return x


N_META = 16
CHUNK = 128
PAD = CHUNK - N_META
CONF_WIDTH = D_MODEL
CONF_KERNEL = 31
SSM_INNER = 2 * D_MODEL
SSM_HEAD_DIM = 64
SSM_HEADS = SSM_INNER // SSM_HEAD_DIM
SSM_GROUPS = 4
SSM_STATE = 128
SSM_CONV = 7
XBC_WIDTH = SSM_INNER + 2 * SSM_GROUPS * SSM_STATE
N_BRANCHES = 2
N_EXPERTS = 16
CAPACITY_FACTOR = 2
EXPERT_FF = 2 * D_MODEL
OFF_CONF = 0
OFF_Z = OFF_CONF + 2 * CONF_WIDTH
OFF_XBC = OFF_Z + SSM_INNER
OFF_DT = OFF_XBC + XBC_WIDTH
OFF_GATE = OFF_DT + 2 * SSM_HEADS
IN_WIDTH_2 = OFF_GATE + N_BRANCHES * D_MODEL
EPS = 1e-6


def rms_norm(x, w):
    xf = x.astype(jnp.float32)
    y = xf * lax.rsqrt(jnp.mean(xf * xf, axis=-1, keepdims=True) + EPS)
    return (y * w.astype(jnp.float32)).astype(x.dtype)

def layer_norm(x, g, b):
    xf = x.astype(jnp.float32)
    mu = jnp.mean(xf, axis=-1, keepdims=True)
    var = jnp.mean(jnp.square(xf - mu), axis=-1, keepdims=True)
    y = (xf - mu) * lax.rsqrt(var + EPS)
    return (y * g.astype(jnp.float32) + b.astype(jnp.float32)).astype(x.dtype)

def depthwise_conv(x, w, b):
    y = lax.conv_general_dilated(x, w[:, None, :].astype(x.dtype), window_strides=(1,), padding='SAME',
                                 dimension_numbers=('NWC', 'WIO', 'NWC'), feature_group_count=x.shape[-1])
    return y + b.astype(x.dtype)

def pad_front(a):
    return jnp.pad(a, [(0, 0), (PAD, 0)] + [(0, 0)] * (a.ndim - 2))

def ssd_scan(x, dt, A, B, C):
    b, T, h, p = x.shape
    g, n = B.shape[2], B.shape[3]
    j = h // g
    c = T // CHUNK
    xd = (x * dt[..., None]).reshape(b, c, CHUNK, g, j, p)
    a = jnp.moveaxis((dt * A).reshape(b, c, CHUNK, g, j), 2, -1)
    a_cs = jnp.cumsum(a, axis=-1)
    Bc = B.reshape(b, c, CHUNK, g, n)
    Cc = C.reshape(b, c, CHUNK, g, n)
    seg = a_cs[..., :, None] - a_cs[..., None, :]
    mask = jnp.tril(jnp.ones((CHUNK, CHUNK), dtype=bool))
    decay = jnp.exp(jnp.where(mask, seg, -jnp.inf))
    cb = jnp.einsum('bclgn,bcsgn->bcgls', Cc, Bc)
    y_diag = jnp.einsum('bcgls,bcgjls,bcsgjp->bclgjp', cb, decay, xd)
    decay_to_end = jnp.exp(a_cs[..., -1:] - a_cs)
    states = jnp.einsum('bclgn,bcgjl,bclgjp->bcgjpn', Bc, decay_to_end, xd)
    chunk_decay = jnp.exp(a_cs[..., -1])

    def step(carry, inp):
        st, dec = inp
        return carry * dec[..., None, None] + st, carry

    init = jnp.zeros((b, g, j, p, n), dtype=states.dtype)
    _, prev = lax.scan(step, init, (jnp.moveaxis(states, 1, 0), jnp.moveaxis(chunk_decay, 1, 0)))
    prev = jnp.moveaxis(prev, 0, 1)
    y_off = jnp.einsum('bclgn,bcgjpn,bcgjl->bclgjp', Cc, prev, jnp.exp(a_cs))
    return (y_diag + y_off).reshape(b, T, h, p)

def bidir_ssd(xs, dt_raw, dt_bias, a_log, Bs, Cs, d_skip):
    f32 = jnp.float32
    xf, Bf, Cf = xs.astype(f32), Bs.astype(f32), Cs.astype(f32)
    dtr = dt_raw.astype(f32)
    dt_f = jax.nn.softplus(dtr[..., :SSM_HEADS] + dt_bias[0].astype(f32))
    dt_b = jax.nn.softplus(dtr[..., SSM_HEADS:] + dt_bias[1].astype(f32))
    A = -jnp.exp(a_log.astype(f32))
    xp, Bp, Cp = pad_front(xf), pad_front(Bf), pad_front(Cf)
    y_f = ssd_scan(xp, pad_front(dt_f), A[0], Bp, Cp)
    fl = lambda t: jnp.flip(t, axis=1)
    y_b = fl(ssd_scan(fl(xp), fl(pad_front(dt_b)), A[1], fl(Bp), fl(Cp)))
    y = (y_f + y_b)[:, PAD:] + d_skip.astype(f32)[:, None] * xf
    return y.astype(xs.dtype)

def expert_choice_ffn(xn, w_router, w_gate, w_up, w_down):
    b, T, d = xn.shape
    cap = CAPACITY_FACTOR * T // N_EXPERTS
    aff = jax.nn.softmax(jnp.einsum('btd,de->bte', xn, w_router).astype(jnp.float32), axis=-1)
    top_aff, top_idx = lax.top_k(jnp.swapaxes(aff, 1, 2), cap)
    bi = jnp.arange(b)[:, None, None]
    xg = xn[bi, top_idx]
    hg = jnp.einsum('becd,edf->becf', xg, w_gate)
    hu = jnp.einsum('becd,edf->becf', xg, w_up)
    y = jnp.einsum('becf,efd->becd', jax.nn.silu(hg) * hu, w_down)
    y = y * top_aff[..., None].astype(y.dtype)
    return jnp.zeros_like(xn).at[bi, top_idx].add(y)

def second_inputs(seed: int = 0) -> dict:
    key = jax.random.key(seed)
    ks = jax.random.split(key, 24)
    f32 = jnp.float32
    nrm = lambda k, shape, scale: jax.random.normal(k, shape, f32) * scale
    gain = lambda k, shape: 1.0 + 0.02 * jax.random.normal(k, shape, f32)
    L = DEPTH
    dt0 = jnp.exp(jax.random.uniform(ks[10], (L, 2, SSM_HEADS), f32, np.log(1e-3), np.log(1e-1)))
    dt_bias = dt0 + jnp.log(-jnp.expm1(-dt0))
    a_log = jnp.log(jax.random.uniform(ks[11], (L, 2, SSM_HEADS), f32, 1.0, 16.0))
    return {
        "x": jax.random.normal(ks[0], (BATCH, SEQ, D_MODEL), f32),
        "meta_tokens": nrm(ks[1], (N_META, D_MODEL), 1.0),
        "w_norm_mix": gain(ks[2], (L, D_MODEL)),
        "w_in": nrm(ks[3], (L, D_MODEL, IN_WIDTH_2), D_MODEL ** -0.5),
        "w_conf_dw": nrm(ks[4], (L, CONF_KERNEL, CONF_WIDTH), CONF_KERNEL ** -0.5),
        "b_conf_dw": nrm(ks[5], (L, CONF_WIDTH), 0.02),
        "conf_ln_g": gain(ks[6], (L, CONF_WIDTH)),
        "conf_ln_b": nrm(ks[7], (L, CONF_WIDTH), 0.02),
        "w_conf_out": nrm(ks[8], (L, CONF_WIDTH, D_MODEL), CONF_WIDTH ** -0.5),
        "w_ssm_conv": nrm(ks[9], (L, SSM_CONV, XBC_WIDTH), SSM_CONV ** -0.5),
        "b_ssm_conv": nrm(ks[12], (L, XBC_WIDTH), 0.02),
        "ssm_dt_bias": dt_bias,
        "ssm_a_log": a_log,
        "ssm_d": gain(ks[13], (L, SSM_HEADS)),
        "w_ssm_norm": gain(ks[14], (L, SSM_INNER)),
        "w_ssm_out": nrm(ks[15], (L, SSM_INNER, D_MODEL), SSM_INNER ** -0.5),
        "w_out": nrm(ks[16], (L, D_MODEL, D_MODEL), D_MODEL ** -0.5),
        "w_norm_ffn": gain(ks[17], (L, D_MODEL)),
        "w_router": nrm(ks[18], (L, D_MODEL, N_EXPERTS), D_MODEL ** -0.5),
        "w_exp_gate": nrm(ks[19], (L, N_EXPERTS, D_MODEL, EXPERT_FF), D_MODEL ** -0.5),
        "w_exp_up": nrm(ks[20], (L, N_EXPERTS, D_MODEL, EXPERT_FF), D_MODEL ** -0.5),
        "w_exp_down": nrm(ks[21], (L, N_EXPERTS, EXPERT_FF, D_MODEL), EXPERT_FF ** -0.5),
        "w_norm_final": gain(ks[22], (D_MODEL,)),
    }

def second_block(x, meta_tokens, w_norm_mix, w_in, w_conf_dw, b_conf_dw, conf_ln_g, conf_ln_b, w_conf_out,
              w_ssm_conv, b_ssm_conv, ssm_dt_bias, ssm_a_log, ssm_d, w_ssm_norm, w_ssm_out, w_out,
              w_norm_ffn, w_router, w_exp_gate, w_exp_up, w_exp_down, w_norm_final):
    b = x.shape[0]
    meta = jnp.broadcast_to(meta_tokens[None].astype(x.dtype), (b, N_META, D_MODEL))
    h = jnp.concatenate([meta, x], axis=1)
    Lt = h.shape[1]
    for l in range(DEPTH):
        u = rms_norm(h, w_norm_mix[l])
        proj = jnp.einsum('btd,dk->btk', u, w_in[l])
        conf_a = proj[..., OFF_CONF:OFF_CONF + CONF_WIDTH]
        conf_g = proj[..., OFF_CONF + CONF_WIDTH:OFF_Z]
        z = proj[..., OFF_Z:OFF_XBC]
        xbc = proj[..., OFF_XBC:OFF_DT]
        dt_raw = proj[..., OFF_DT:OFF_GATE]
        gates = jax.nn.sigmoid(proj[..., OFF_GATE:].astype(jnp.float32)).astype(h.dtype)

        c = conf_a * jax.nn.sigmoid(conf_g)
        c = depthwise_conv(c, w_conf_dw[l], b_conf_dw[l])
        c = jax.nn.silu(layer_norm(c, conf_ln_g[l], conf_ln_b[l]))
        branch_conf = jnp.einsum('btc,cd->btd', c, w_conf_out[l])

        xbc = jax.nn.silu(depthwise_conv(xbc, w_ssm_conv[l], b_ssm_conv[l]))
        xs = xbc[..., :SSM_INNER].reshape(b, Lt, SSM_HEADS, SSM_HEAD_DIM)
        Bs = xbc[..., SSM_INNER:SSM_INNER + SSM_GROUPS * SSM_STATE].reshape(b, Lt, SSM_GROUPS, SSM_STATE)
        Cs = xbc[..., SSM_INNER + SSM_GROUPS * SSM_STATE:].reshape(b, Lt, SSM_GROUPS, SSM_STATE)
        y = bidir_ssd(xs, dt_raw, ssm_dt_bias[l], ssm_a_log[l], Bs, Cs, ssm_d[l]).reshape(b, Lt, SSM_INNER)
        y = rms_norm(y * jax.nn.silu(z), w_ssm_norm[l])
        branch_ssm = jnp.einsum('btc,cd->btd', y, w_ssm_out[l])

        merged = gates[..., :D_MODEL] * branch_conf + gates[..., D_MODEL:] * branch_ssm
        h = h + jnp.einsum('btd,de->bte', merged, w_out[l])

        hn = rms_norm(h, w_norm_ffn[l])
        h = h + expert_choice_ffn(hn, w_router[l], w_exp_gate[l], w_exp_up[l], w_exp_down[l])
    return rms_norm(h[:, N_META:], w_norm_final)


def setup_inputs(seed=0):
    out = dict(first_inputs(seed))
    for name, value in second_inputs(seed + 1).items():
        if name != "x":
            out[name + "_2"] = value
    return out


def reference(
    x, attn_norm_g, w_in, diff_q_norm_g, diff_k_norm_g, lambda_q1, lambda_k1, lambda_q2,
    lambda_k2, diff_subln_g, w_o, ffn_norm_g, w_gate, w_up, w_down, meta_tokens_2, w_norm_mix_2,
    w_in_2, w_conf_dw_2, b_conf_dw_2, conf_ln_g_2, conf_ln_b_2, w_conf_out_2, w_ssm_conv_2,
    b_ssm_conv_2, ssm_dt_bias_2, ssm_a_log_2, ssm_d_2, w_ssm_norm_2, w_ssm_out_2, w_out_2,
    w_norm_ffn_2, w_router_2, w_exp_gate_2, w_exp_up_2, w_exp_down_2, w_norm_final_2,
):
    x = first_block(
        x, attn_norm_g, w_in, diff_q_norm_g, diff_k_norm_g, lambda_q1, lambda_k1, lambda_q2,
        lambda_k2, diff_subln_g, w_o, ffn_norm_g, w_gate, w_up, w_down,
    )
    return second_block(
        x, meta_tokens_2, w_norm_mix_2, w_in_2, w_conf_dw_2, b_conf_dw_2, conf_ln_g_2,
        conf_ln_b_2, w_conf_out_2, w_ssm_conv_2, b_ssm_conv_2, ssm_dt_bias_2, ssm_a_log_2,
        ssm_d_2, w_ssm_norm_2, w_ssm_out_2, w_out_2, w_norm_ffn_2, w_router_2, w_exp_gate_2,
        w_exp_up_2, w_exp_down_2, w_norm_final_2,
    )


_drawn_inputs = setup_inputs


def setup_inputs(seed=0):
    import zlib

    import numpy as np

    out = dict(_drawn_inputs(seed))
    spreads = {}
    factors = {'diff_q_norm_g': 3.395,
     'diff_k_norm_g': 3.938,
     'lambda_q1': 8.0,
     'diff_subln_g': 3.678,
     'ffn_norm_g': 3.42,
     'w_norm_mix_2': 3.529,
     'b_conf_dw_2': 4.931,
     'conf_ln_g_2': 6.998,
     'conf_ln_b_2': 7.933,
     'b_ssm_conv_2': 4.201,
     'ssm_d_2': 8.0,
     'w_ssm_norm_2': 6.086,
     'w_norm_ffn_2': 5.038,
     'w_norm_final_2': 2.958}
    for name, (base, spread) in spreads.items():
        noise = np.random.default_rng([zlib.crc32(name.encode()), seed]).standard_normal(out[name].shape)
        drawn = base * np.exp(spread * noise) if base else spread * noise
        out[name] = __import__('jax').numpy.asarray(drawn.astype(out[name].dtype))
    for name, factor in factors.items():
        out[name] = (out[name] * factor).astype(out[name].dtype)
    return out
```

```python
import math
from contextlib import ExitStack

import concourse.bass as bass
import numpy as np
from concourse import mybir

F32 = mybir.dt.float32
ALU = mybir.AluOpType
ACT = mybir.ActivationFunctionType
AX_X = mybir.AxisListType.X

P = 128
D = 1024
DT = D // P
SEQ = 512
META = 16
T2 = SEQ + META
HT = T2 // 2
HD = 64
QB = SEQ // P
SB_HEADS, DIFF_HEADS = 8, 4
FF = 2816
FFT = FF // P
CONF_TAPS, SSM_TAPS = 31, 7
INNER, GROUPS, STATE, HEADS = 2048, 4, 128, 32
GH = HEADS // GROUPS
OFF_G, OFF_Z = 1024, 2048
OFF_X = OFF_Z + INNER
OFF_B = OFF_X + INNER
OFF_C = OFF_B + GROUPS * STATE
OFF_DT = OFF_C + GROUPS * STATE
OFF_GATE = OFF_DT + 2 * HEADS
EXPERTS, EFF = 16, 2048
EFT = EFF // P
CAP = 2 * T2 // EXPERTS
CHUNKS = [(c * P, min(P, T2 - c * P)) for c in range(-(-T2 // P))]
NC = len(CHUNKS)
SLOT = 4096
RING = 4
BIG = 1e30
LAMBDA_INIT = 0.8 - 0.6 * math.exp(0.0)
EPS, SUBLN_EPS = 1e-6, 1e-5
TOPK_ROUNDS = -(-CAP // 8)

PARAMS = {}
CONSTS = {}


def _columns(table, sizes):
    at = 0
    for name, n in sizes:
        table[name] = at
        at += n
    return at


N_PARAMS = _columns(PARAMS, [
    ("attn_g", DT), ("ffn_g", DT), ("mix_g", DT), ("ffn2_g", DT), ("final_g", DT), ("subln_g", 1),
    ("q_g", 1), ("k_g", 1), ("lam", 4), ("conf_w", DT * CONF_TAPS), ("conf_b", DT), ("ln_g", DT),
    ("ln_b", DT), ("ssm_w", 24 * SSM_TAPS), ("ssm_b", 24), ("ssm_norm_g", 16), ("dt_bias", 1),
    ("a_log", 1), ("ssm_d", HEADS), ("router", DT * EXPERTS), ("eps", 1), ("subln_eps", 1), ("one", 1)])
N_CONSTS = _columns(CONSTS, [
    ("ident", P), ("ones", P), ("upper", P), ("lower", P), ("heads", P), ("rot", P), ("iota", CAP),
    ("causal", P)])


def program(nc, inp, out):
    ctx = ExitStack()
    with ctx:
        def sb(name, shape):
            return ctx.enter_context(nc.sbuf_tensor(name, shape, F32))

        sems = {}

        def S(name):
            if name not in sems:
                sems[name] = ctx.enter_context(nc.semaphore(name))
            return sems[name]

        H = sb("H", [P, DT, T2])
        U = sb("U", [P, DT, T2])
        ring = sb("ring", [P, RING, SLOT])
        consts = sb("consts_sb", [P, N_CONSTS])
        par = sb("par", [P, N_PARAMS])
        SQ = sb("SQ", [P, 2, T2])
        RS = sb("RS", [P, T2])
        small = sb("small", [P, 256])
        AR = 24200
        arena = sb("arena", [P, AR])
        PS = ctx.enter_context(nc.psum_tensor("PS", [P, 8, 512], F32))
        fr_dram = nc.dram_tensor("ssd_sums", [2 * HEADS, T2], F32).ap()
        h_dram = nc.dram_tensor("residual", [P, DT, T2], F32).ap()

        def area(sizes):
            at, views = 0, []
            for shape in sizes:
                n = int(np.prod(shape))
                v = arena[:, at:at + n]
                if len(shape) == 2:
                    v = v.rearrange("p (a b) -> p a b", a=shape[0])
                if len(shape) == 3:
                    v = v.rearrange("p (a b c) -> p a b c", a=shape[0], b=shape[1])
                views.append(v)
                at += n
            assert at <= AR, at
            return views

        def C(name, n=P):
            return consts[:, CONSTS[name]:CONSTS[name] + n]

        def pcol(name, i=0):
            return par[:, PARAMS[name] + i:PARAMS[name] + i + 1]

        ident, ones, upper, lower = C("ident"), C("ones"), C("upper"), C("lower")
        heads_ones, rot, iota, causal = C("heads"), C("rot"), C("iota", CAP), C("causal")

        def halves(T):
            return [(0, T)] if T <= 512 else [(0, HT), (HT, T2)]

        def ps(banks, T):
            return PS[:, banks[0], 0:T] if T <= 512 else PS[:, banks[0]:banks[0] + 2, 0:HT]

        def tok(ap, T):
            return ap if T <= 512 else ap.rearrange("p (h n) -> p h n", h=2)

        QK, V, MIX, COS, SIN, Z, SP = area([(16, SEQ), (QB, D), (DT, SEQ), (SEQ,), (SEQ,), (3, 1280), (2, 1280)])
        scr = arena[:, 17408:17408 + 6400]
        PR = scr[:, 0:2048].rearrange("p (b c n) -> p b c n", b=2, c=2)
        DA = scr[:, 2048:3072].rearrange("p (b n) -> p b n", b=2)
        DAT = scr[:, 3072:4096].rearrange("p (b n) -> p b n", b=2)
        DA2 = scr[:, 4096:5120].rearrange("p (b n) -> p b n", b=2)
        G, SG = area([(FFT, SEQ), (2, SEQ)])
        ZO = [0, 512, 1024, 896]
        (XS, BF, CF, BT, SNAP, YT, XP, CP, ST, M1, XW, YC, XD, YB, CBM, DTT, AAT, FT, EF, W2, ET) = area([
            (NC, 512), (T2,), (T2,), (NC, P), (4, 512), (16, T2), (2, T2 + SSM_TAPS - 1),
            (2, T2 + CONF_TAPS - 1), (2, 512), (GH, P), (2, 512), (512,), (512,), (512,), (2, P), (NC, 64),
            (NC, 64), (NC, 64), (NC, 64), (NC, 64), (NC, 64)])
        CACC = H
        CO = SQ
        SGB = RS
        FR = [[ring[:, 2 * b + d, 3072:4096].rearrange("p (h n) -> p h n", h=GH) for d in range(2)]
              for b in range(2)]
        MG = arena[:, 0:DT * T2].rearrange("p (a n) -> p a n", a=DT)
        GT = arena[:, 4224:4224 + 2 * T2].rearrange("p (a n) -> p a n", a=2)
        DTF = arena[:, 6304:6304 + 6 * T2].rearrange("p (a n) -> p a n", a=6)
        XNT, XG, HG, SIL, YF, YE, SAT, SE, SA, AFF, SLT, TK, TV = area([
            (NC, D), (DT, CAP), (EFT, CAP), (2, 4 * CAP), (DT, CAP), (D,), (T2,), (NC, CAP), (NC, CAP),
            (NC, EXPERTS), (NC, EXPERTS), (8, T2), (8 * TOPK_ROUNDS,)])
        AFS, SLS = small[:, 128:128 + NC], small[:, 136:136 + NC]

        loads = []

        def rows(w, k, lo, hi):
            return w[0:k * P, lo:hi].rearrange("(k p) n -> p k n", p=P)

        def block(name, *parts):
            at, put = 0, []
            for src in parts:
                k, n = src.shape[1], src.shape[2]
                put.append((at, k, n, src))
                at += k * n
            assert at <= SLOT
            loads.append((name, put))

        w1, w2 = inp["w_in"], inp["w_in_2"]
        for b in range(6):
            block(("in", b), rows(w1, DT, b * 512, b * 512 + 512))
        for b in range(2):
            block(("wo", b), rows(inp["w_o"], DT, b * 512, b * 512 + 512))
        for b in range(FFT // 2):
            block(("gu", b), rows(inp["w_gate"], DT, b * 256, b * 256 + 256),
                  rows(inp["w_up"], DT, b * 256, b * 256 + 256))
        for b in range(4):
            for kh in range(2):
                block(("down", b, kh), inp["w_down"][kh * 11 * P:(kh + 1) * 11 * P, b * 256:b * 256 + 256]
                      .rearrange("(k p) n -> p k n", p=P))
        block(("dt",), rows(w2, DT, OFF_DT, OFF_DT + 64))
        for g in range(GROUPS):
            for i in range(2):
                bc = (OFF_B, OFF_C)[i] + g * P
                block(("xbc", g, i), rows(w2, DT, OFF_X + g * 512 + i * 256, OFF_X + g * 512 + i * 256 + 256),
                      rows(w2, DT, bc, bc + P))
            for i in range(2):
                block(("z", g, i), rows(w2, DT, OFF_Z + g * 512 + i * 256, OFF_Z + g * 512 + i * 256 + 256))
            for i in range(2):
                u = 2 * g + i
                block(("conf", u), rows(w2, DT, u * P, u * P + P), rows(w2, DT, OFF_G + u * P, OFF_G + u * P + P))
        for b in range(2):
            block(("g1", b), rows(w2, DT, OFF_GATE + b * 512, OFF_GATE + b * 512 + 512))
            block(("co", b), rows(inp["w_conf_out_2"], DT, b * 512, b * 512 + 512))
        for b in range(4):
            block(("g2", b), rows(w2, DT, OFF_GATE + D + b * 256, OFF_GATE + D + b * 256 + 256))
            block(("so", b), rows(inp["w_ssm_out_2"], 16, b * 256, b * 256 + 256))
        for b in range(2):
            block(("out", b), rows(inp["w_out_2"], DT, b * 512, b * 512 + 512))
        N_DENSE = len(loads)
        where = {name: n for n, (name, _) in enumerate(loads)}
        landed, count = {}, [0] * RING
        for n, (name, put) in enumerate(loads):
            count[n % RING] += 16 * len(put)
            landed[name] = count[n % RING]
        RING0 = list(count)
        last_read = {}

        def slot(name, part=0):
            at, k, n, _ = loads[where[name]][1][part]
            return ring[:, where[name] % RING, at:at + k * n].rearrange("p (k n) -> p k n", k=k)

        uses, last_tag, order, filled_n, freed_n = [0] * 8, [None] * 8, {}, [0] * 8, [0] * 8

        def filled(tag):
            b, n = order[tag]
            return S(f"filled{b}"), n

        def freed(tag):
            b, n = order[tag]
            return S(f"freed{b}"), n

        def got(eng, tag):
            eng.wait_ge(*filled(tag))

        def free(ins, tag):
            return ins.then_inc(S(f"freed{order[tag][0]}"), 1)

        def bank(tag):
            return order[tag][0]

        def chain(eng, name):
            n = [0]

            def link(ins):
                n[0] += 1
                ins.then_inc(S(name), 1)
                eng.wait_ge(S(name), n[0])
            return link

        NORMS = [("n1", DT, SEQ, 1 / D, "eps", "attn_g"), ("n2", DT, SEQ, 1 / D, "eps", "ffn_g"),
                 ("n3", DT, T2, 1 / D, "eps", "mix_g"), ("lnv", DT, T2, 1 / D, "eps", "ln_g"),
                 ("ny", 16, T2, 1 / INNER, "eps", "ssm_norm_g"), ("n6", DT, T2, 1 / D, "eps", "ffn2_g"),
                 ("n7", DT, T2, 1 / D, "eps", "final_g")]
        sq_base, used_base = {}, {}
        a = b_ = 0
        for nm, K, *_ in NORMS:
            sq_base[nm], used_base[nm] = a, b_
            a += K
            b_ += K - 1
        NORM = {x[0]: x for x in NORMS}
        u_base = {"n1": 0, "n2": DT, "n3": 2 * DT, "n6": 3 * DT}

        blk = ctx.enter_context(nc.Block())

        @blk.tensor
        def _(pe):
            def open_(tag, *banks):
                for b in banks:
                    if last_tag[b] is not None:
                        pe.wait_ge(*freed(last_tag[b]))
                    last_tag[b] = tag
                uses[banks[0]] += 1
                order[tag] = (banks[0], uses[banks[0]])

            def fill(ins, tag):
                ins.then_inc(S(f"filled{order[tag][0]}"), 1)

            def arrived(name):
                pe.wait_ge(S(f"ring{where[name] % RING}"), landed[name])

            def dense(tag, banks, K, T, lhs, rhs, M=P, reads=None):
                open_(tag, *banks)
                for k in range(K):
                    for i, (lo, hi) in enumerate(halves(T)):
                        last = nc.tensor.matmul(PS[0:M, banks[i], 0:hi - lo], lhs(k), rhs(k)[:, lo:hi],
                                                start=(k == 0), stop=(k == K - 1))
                fill(last, tag)
                if reads:
                    last_read[reads] = tag

            def norm_sum(nm, banks):
                _, K, T, *_ = NORM[nm]
                open_(nm, *banks)
                for k in range(K):
                    pe.wait_ge(S("sq_ready"), sq_base[nm] + k + 1)
                    for i, (lo, hi) in enumerate(halves(T)):
                        last = nc.tensor.matmul(PS[:, banks[i], 0:hi - lo], ones, SQ[:, k % 2, lo:hi],
                                                start=(k == 0), stop=(k == K - 1))
                    if k < K - 1:
                        last.then_inc(S("sq_used"), 1)
                fill(last, nm)

            pe.wait_ge(S("consts_in"), 48)
            pe.wait_ge(S("lam_prod"), 1)
            open_("lam", 7)
            fill(nc.tensor.matmul(PS[:, 7, 0:2], ones[0:HD, :], small[0:HD, 0:2], start=True, stop=True), "lam")
            norm_sum("n1", (6,))
            pe.wait_ge(S("u_ready"), DT)
            n = 0
            for b, kind in enumerate(("q", "k", "v", "q", "k", "v")):
                arrived(("in", b))
                w = slot(("in", b))
                for m in range(4):
                    tag = ("in", b, m)
                    if kind == "v":
                        dense(tag, (n % 4,), DT, SEQ, lambda k: U[:, k, m * P:m * P + P], lambda k: w[:, k, :],
                              reads=("in", b))
                    else:
                        dense(tag, (n % 4,), DT, SEQ, lambda k: w[:, k, m * P:m * P + P],
                              lambda k: U[:, k, 0:SEQ], reads=("in", b))
                    n += 1
            for j in range(8):
                pe.wait_ge(S("rope_sq"), j + 1)
                open_(("rn", j), 6 + j % 2)
                fill(nc.tensor.matmul(PS[:, 6 + j % 2, :], heads_ones, SQ[:, j % 2, 0:SEQ], start=True, stop=True),
                     ("rn", j))
            for i in range(SB_HEADS + 2):
                if i < SB_HEADS:
                    j, r = i // 2, HD * (i % 2)
                    if i == 0:
                        for b in (0, 1):
                            for m in range(4):
                                pe.wait_ge(*freed(("in", b, m)))
                    open_(("z", i), 0, 1, 2)
                    for kb in range(QB):
                        o = ZO[kb]
                        last = nc.tensor.matmul(PS[:, o // 512, o % 512:o % 512 + SEQ - kb * P],
                                                QK[r:r + HD, 4 + j, kb * P:kb * P + P], QK[r:r + HD, j, kb * P:SEQ],
                                                start=True, stop=True)
                    fill(last, ("z", i))
                    pe.wait_ge(S("rope_normed"), i + 1)
                    open_(("rot", i), 7)
                    fill(nc.tensor.matmul(PS[:, 7, :], rot, QK[:, 8 + i, :], start=True, stop=True), ("rot", i))
                if 1 <= i <= SB_HEADS:
                    h = i - 1
                    pe.wait_ge(S("sp_masked"), h + 1)
                    open_(("c", h), 3, 4, 5)
                    for kb in range(QB):
                        for k2 in range(kb, QB):
                            o = ZO[kb] + (k2 - kb) * P
                            last = nc.tensor.matmul(PS[:, 3 + o // 512, o % 512:o % 512 + SEQ - k2 * P],
                                                    lower if k2 == kb else ones,
                                                    SP[:, h % 2, ZO[k2]:ZO[k2] + SEQ - k2 * P],
                                                    start=(k2 == kb), stop=(k2 == QB - 1))
                    fill(last, ("c", h))
                if i >= 2:
                    h = i - 2
                    r = HD * (h % 2)
                    pe.wait_ge(S("w_ready"), h + 1)
                    if h == 0:
                        for b in (2, 5):
                            for m in range(4):
                                pe.wait_ge(*freed(("in", b, m)))
                    open_(("o", h), 6)
                    for kb in range(QB):
                        last = nc.tensor.matmul(PS[r:r + HD, 6, kb * P:SEQ], V[:, kb, h * HD:h * HD + HD],
                                                Z[:, h % 3, ZO[kb]:ZO[kb] + SEQ - kb * P],
                                                start=(kb == 0), stop=(kb == QB - 1))
                    fill(last, ("o", h))
            pe.wait_ge(S("rope_done"), 8)
            steps = [(h, qb) for h in range(DIFF_HEADS) for qb in range(QB)]
            for n in range(len(steps) + 2):
                if n < len(steps):
                    h, qb = steps[n]
                    b0 = 2 * (n % 2)
                    open_(("s", n), b0, b0 + 1)
                    for c in range(2):
                        last = nc.tensor.matmul(PS[:, b0 + c, 0:(qb + 1) * P],
                                                QK[HD * c:HD * c + HD, 8 + h, qb * P:qb * P + P],
                                                QK[HD * c:HD * c + HD, 12 + h, 0:(qb + 1) * P], start=True, stop=True)
                    fill(last, ("s", n))
                if 1 <= n <= len(steps):
                    m = n - 1
                    pe.wait_ge(S("diff_map"), m + 1)
                    open_(("at", m), 4 + m % 2)
                    for kb in range(steps[m][1] + 1):
                        last = nc.tensor.transpose(PS[:, 4 + m % 2, kb * P:kb * P + P],
                                                   DA[:, m % 2, kb * P:kb * P + P], ident)
                    fill(last, ("at", m))
                if n >= 2:
                    m = n - 2
                    h, qb = steps[m]
                    pe.wait_ge(*freed(("at", m)))
                    if qb == 0:
                        open_(("do", h), 6 + h % 2)
                    for kb in range(qb + 1):
                        last = nc.tensor.matmul(PS[:, 6 + h % 2, qb * P:qb * P + P],
                                                V[:, kb, 512 + h * P:512 + h * P + P],
                                                DAT[:, m % 2, kb * P:kb * P + P], start=(kb == 0), stop=(kb == qb))
                    if qb == QB - 1:
                        fill(last, ("do", h))
                    else:
                        last.then_inc(S("diff_o"), 1)
            for h in range(DIFF_HEADS):
                pe.wait_ge(S("subln_sq"), h + 1)
                open_(("sl", h), 6 + h % 2)
                fill(nc.tensor.matmul(PS[:, 6 + h % 2, :], ones, SQ[:, h % 2, 0:SEQ], start=True, stop=True), ("sl", h))
            pe.wait_ge(*freed(("o", SB_HEADS - 1)))
            pe.wait_ge(S("mix_ready"), DIFF_HEADS)
            for m in range(DT):
                name = ("wo", m // 4)
                arrived(name)
                w = slot(name)
                dense(("wo", m), (m % 4,), DT, SEQ, lambda k: w[:, k, (m % 4) * P:(m % 4) * P + P],
                      lambda k: MIX[:, k, :], reads=name)
            norm_sum("n2", (6,))
            pe.wait_ge(S("u_ready"), u_base["n2"] + DT)
            for m in range(FFT):
                name = ("gu", m // 2)
                arrived(name)
                cols = slice((m % 2) * P, (m % 2) * P + P)
                for part, kind in enumerate(("ga", "up")):
                    w = slot(name, part)
                    dense((kind, m), (2 * (m % 3) + part,), DT, SEQ, lambda k: w[:, k, cols],
                          lambda k: U[:, k, 0:SEQ], reads=name)
            for b in range(4):
                banks = [2 * (b % 3), 2 * (b % 3) + 1]
                for kh in range(2):
                    name = ("down", b, kh)
                    arrived(name)
                    w = slot(name)
                    for mm in range(2):
                        tag = ("dn", 2 * b + mm)
                        if kh == 0:
                            open_(tag, banks[mm])
                        if kh == 1 and b == 0 and mm == 0:
                            pe.wait_ge(*freed(("up", FFT - 1)))
                        if kh == 0 and b == 0 and mm == 0:
                            pe.wait_ge(*freed(("up", FFT // 2 - 1)))
                        for k in range(11):
                            last = nc.tensor.matmul(PS[:, banks[mm], :], w[:, k, mm * P:mm * P + P],
                                                    G[:, 11 * kh + k, :], start=(kh == 0 and k == 0),
                                                    stop=(kh == 1 and k == 10))
                        if kh == 1:
                            fill(last, tag)
                            last_read[name] = tag
                        elif mm == 1:
                            last.then_inc(S("down_half"), 1)
                            last_read[name] = ("sem", "down_half", b + 1)
            norm_sum("n3", (6, 7))
            pe.wait_ge(S("u_ready"), u_base["n3"] + DT)
            arrived(("dt",))
            w = slot(("dt",))
            dense("dt", (0, 1), DT, T2, lambda k: w[:, k, :], lambda k: U[:, k, :], M=64, reads=("dt",))
            pe.wait_ge(S("dt_done"), 2)
            for part, src in enumerate((0, 5)):
                open_(("dtT", part), 2 + part)
                for c, (t0, n) in enumerate(CHUNKS):
                    last = nc.tensor.transpose(PS[0:n, 2 + part, c * 64:c * 64 + 64], DTF[0:64, src, t0:t0 + n],
                                               ident[0:64, 0:64])
                fill(last, ("dtT", part))
            pe.wait_ge(*freed(("dtT", 1)))
            open_("F", 4)
            for c, (t0, n) in enumerate(CHUNKS):
                for d, tri in enumerate((upper, lower)):
                    last = nc.tensor.matmul(PS[0:n, 4, c * 64 + 32 * d:c * 64 + 32 * d + 32], tri[0:n, 0:n],
                                            AAT[0:n, c, 32 * d:32 * d + 32], start=True, stop=True)
            fill(last, "F")
            open_("TOT", 5)
            for c, (t0, n) in enumerate(CHUNKS):
                last = nc.tensor.matmul(PS[:, 5, c * 64:c * 64 + 64], ones[0:n, :], AAT[0:n, c, :], start=True, stop=True)
            fill(last, "TOT")
            open_("FR", 6, 7)
            for c, (t0, n) in enumerate(CHUNKS):
                for d, tri in enumerate((upper, lower)):
                    last = nc.tensor.matmul(PS[32 * d:32 * d + 32, 6 + c // 4, (c % 4) * P:(c % 4) * P + n],
                                            AAT[0:n, c, 32 * d:32 * d + 32], tri[0:n, 0:n], start=True, stop=True)
            fill(last, "FR")

            pair = [0]

            def proj(tag, w, cols, name):
                b = 2 * (pair[0] % 2)
                pair[0] += 1
                dense(tag, (b, b + 1), DT, T2, lambda k: w[:, k, cols], lambda k: U[:, k, :], reads=name)

            def xbc(g, i, j):
                name = ("xbc", g, i)
                arrived(name)
                if j < 2:
                    proj(("xb", g, 3 * i + j), slot(name, 0), slice(j * P, j * P + P), name)
                else:
                    proj(("xb", g, 3 * i + 2), slot(name, 1), slice(0, P), name)

            def conf(u, part):
                arrived(("conf", u))
                proj((("ca", "cg")[part], u), slot(("conf", u), part), slice(0, P), ("conf", u))

            def turn(g, t):
                src = CO[:, (6 * g + t) % 2, :] if t != 2 else BF[:, :]
                pe.wait_ge(S("conv_ready"), 6 * g + t + 1)
                open_(("tr", g, t), 4, 5)
                for c, (t0, n) in enumerate(CHUNKS):
                    last = nc.tensor.transpose(PS[0:n, 4 + c // 4, (c % 4) * P:(c % 4) * P + P], src[:, t0:t0 + n], ident)
                fill(last, ("tr", g, t))

            for g in range(GROUPS):
                tiles = [(i, j) for i in range(2) for j in range(3)]
                for t, (i, j) in enumerate(tiles):
                    xbc(g, i, j)
                    if t >= 2:
                        turn(g, t - 2)
                turn(g, 4)
                pe.wait_ge(S("conv_ready"), 6 * g + 6)
                pe.wait_ge(*freed(("tr", g, 2)))
                pe.wait_ge(*freed(("tr", g, 4)))
                for s, c in enumerate(range(NC - 1, 0, -1)):
                    t0, n = CHUNKS[c]
                    pe.wait_ge(S("xwb_ready"), 4 * g + s + 1)
                    open_(("sb", g, c), 6)
                    fill(nc.tensor.matmul(PS[:, 6, :], BT[0:n, c, :], XW[0:n, s % 2, :], start=True, stop=True),
                         ("sb", g, c))
                    name = ("z", g, s // 2)
                    arrived(name)
                    proj(("zt", 4 * g + s), slot(name), slice((s % 2) * P, (s % 2) * P + P), name)
                for c, (t0, n) in enumerate(CHUNKS):
                    if c == 0:
                        open_(("cb", g, 0), 4)
                        fill(nc.tensor.matmul(PS[0:n, 4, 0:n], BF[:, 0:n], CF[:, 0:n], start=True, stop=True), ("cb", g, 0))
                    if c < 4:
                        conf(2 * g + c // 2, c % 2)
                        pe.wait_ge(*freed(("sb", g, c + 1)))
                        open_(("ob", g, c), 7)
                        fill(nc.tensor.matmul(PS[0:n, 7, :], CF[:, t0:t0 + n], SNAP[:, c, :], start=True, stop=True),
                             ("ob", g, c))
                    if c > 0:
                        pe.wait_ge(*freed(("sf", g, c - 1)))
                        open_(("of", g, c), 6)
                        fill(nc.tensor.matmul(PS[0:n, 6, :], CF[:, t0:t0 + n], ST[:, (c - 1) % 2, :], start=True, stop=True),
                             ("of", g, c))
                    pe.wait_ge(S("m_ready"), NC * g + c + 1)
                    open_(("yd", g, c), 5)
                    for h in range(GH):
                        last = nc.tensor.matmul(PS[0:n, 5, h * HD:h * HD + HD], M1[0:n, h, 0:n],
                                                XS[0:n, c, h * HD:h * HD + HD], start=True, stop=True)
                    fill(last, ("yd", g, c))
                    if c < 4:
                        pe.wait_ge(S("xwf_ready"), 4 * g + c + 1)
                        open_(("sf", g, c), 6)
                        fill(nc.tensor.matmul(PS[:, 6, :], BT[0:n, c, :], XW[0:n, c % 2, :], start=True, stop=True),
                             ("sf", g, c))
                        t1, n1 = CHUNKS[c + 1]
                        open_(("cb", g, c + 1), 4)
                        fill(nc.tensor.matmul(PS[0:n1, 4, 0:n1], BF[:, t1:t1 + n1], CF[:, t1:t1 + n1], start=True,
                                              stop=True), ("cb", g, c + 1))
                    pe.wait_ge(*freed(("yd", g, c)))
                    open_(("yt", g, c), 5)
                    for j in range(4):
                        last = nc.tensor.transpose(PS[:, 5, j * P:j * P + n], YC[0:n, j * P:j * P + P], ident[0:n, 0:n])
                    fill(last, ("yt", g, c))
            pe.wait_ge(S("cacc_done"), DT)
            open_("lnm", 6, 7)
            for k in range(DT):
                for i, (lo, hi) in enumerate(halves(T2)):
                    last = nc.tensor.matmul(PS[:, 6 + i, 0:HT], ones, CACC[:, k, lo:hi], start=(k == 0), stop=(k == DT - 1))
            fill(last, "lnm")
            norm_sum("lnv", (6, 7))
            n = 0
            for m in range(DT):
                for kind, src in (("g1", U), ("co", CACC)):
                    name = (kind, m // 4)
                    arrived(name)
                    w = slot(name)
                    if kind == "co" and m == 0:
                        pe.wait_ge(S("conf_ready"), DT)
                    dense((kind, m), (2 * (n % 3), 2 * (n % 3) + 1), DT, T2,
                          lambda k: w[:, k, (m % 4) * P:(m % 4) * P + P], lambda k: src[:, k, :], reads=name)
                    n += 1
            norm_sum("ny", (6, 7))
            for m in range(DT):
                for kind, src, K in (("g2", U, DT), ("so", YT, 16)):
                    name = (kind, m // 2)
                    arrived(name)
                    w = slot(name)
                    if kind == "so" and m == 0:
                        pe.wait_ge(S("y_ready"), 16)
                    dense((kind, m), (2 * (n % 3), 2 * (n % 3) + 1), K, T2,
                          lambda k: w[:, k, (m % 2) * P:(m % 2) * P + P], lambda k: src[:, k, :], reads=name)
                    n += 1
            pe.wait_ge(S("merged"), DT)
            for m in range(DT):
                name = ("out", m // 4)
                arrived(name)
                w = slot(name)
                dense(("out", m), (2 * (n % 3), 2 * (n % 3) + 1), DT, T2,
                      lambda k: w[:, k, (m % 4) * P:(m % 4) * P + P], lambda k: MG[:, k, :], reads=name)
                n += 1
            norm_sum("n6", (6, 7))
            pe.wait_ge(S("u_ready"), u_base["n6"] + DT)
            open_("lg", 0)
            for c, (t0, n) in enumerate(CHUNKS):
                for k in range(DT):
                    r0 = PARAMS["router"] + k * EXPERTS
                    last = nc.tensor.matmul(PS[0:n, 0, c * EXPERTS:(c + 1) * EXPERTS], U[:, k, t0:t0 + n],
                                            par[:, r0:r0 + EXPERTS], start=(k == 0), stop=(k == DT - 1))
            fill(last, "lg")
            for c, (t0, n) in enumerate(CHUNKS):
                for hf in range(2):
                    b = 2 + (2 * c + hf) % 2
                    open_(("xn", c, hf), b)
                    for k in range(4):
                        last = nc.tensor.transpose(PS[0:n, b, k * P:k * P + P], U[:, 4 * hf + k, t0:t0 + n], ident)
                    fill(last, ("xn", c, hf))
            pe.wait_ge(S("aff_ready"), 2)
            open_("af", 4, 5)
            for c, (t0, n) in enumerate(CHUNKS):
                last = nc.tensor.transpose(PS[0:EXPERTS, 4 + c // 4, (c % 4) * P:(c % 4) * P + n], AFF[0:n, c, :],
                                           ident[0:n, 0:n])
            fill(last, "af")
            pe.wait_ge(S("slots_ready"), 1)
            open_("sl16", 0)
            for c, (t0, n) in enumerate(CHUNKS):
                last = nc.tensor.transpose(PS[0:n, 0, c * EXPERTS:(c + 1) * EXPERTS], TK[0:EXPERTS, 0, t0:t0 + n],
                                           ident[0:EXPERTS, 0:EXPERTS])
            fill(last, "sl16")
            for b in range(8):
                if last_tag[b] is not None:
                    pe.wait_ge(*freed(last_tag[b]))

            pe.sem_inc(S("combined"), 1)
            with pe.Fori(0, EXPERTS) as e:
                def here(i):
                    s = (N_DENSE + i) % RING
                    pe.wait_ge(S(f"ring{s}"), e * (16 * 12 // RING) + RING0[s] + 16 * (i // RING + 1))

                pe.wait_ge(S("sel_ready"), e * 2 + 2)
                pe.wait_ge(S("ye_ready"), 1 + e * 2)
                for hf in range(2):
                    for k in range(4):
                        for c, (t0, n) in enumerate(CHUNKS):
                            last = nc.tensor.matmul(PS[:, hf, k * CAP:(k + 1) * CAP],
                                                    XNT[0:n, c, (4 * hf + k) * P:(4 * hf + k + 1) * P],
                                                    SE[0:n, c, :], start=(c == 0), stop=(c == NC - 1))
                    last.then_inc(S("x_gathered"), 1)
                pe.wait_ge(S("xg_ready"), e * 2 + 2)
                for b in range(4):
                    for part, nm in enumerate(("gate_done", "up_done")):
                        here(2 * b + part)
                        w = ring[:, (N_DENSE + 2 * b + part) % RING, :].rearrange("p (k n) -> p k n", k=DT)
                        bank = 2 + b % 2 + 2 * part
                        if b < 2 and part == 1:
                            pe.wait_ge(S("h_added"), 1 + e * DT)
                        elif b < 2:
                            pe.wait_ge(S("sat_ready"), 1 + e)
                        elif part == 0:
                            pe.wait_ge(S("gate_act"), e * 4 + b - 1)
                        else:
                            pe.wait_ge(S("hg_ready"), 1 + e * 4 + b - 1)
                        for m in range(4):
                            for k in range(DT):
                                last = nc.tensor.matmul(PS[:, bank, m * CAP:(m + 1) * CAP], w[:, k, m * P:m * P + P],
                                                        XG[:, k, :], start=(k == 0), stop=(k == DT - 1))
                        last.then_inc(S(nm), 1)
                pe.wait_ge(S("gate_act"), e * 4 + 4)
                for c, (t0, n) in enumerate(CHUNKS):
                    last = nc.tensor.transpose(PS[0:CAP, 2 + c // 4, (c % 4) * P:(c % 4) * P + n], SA[0:n, c, :],
                                               ident[0:n, 0:n])
                last.then_inc(S("sa_turned"), 1)
                pe.wait_ge(S("hg_ready"), 1 + e * 4 + 4)
                for b in range(4):
                    here(8 + b)
                    w = ring[:, (N_DENSE + 8 + b) % RING, :].rearrange("p (k n) -> p k n", k=EFT)
                    if b % 2 == 0:
                        pe.wait_ge(S("yf_ready"), 1 + e * 2)
                    for m in range(2):
                        col = ((b % 2) * 2 + m) * CAP
                        for k in range(EFT):
                            last = nc.tensor.matmul(PS[:, 6 + b // 2, col:col + CAP], w[:, k, m * P:m * P + P],
                                                    HG[:, k, :], start=(k == 0), stop=(k == EFT - 1))
                    last.then_inc(S("down_done"), 1)
                for hf in range(2):
                    pe.wait_ge(S("yf_ready"), 1 + e * 2 + hf + 1)
                    pe.wait_ge(S("xg_ready"), e * 2 + 2)
                    for k in range(4):
                        last = nc.tensor.transpose(PS[0:CAP, hf, k * P:k * P + P], YF[:, 4 * hf + k, :], ident)
                    last.then_inc(S("y_turned"), 1)
                pe.wait_ge(S("sat_ready"), 1 + e + 1)
                for m in range(DT):
                    if m % 4 == 0:
                        pe.wait_ge(S("ye_ready"), 1 + e * 2 + m // 4 + 1)
                    if m >= 2:
                        pe.wait_ge(S("h_added"), 1 + e * DT + m - 1)
                    for i, (lo, hi) in enumerate(halves(T2)):
                        last = nc.tensor.matmul(PS[:, 4 + 2 * (m % 2) + i, 0:HT], YE[0:CAP, m * P:m * P + P],
                                                SAT[0:CAP, lo:hi], start=True, stop=True)
                    last.then_inc(S("combined"), 1)
            pe.wait_ge(S("h_added"), 1 + EXPERTS * DT)
            for b in range(8):
                last_tag[b] = None
            norm_sum("n7", (6, 7))

        @blk.scalar
        def _(act):
            A = nc.scalar.activation
            link = chain(act, "act_chain")

            def squares(nm, src):
                _, K, T, *_ = NORM[nm]
                for k in range(K):
                    if k >= 2:
                        act.wait_ge(S("sq_used"), used_base[nm] + k - 1)
                    A(SQ[:, k % 2, 0:T], src(k), ACT.Square).then_inc(S("sq_ready"), 1)

            def root(nm, banks):
                _, K, T, scale, eps, _ = NORM[nm]
                got(act, nm)
                free(A(tok(RS[:, 0:T], T), ps(banks, T), ACT.Sqrt, bias=pcol(eps), scale=scale), nm)

            act.dma_start(H[:, :, :], inp["h_t"].rearrange("(k p) n -> p k n", p=P)).then_inc(S("h_in"), 16)
            act.wait_ge(S("consts_in"), 48)
            act.wait_ge(S("h_in"), 16)
            squares("n1", lambda k: H[:, k, META:T2])
            root("n1", (6,))
            got(act, "lam")
            free(A(small[:, 2:4], PS[:, 7, 0:2], ACT.Exp), "lam")
            for b in (0, 1, 3, 4):
                for m in range(4):
                    got(act, ("in", b, m))
                    at = {0: 0, 1: 4, 3: 8, 4: 12}[b] + m
                    free(A(QK[:, at, :], PS[:, (4 * b + m) % 4, :], ACT.Copy, scale=HD ** -0.5 if b == 0 else 1.0),
                         ("in", b, m))
            def rope_root(j):
                got(act, ("rn", j))
                free(A(MIX[:, j, :], PS[:, bank(("rn", j)), :], ACT.Sqrt, bias=pcol("eps"), scale=1.0 / HD), ("rn", j))

            for j in range(8):
                act.wait_ge(*freed(("in", 3 + j // 4, j % 4)))
                if j >= 2:
                    got(act, ("rn", j - 2))
                A(SQ[:, j % 2, 0:SEQ], QK[:, 8 + j, :], ACT.Square).then_inc(S("rope_sq"), 1)
                if j >= 1:
                    rope_root(j - 1)
            rope_root(7)
            nc.scalar.preload_act_table_set("natural_log_exp_and_others")
            for i in range(SB_HEADS + 1):
                if i < SB_HEADS:
                    got(act, ("z", i))
                    if i >= 3:
                        got(act, ("o", i - 3))
                    free(A(Z[:, i % 3, :], PS[:, 0:3, :].rearrange("p a n -> p (a n)")[:, 0:1280], ACT.Copy), ("z", i))
                    act.wait_ge(*freed(("z", i)))
                    if i >= 2:
                        got(act, ("c", i - 2))
                    link(A(SP[:, i % 2, :], Z[:, i % 3, :], ACT.Abs))
                    link(A(SP[:, i % 2, :], SP[:, i % 2, :], ACT.Exp, scale=-1.0))
                    A(SP[:, i % 2, :], SP[:, i % 2, :], ACT.Ln, bias=pcol("one")).then_inc(S("ln_ready"), 1)
                if i >= 1:
                    act.wait_ge(S("arg_masked"), i)
                    A(Z[:, (i - 1) % 3, :], Z[:, (i - 1) % 3, :], ACT.Exp).then_inc(S("w_ready"), 1)
            for n in range(DIFF_HEADS * QB + 1):
                if n < DIFF_HEADS * QB:
                    qb, b0 = n % QB, 2 * (n % 2)
                    act.wait_ge(S("diff_max"), n + 1)
                    if n == 0:
                        got(act, ("o", SB_HEADS - 1))
                    if n >= 2:
                        act.wait_ge(S("diff_map"), n - 1)
                    for c in range(2):
                        ins = A(PR[:, n % 2, c, 0:(qb + 1) * P], PS[:, b0 + c, 0:(qb + 1) * P], ACT.Exp,
                                bias=small[:, 16 + 2 * (n % 2) + c:17 + 2 * (n % 2) + c], scale=HD ** -0.5,
                                accum_out=small[:, 24 + 2 * (n % 2) + c:25 + 2 * (n % 2) + c])
                        if c == 0:
                            ins.then_inc(S("diff_exp0"), 1)
                    free(ins, ("s", n))
                if n >= 1:
                    m = n - 1
                    got(act, ("at", m))
                    if m >= 2 and (m - 2) % QB == QB - 1:
                        got(act, ("do", (m - 2) // QB))
                    elif m >= 2:
                        act.wait_ge(S("diff_o"), (QB - 1) * ((m - 2) // QB) + (m - 2) % QB + 1)
                    free(A(DAT[:, m % 2, 0:(m % QB + 1) * P], PS[:, 4 + m % 2, 0:(m % QB + 1) * P], ACT.Copy), ("at", m))
            def subln_root(h):
                got(act, ("sl", h))
                free(A(QK[:, h, :], PS[:, bank(("sl", h)), :], ACT.Sqrt, bias=pcol("subln_eps"), scale=1.0 / P), ("sl", h))

            for h in range(DIFF_HEADS):
                act.wait_ge(*freed(("do", h)))
                if h >= 2:
                    got(act, ("sl", h - 2))
                A(SQ[:, h % 2, 0:SEQ], MIX[:, 4 + h, :], ACT.Square).then_inc(S("subln_sq"), 1)
                if h >= 1:
                    subln_root(h - 1)
            subln_root(DIFF_HEADS - 1)
            for m in range(DT):
                act.wait_ge(*freed(("wo", m)))
                if m >= 2:
                    act.wait_ge(S("sq_used"), used_base["n2"] + m - 1)
                A(SQ[:, m % 2, 0:SEQ], H[:, m, META:T2], ACT.Square).then_inc(S("sq_ready"), 1)
            root("n2", (6,))
            for m in range(FFT):
                got(act, ("ga", m))
                if m >= 2:
                    act.wait_ge(*freed(("up", m - 2)))
                free(A(SG[:, m % 2, :], PS[:, 2 * (m % 3), :], ACT.Silu), ("ga", m))
            for m in range(DT):
                act.wait_ge(*freed(("dn", m)))
                if m >= 2:
                    act.wait_ge(S("sq_used"), used_base["n3"] + m - 1)
                A(SQ[:, m % 2, :], H[:, m, :], ACT.Square).then_inc(S("sq_ready"), 1)
            root("n3", (6, 7))
            got(act, "dt")
            free(A(tok(DTF[0:64, 1, :], T2), PS[0:64, 0:2, 0:HT], ACT.Identity, bias=par[0:64, PARAMS["dt_bias"]:PARAMS["dt_bias"] + 1]), "dt")
            act.wait_ge(*freed("dt"))
            nc.scalar.preload_act_table_set("natural_log_exp_and_others")
            link(A(DTF[0:64, 2, :], DTF[0:64, 1, :], ACT.Abs))
            link(A(DTF[0:64, 2, :], DTF[0:64, 2, :], ACT.Exp, scale=-1.0))
            A(small[0:64, 32:33], par[0:64, PARAMS["a_log"]:PARAMS["a_log"] + 1], ACT.Exp).then_inc(S("dt_parts"), 1)
            A(DTF[0:64, 2, :], DTF[0:64, 2, :], ACT.Ln, bias=par[0:64, PARAMS["one"]:PARAMS["one"] + 1]).then_inc(S("dt_parts"), 1)
            got(act, "FR")
            link(A(DTF[0:64, 3, 0:512], PS[0:64, 6, :], ACT.Copy))
            free(A(DTF[0:64, 3, 512:T2], PS[0:64, 7, 0:META], ACT.Copy), "FR")
            act.wait_ge(*freed("FR"))
            act.dma_start(fr_dram, DTF[0:64, 3, :]).then_inc(S("fr_out"), 16)
            act.wait_ge(S("w2_arg"), 2)
            for i, (n, cs) in enumerate(((P, slice(0, 4)), (META, slice(4, 5)))):
                A(EF[0:n, cs, :], FT[0:n, cs, :], ACT.Exp).then_inc(S("ssd_exp"), 1)
                A(W2[0:n, cs, :], W2[0:n, cs, :], ACT.Exp).then_inc(S("ssd_exp"), 1)
            A(ET[:, :, :], ET[:, :, :], ACT.Exp).then_inc(S("ssd_exp"), 1)
            act.wait_ge(S("fr_out"), 16)

            def fr_load(g, c):
                i = NC * g + c
                t0, n = CHUNKS[c]
                if i >= 2:
                    act.wait_ge(S("m_ready"), i - 1)
                for d in range(2):
                    src = fr_dram[32 * d + GH * g:32 * d + GH * (g + 1), t0:t0 + n]
                    act.dma_start(FR[i % 2][d][:, :, 0:n], src.partition_broadcast(P)).then_inc(S(f"fr_in{i % 2}"), 16)

            def conv_tile(g, t):
                got(act, ("xb", g, t))
                i = 6 * g + t
                if i >= 2:
                    act.wait_ge(S("conv_done"), i - 1)
                b = bank(("xb", g, t))
                free(A(tok(XP[:, i % 2, 3:3 + T2], T2), PS[:, b:b + 2, 0:HT], ACT.Copy), ("xb", g, t))

            def conv_silu(g, t):
                i = 6 * g + t
                act.wait_ge(S("conv_done"), i + 1)
                j = 16 + (0 if t == 2 else 4) + g if t in (2, 5) else 4 * g + (t if t < 2 else t - 1)
                co = CO[:, (6 * g + t) % 2, :]
                if t in (2, 5):
                    if g > 0:
                        got(act, ("of", g - 1, NC - 1))
                        act.wait_ge(S("m_ready"), NC * g)
                    ins = A(BF if t == 2 else CF, CO[:, (6 * g + t) % 2, :], ACT.Silu, bias=pcol("ssm_b", j))
                else:
                    ins = A(co, co, ACT.Silu, bias=pcol("ssm_b", j))
                ins.then_inc(S("conv_ready"), 1)

            def take_turned(g, t):
                tag = ("tr", g, t)
                got(act, tag)
                if g > 0:
                    got(act, ("yt", g - 1, NC - 1))
                dst = BT if t == 2 else XS[:, :, XS_AT[t] * P:XS_AT[t] * P + P]
                link(A(dst[:, 0:4, :], PS[:, 4, :].rearrange("p (c n) -> p c n", c=4), ACT.Copy))
                free(A(dst[0:META, 4, :], PS[0:META, 5, 0:P], ACT.Copy), tag)

            XS_AT = {0: 0, 1: 1, 3: 2, 4: 3}
            for g in range(GROUPS):
                for t in range(6):
                    conv_tile(g, t)
                    if t >= 1:
                        conv_silu(g, t - 1)
                    if t >= 3:
                        take_turned(g, t - 3)
                conv_silu(g, 5)
                take_turned(g, 3)
                take_turned(g, 4)
                fr_load(g, 0)
                fr_load(g, 1)
                for s in range(4):
                    tag = ("zt", 4 * g + s)
                    got(act, tag)
                    b = bank(tag)
                    free(A(tok(YT[:, 4 * g + s, :], T2), PS[:, b:b + 2, 0:HT], ACT.Silu), tag)
                for c, (t0, n) in enumerate(CHUNKS):
                    i = NC * g + c
                    act.wait_ge(S("min_ready"), i + 1)
                    A(FR[i % 2][0][0:n, :, 0:n], FR[i % 2][0][0:n, :, 0:n], ACT.Exp).then_inc(S("e_ready"), 1)
                    if c % 2 == 1:
                        u = 2 * g + c // 2
                        got(act, ("cg", u))
                        if u >= 1:
                            act.wait_ge(*freed(("ca", u - 1)))
                        b = bank(("cg", u))
                        free(A(tok(SGB[:, :], T2), PS[:, b:b + 2, 0:HT], ACT.Sigmoid), ("cg", u))
                    if c + 2 < NC:
                        fr_load(g, c + 2)
            for k in range(DT):
                act.wait_ge(S("ln_centred"), k + 1)
                if k >= 2:
                    act.wait_ge(S("sq_used"), used_base["lnv"] + k - 1)
                A(SQ[:, k % 2, :], CACC[:, k, :], ACT.Square).then_inc(S("sq_ready"), 1)
            root("lnv", (6, 7))
            for k in range(DT):
                act.wait_ge(S("ln_scaled"), k + 1)
                A(CACC[:, k, :], CACC[:, k, :], ACT.Silu, bias=pcol("ln_b", k)).then_inc(S("conf_ready"), 1)
            for m in range(DT):
                got(act, ("g1", m))
                if m >= 2:
                    act.wait_ge(*freed(("co", m - 2)))
                if m == 0:
                    act.wait_ge(S("ln_centred"), DT)
                b = bank(("g1", m))
                free(A(tok(GT[:, m % 2, :], T2), PS[:, b:b + 2, 0:HT], ACT.Sigmoid), ("g1", m))
            squares("ny", lambda k: YT[:, k, :])
            root("ny", (6, 7))
            for m in range(DT):
                got(act, ("g2", m))
                if m >= 2:
                    act.wait_ge(S("merged"), m - 1)
                else:
                    act.wait_ge(*freed(("co", DT - 1)))
                b = bank(("g2", m))
                free(A(tok(GT[:, m % 2, :], T2), PS[:, b:b + 2, 0:HT], ACT.Sigmoid), ("g2", m))
            for m in range(DT):
                act.wait_ge(*freed(("out", m)))
                if m >= 2:
                    act.wait_ge(S("sq_used"), used_base["n6"] + m - 1)
                A(SQ[:, m % 2, :], H[:, m, :], ACT.Square).then_inc(S("sq_ready"), 1)
            root("n6", (6, 7))
            for c, (t0, n) in enumerate(CHUNKS):
                act.wait_ge(S("lg_max"), NC)
                ins = A(AFF[0:n, c, :], PS[0:n, 0, c * EXPERTS:(c + 1) * EXPERTS], ACT.Exp,
                        bias=small[0:n, 48 + c:49 + c], accum_out=small[0:n, 56 + c:57 + c])
                if c < NC - 1:
                    ins.then_inc(S("aff_exp"), 1)
            free(ins, "lg")
            for c, (t0, n) in enumerate(CHUNKS):
                for hf in range(2):
                    got(act, ("xn", c, hf))
                    free(A(XNT[0:n, c, 512 * hf:512 * hf + 512], PS[0:n, 2 + hf, :], ACT.Copy), ("xn", c, hf))
            nc.scalar.preload_act_table_set("silu_and_others")
            act.sem_inc(S("yf_ready"), 1)
            act.sem_inc(S("ye_ready"), 1)
            with act.Fori(0, EXPERTS) as e:
                for hf in range(2):
                    act.wait_ge(S("x_gathered"), e * 2 + hf + 1)
                    A(XG[:, 4 * hf:4 * hf + 4, :], PS[:, hf, 0:4 * CAP].rearrange("p (k n) -> p k n", k=4),
                      ACT.Copy).then_inc(S("xg_ready"), 1)
                for b in range(4):
                    act.wait_ge(S("gate_done"), e * 4 + b + 1)
                    act.wait_ge(S("hg_ready"), e * 4 + max(b, 1))
                    A(SIL[:, b % 2, :], PS[:, 2 + b % 2, 0:4 * CAP], ACT.Silu).then_inc(S("gate_act"), 1)
                for hf in range(2):
                    act.wait_ge(S("down_done"), e * 4 + 2 * hf + 2)
                    A(YF[:, 4 * hf:4 * hf + 4, :], PS[:, 6 + hf, 0:4 * CAP].rearrange("p (k n) -> p k n", k=4),
                      ACT.Copy).then_inc(S("yf_ready"), 1)
                for hf in range(2):
                    act.wait_ge(S("y_turned"), e * 2 + hf + 1)
                    A(YE[0:CAP, 512 * hf:512 * hf + 512], PS[0:CAP, hf, :], ACT.Copy).then_inc(S("ye_ready"), 1)
            act.wait_ge(S("h_added"), 1 + EXPERTS * DT)
            squares("n7", lambda k: H[:, k, :])
            root("n7", (6, 7))

        @blk.vector
        def _(dve):
            V_ = nc.vector
            link = chain(dve, "dve_chain")
            MUL, ADD, SUB = ALU.mult, ALU.add, ALU.subtract

            def norm_apply(nm, src, dst, sem):
                _, K, T, _, _, gain = NORM[nm]
                dve.wait_ge(*freed(nm))
                link(V_.reciprocal(RS[:, 0:T], RS[:, 0:T]))
                for k in range(K):
                    V_.scalar_tensor_tensor(dst(k), src(k), pcol(gain, k), RS[:, 0:T], MUL, MUL).then_inc(S(sem), 1)

            dve.wait_ge(S("consts_in"), 48)
            l0 = PARAMS["lam"]
            V_.tensor_tensor(small[0:HD, 0:2], par[0:HD, l0:l0 + 4:2], par[0:HD, l0 + 1:l0 + 4:2], MUL).then_inc(S("lam_prod"), 1)
            norm_apply("n1", lambda k: H[:, k, META:T2], lambda k: U[:, k, 0:SEQ], "u_ready")
            dve.wait_ge(*freed("lam"))
            link(V_.tensor_tensor(small[:, 4:5], small[:, 3:4], small[:, 2:3], SUB))
            link(V_.tensor_scalar(small[:, 4:5], small[:, 4:5], LAMBDA_INIT, None, SUB))
            link(V_.tensor_scalar(small[:, 5:6], pcol("subln_g"), 1.0 - LAMBDA_INIT, None, MUL))
            for i, b in enumerate((2, 5)):
                for m in range(4):
                    got(dve, ("in", b, m))
                    tag = ("in", b, m)
                    free(V_.tensor_copy(V[:, m, 512 * i:512 * i + 512], PS[:, bank(tag), :]), tag)
            for j in range(8):
                dve.wait_ge(*freed(("rn", j)))
                R = MIX[:, j, :]
                link(V_.reciprocal(R, R))
                gain = pcol("q_g") if j < 4 else pcol("k_g")
                V_.scalar_tensor_tensor(QK[:, 8 + j, :], QK[:, 8 + j, :], gain, R, MUL, MUL).then_inc(S("rope_normed"), 1)
            def stick_out(h):
                r0 = HD * (h % 2)
                got(dve, ("o", h))
                free(V_.tensor_copy(MIX[r0:r0 + HD, h // 2, :], PS[r0:r0 + HD, 6, :]), ("o", h))

            def diff_out(h):
                got(dve, ("do", h))
                free(V_.tensor_copy(MIX[:, 4 + h, :], PS[:, bank(("do", h)), :]), ("do", h))

            for i in range(SB_HEADS + 1):
                if i < SB_HEADS:
                    dve.wait_ge(S("ln_ready"), i + 1)
                    V_.scalar_tensor_tensor(SP[:, i % 2, :], Z[:, i % 3, :], 0.0, SP[:, i % 2, :], ALU.max, ADD)\
                        .then_inc(S("sp_ready"), 1)
                    got(dve, ("rot", i))
                    dve.wait_ge(S("cos_part"), i + 1)
                    RB = MIX[:, 4 + i % 2, :]
                    if i == 0:
                        dve.wait_ge(S("rope_normed"), 8)
                    if i >= 2:
                        dve.wait_ge(S("rope_done"), i - 1)
                    free(V_.tensor_tensor(RB, PS[:, 7, :], SIN, MUL), ("rot", i))
                    dve.wait_ge(*freed(("rot", i)))
                    V_.tensor_tensor(QK[:, 8 + i, :], RB, MIX[:, 6 + i % 2, :], ADD).then_inc(S("rope_done"), 1)
                if i >= 1:
                    h = i - 1
                    got(dve, ("c", h))
                    free(V_.tensor_tensor(Z[:, h % 3, :], Z[:, h % 3, :],
                                          PS[:, 3:6, :].rearrange("p a n -> p (a n)")[:, 0:1280], SUB), ("c", h))
                if i >= 2:
                    stick_out(i - 2)
            stick_out(SB_HEADS - 1)
            dve.wait_ge(S("rope_done"), 8)
            for n in range(DIFF_HEADS * QB + 1):
                if n < DIFF_HEADS * QB:
                    qb, b0 = n % QB, 2 * (n % 2)
                    N = (qb + 1) * P
                    got(dve, ("s", n))
                    link(V_.tensor_tensor(PS[:, b0:b0 + 2, qb * P:N], PS[:, b0:b0 + 2, qb * P:N],
                                          causal.unsqueeze(1).to_broadcast([P, 2, P]), ADD))
                    link(V_.tensor_reduce(small[:, 8:10], PS[:, b0:b0 + 2, 0:N], AX_X, ALU.max))
                    V_.tensor_scalar(small[:, 16 + 2 * (n % 2):18 + 2 * (n % 2)], small[:, 8:10], -HD ** -0.5, None, MUL)\
                        .then_inc(S("diff_max"), 1)
                    dve.wait_ge(S("diff_max"), n + 1)
                if n >= 1:
                    m = n - 1
                    N = (m % QB + 1) * P
                    s0 = 24 + 2 * (m % 2)
                    dve.wait_ge(*freed(("s", m)))
                    dve.wait_ge(S("diff_exp0"), m + 1)
                    link(V_.reciprocal(small[:, s0:s0 + 2], small[:, s0:s0 + 2]))
                    link(V_.tensor_tensor(small[:, s0 + 1:s0 + 2], small[:, s0 + 1:s0 + 2], small[:, 4:5], MUL))
                    link(V_.tensor_scalar(DA2[:, m % 2, 0:N], PR[:, m % 2, 1, 0:N], small[:, s0 + 1:s0 + 2], None, MUL))
                    if m >= 2:
                        got(dve, ("at", m - 2))
                    V_.scalar_tensor_tensor(DA[:, m % 2, 0:N], PR[:, m % 2, 0, 0:N], small[:, s0:s0 + 1],
                                            DA2[:, m % 2, 0:N], MUL, ADD).then_inc(S("diff_map"), 1)
                    dve.wait_ge(S("diff_map"), m + 1)
                if n >= QB + 2 and (n - 2) % QB == 0:
                    diff_out((n - 2) // QB - 1)
            diff_out(DIFF_HEADS - 1)
            for h in range(DIFF_HEADS):
                dve.wait_ge(*freed(("sl", h)))
                R = QK[:, h, :]
                link(V_.reciprocal(R, R))
                V_.scalar_tensor_tensor(MIX[:, 4 + h, :], MIX[:, 4 + h, :], small[:, 5:6], R, MUL, MUL).then_inc(S("mix_ready"), 1)
            for m in range(DT):
                got(dve, ("wo", m))
                free(V_.tensor_tensor(H[:, m, META:T2], H[:, m, META:T2], PS[:, m % 4, :], ADD), ("wo", m))
            norm_apply("n2", lambda k: H[:, k, META:T2], lambda k: U[:, k, 0:SEQ], "u_ready")
            for m in range(FFT):
                got(dve, ("up", m))
                dve.wait_ge(*freed(("ga", m)))
                free(V_.tensor_tensor(G[:, m, :], SG[:, m % 2, :], PS[:, 2 * (m % 3) + 1, :], MUL), ("up", m))
            for m in range(DT):
                got(dve, ("dn", m))
                b = 2 * ((m // 2) % 3) + m % 2
                free(V_.tensor_tensor(H[:, m, META:T2], H[:, m, META:T2], PS[:, b, :], ADD), ("dn", m))
            norm_apply("n3", lambda k: H[:, k, :], lambda k: U[:, k, :], "u_ready")
            for v in (XP[:, :, 0:3], XP[:, :, 3 + T2:6 + T2], CP[:, :, 0:15], CP[:, :, 15 + T2:30 + T2]):
                V_.memset(v, 0.0).then_inc(S("pads"), 1)
            dve.wait_ge(S("dt_parts"), 2)
            V_.scalar_tensor_tensor(DTF[0:64, 0, :], DTF[0:64, 1, :], 0.0, DTF[0:64, 2, :], ALU.max, ADD).then_inc(S("dt_done"), 1)
            dve.wait_ge(S("dt_done"), 1)
            V_.tensor_scalar(DTF[0:64, 5, :], DTF[0:64, 0, :], small[0:64, 32:33], -1.0, MUL, MUL).then_inc(S("dt_done"), 1)
            for part, dst in enumerate((DTT, AAT)):
                got(dve, ("dtT", part))
                link(V_.tensor_copy(dst[:, 0:4, :], PS[:, 2 + part, 0:256].rearrange("p (c n) -> p c n", c=4)))
                free(V_.tensor_copy(dst[0:META, 4, :], PS[0:META, 2 + part, 256:320]), ("dtT", part))
            dve.wait_ge(*freed(("dtT", 1)))
            got(dve, "F")
            got(dve, "TOT")
            free(V_.tensor_copy(ET[:, :, :], PS[:, 5, 0:320].rearrange("p (c n) -> p c n", c=NC)), "TOT")
            dve.wait_ge(*freed("TOT"))
            for n, cs in ((P, slice(0, 4)), (META, slice(4, 5))):
                lo, hi = cs.start * 64, cs.stop * 64
                k = cs.stop - cs.start
                ins = V_.tensor_copy(FT[0:n, cs, :], PS[0:n, 4, lo:hi].rearrange("p (c n) -> p c n", c=k))
                if n == P:
                    link(ins)
                else:
                    free(ins, "F")
                    dve.wait_ge(*freed("F"))
                ins = V_.tensor_tensor(W2[0:n, cs, :], ET[0:n, cs, :], FT[0:n, cs, :], SUB)
                ins.then_inc(S("w2_arg"), 1)
            dve.wait_ge(S("ssd_exp"), 5)
            link(V_.tensor_tensor(W2[:, 0:4, :], W2[:, 0:4, :], DTT[:, 0:4, :], MUL))
            V_.tensor_tensor(W2[0:META, 4, :], W2[0:META, 4, :], DTT[0:META, 4, :], MUL).then_inc(S("w2_ready"), 1)
            dve.wait_ge(S("w2_ready"), 1)
            dve.wait_ge(S("pads"), 4)

            def conv(out_, src, taps, w0, done, bias=None):
                if bias is None:
                    link(V_.tensor_scalar(out_, src[:, 0:T2], par[:, w0:w0 + 1], None, MUL))
                else:
                    link(V_.tensor_scalar(out_, src[:, 0:T2], par[:, w0:w0 + 1], bias, MUL, ADD))
                for j in range(1, taps):
                    ins = V_.scalar_tensor_tensor(out_, src[:, j:j + T2], par[:, w0 + j:w0 + j + 1], out_, MUL, ADD)
                    if j < taps - 1:
                        link(ins)
                    else:
                        ins.then_inc(S(done), 1)

            def bc(ap, n, w):
                return ap.unsqueeze(2).to_broadcast([n, GH, w])

            for g in range(GROUPS):
                h8 = slice(GH * g, GH * g + GH)
                h8b = slice(32 + GH * g, 32 + GH * g + GH)
                for t in range(6):
                    i = 6 * g + t
                    dve.wait_ge(*freed(("xb", g, t)))
                    j = 16 + (0 if t == 2 else 4) + g if t in (2, 5) else 4 * g + (t if t < 2 else t - 1)
                    if i >= 2:
                        g2, t2 = divmod(i - 2, 6)
                        if t2 in (2, 5):
                            dve.wait_ge(S("conv_ready"), i - 1)
                        else:
                            got(dve, ("tr", g2, t2))
                    conv(CO[:, (6 * g + t) % 2, :], XP[:, i % 2, :], SSM_TAPS, PARAMS["ssm_w"] + j * SSM_TAPS, "conv_done")
                for s, c in enumerate(range(NC - 1, 0, -1)):
                    t0, n = CHUNKS[c]
                    got(dve, ("sb", g, c))
                    dst = SNAP[:, c - 1, :]
                    if g > 0 and s == 0:
                        got(dve, ("ob", g - 1, 3))
                    if c == NC - 1:
                        ins = V_.tensor_copy(dst, PS[:, 6, :])
                    else:
                        link(V_.tensor_tensor(dst.rearrange("p (h w) -> p h w", h=GH),
                                              SNAP[:, c, :].rearrange("p (h w) -> p h w", h=GH),
                                              bc(ET[:, c, h8b], P, HD), MUL))
                        ins = V_.tensor_tensor(dst, dst, PS[:, 6, :], ADD)
                    free(ins, ("sb", g, c))
                    dve.wait_ge(*freed(("sb", g, c)))
                for c, (t0, n) in enumerate(CHUNKS):
                    i = NC * g + c
                    F = FR[i % 2]
                    got(dve, ("cb", g, c))
                    link(V_.tensor_tensor(CBM[0:n, 0, 0:n], PS[0:n, 4, 0:n], upper[0:n, 0:n], MUL))
                    free(V_.tensor_tensor(CBM[0:n, 1, 0:n], PS[0:n, 4, 0:n], lower[0:n, 0:n], MUL), ("cb", g, c))
                    dve.wait_ge(S(f"fr_in{i % 2}"), 32 * (i // 2 + 1))
                    link(V_.tensor_tensor(F[0][0:n, :, 0:n], F[0][0:n, :, 0:n], bc(FT[0:n, c, h8], n, n), SUB))
                    dve.wait_ge(S("t2_ready"), i + 1)
                    V_.tensor_tensor(F[0][0:n, :, 0:n], F[0][0:n, :, 0:n], F[1][0:n, :, 0:n], ALU.min).then_inc(S("min_ready"), 1)
                    if i >= 1:
                        got(dve, ("yd", (i - 1) // NC, (i - 1) % NC))
                    link(V_.tensor_tensor(M1[0:n, :, 0:n], CBM[0:n, 0, 0:n].unsqueeze(1).to_broadcast([n, GH, n]),
                                          bc(DTT[0:n, c, h8], n, n), MUL))
                    dve.wait_ge(S("n1_ready"), i + 1)
                    V_.tensor_tensor(M1[0:n, :, 0:n], M1[0:n, :, 0:n], F[1][0:n, :, 0:n], ADD).then_inc(S("m_sum"), 1)
                    if i >= 1:
                        got(dve, ("yt", (i - 1) // NC, (i - 1) % NC))
                    dve.wait_ge(S("xd_ready"), i + 1)
                    yc = YC[0:n, :]
                    yh = yc.rearrange("p (h w) -> p h w", h=GH)
                    if c > 0:
                        got(dve, ("of", g, c))
                        link(V_.tensor_tensor(yh, PS[0:n, 6, :].rearrange("p (h w) -> p h w", h=GH),
                                              bc(EF[0:n, c, h8], n, HD), MUL))
                        free(V_.tensor_tensor(yc, yc, XD[0:n, :], ADD), ("of", g, c))
                        dve.wait_ge(*freed(("of", g, c)))
                        base = yc
                    else:
                        base = XD[0:n, :]
                    if c < 4:
                        got(dve, ("ob", g, c))
                        tmp = YB[0:n, :]
                        free(V_.tensor_tensor(tmp.rearrange("p (h w) -> p h w", h=GH),
                                              PS[0:n, 7, :].rearrange("p (h w) -> p h w", h=GH),
                                              bc(EF[0:n, c, h8b], n, HD), MUL), ("ob", g, c))
                        dve.wait_ge(*freed(("ob", g, c)))
                        link(V_.tensor_tensor(yc, base, tmp, ADD))
                        base = yc
                    got(dve, ("yd", g, c))
                    free(V_.tensor_tensor(yc, base, PS[0:n, 5, :], ADD), ("yd", g, c))
                    if c < 4:
                        got(dve, ("sf", g, c))
                        st = ST[:, c % 2, :]
                        if c == 0:
                            ins = V_.tensor_copy(st, PS[:, 6, :])
                        else:
                            link(V_.tensor_tensor(st.rearrange("p (h w) -> p h w", h=GH),
                                                  ST[:, (c - 1) % 2, :].rearrange("p (h w) -> p h w", h=GH),
                                                  bc(ET[:, c, h8], P, HD), MUL))
                            ins = V_.tensor_tensor(st, st, PS[:, 6, :], ADD)
                        free(ins, ("sf", g, c))
                        dve.wait_ge(*freed(("sf", g, c)))
                    if c % 2 == 1:
                        u = 2 * g + c // 2
                        got(dve, ("ca", u))
                        dve.wait_ge(*freed(("cg", u)))
                        b = bank(("ca", u))
                        if u >= 2:
                            dve.wait_ge(S("cacc_done"), u - 1)
                        free(V_.tensor_tensor(tok(CP[:, u % 2, 15:15 + T2], T2), tok(SGB[:, :], T2), PS[:, b:b + 2, 0:HT],
                                              MUL), ("ca", u))
                    got(dve, ("yt", g, c))
                    if c == 0:
                        dve.wait_ge(*freed(("zt", 4 * g + 3)))
                    yv = YT[:, 4 * g:4 * g + 4, t0:t0 + n]
                    free(V_.tensor_tensor(yv, yv, PS[:, 5, :].rearrange("p (j n) -> p j n", j=4)[:, :, 0:n], MUL), ("yt", g, c))
                    dve.wait_ge(*freed(("yt", g, c)))
                for u in (2 * g, 2 * g + 1):
                    if u == 0:
                        dve.wait_ge(S("h_saved"), 16)
                    dve.wait_ge(*freed(("ca", u)))
                    conv(CACC[:, u, :], CP[:, u % 2, :], CONF_TAPS, PARAMS["conf_w"] + u * CONF_TAPS, "cacc_done",
                         bias=pcol("conf_b", u))
                    dve.wait_ge(S("cacc_done"), u + 1)
            got(dve, "lnm")
            mean = GT[:, 0, :]
            free(V_.tensor_scalar(tok(mean, T2), PS[:, 6:8, 0:HT], 1.0 / D, None, MUL), "lnm")
            dve.wait_ge(*freed("lnm"))
            for k in range(DT):
                V_.tensor_tensor(CACC[:, k, :], CACC[:, k, :], mean, SUB).then_inc(S("ln_centred"), 1)
            dve.wait_ge(S("ln_centred"), DT)
            norm_apply("lnv", lambda k: CACC[:, k, :], lambda k: CACC[:, k, :], "ln_scaled")
            for m in range(DT):
                got(dve, ("co", m))
                dve.wait_ge(*freed(("g1", m)))
                b = bank(("co", m))
                free(V_.tensor_tensor(tok(MG[:, m, :], T2), tok(GT[:, m % 2, :], T2), PS[:, b:b + 2, 0:HT], MUL),
                     ("co", m))
            norm_apply("ny", lambda k: YT[:, k, :], lambda k: YT[:, k, :], "y_ready")
            for m in range(DT):
                got(dve, ("so", m))
                dve.wait_ge(*freed(("g2", m)))
                b = bank(("so", m))
                free(V_.tensor_tensor(tok(GT[:, m % 2, :], T2), tok(GT[:, m % 2, :], T2), PS[:, b:b + 2, 0:HT], MUL),
                     ("so", m))
                dve.wait_ge(*freed(("so", m)))
                V_.tensor_tensor(MG[:, m, :], MG[:, m, :], GT[:, m % 2, :], ADD).then_inc(S("merged"), 1)
            dve.wait_ge(S("h_back"), 16)
            for m in range(DT):
                got(dve, ("out", m))
                b = bank(("out", m))
                free(V_.tensor_tensor(tok(H[:, m, :], T2), tok(H[:, m, :], T2), PS[:, b:b + 2, 0:HT], ADD), ("out", m))
            norm_apply("n6", lambda k: H[:, k, :], lambda k: U[:, k, :], "u_ready")
            got(dve, "lg")
            for c, (t0, n) in enumerate(CHUNKS):
                V_.tensor_reduce(small[0:n, 48 + c:49 + c], PS[0:n, 0, c * EXPERTS:(c + 1) * EXPERTS], AX_X, ALU.max,
                                 negate=True).then_inc(S("lg_max"), 1)
            dve.wait_ge(*freed("lg"))
            dve.wait_ge(S("aff_exp"), NC - 1)
            link(V_.reciprocal(small[:, 56:60], small[:, 56:60]))
            link(V_.reciprocal(small[0:META, 60:61], small[0:META, 60:61]))
            for n, cs in ((P, slice(0, 4)), (META, slice(4, 5))):
                k = cs.stop - cs.start
                V_.tensor_tensor(AFF[0:n, cs, :], AFF[0:n, cs, :],
                                 small[0:n, 56 + cs.start:56 + cs.stop].unsqueeze(2).to_broadcast([n, k, EXPERTS]),
                                 MUL).then_inc(S("aff_ready"), 1)
            E_ = EXPERTS
            TKR = [TK[0:E_, r, :] for r in range(8)]
            got(dve, "af")
            link(V_.tensor_copy(TKR[0][:, 0:512], PS[0:E_, 4, :]))
            free(V_.tensor_copy(TKR[0][:, 512:T2], PS[0:E_, 5, 0:META]), "af")
            dve.wait_ge(*freed("af"))
            src = TKR[0]
            for r in range(TOPK_ROUNDS):
                v8 = TV[0:E_, 8 * r:8 * r + 8]
                link(V_.max(v8, src))
                if r < TOPK_ROUNDS - 1:
                    link(V_.match_replace(TKR[1 + r % 2], v8, src, -1.0))
                    src = TKR[1 + r % 2]
            least = TV[0:E_, CAP - 1:CAP]
            link(V_.tensor_scalar(TKR[1], TKR[0], least, None, ALU.is_gt))
            link(V_.tensor_scalar(TKR[2], TKR[0], least, None, ALU.is_equal))
            link(V_.tensor_reduce(small[0:E_, 64:65], TKR[1], AX_X, ADD))
            link(V_.tensor_scalar(small[0:E_, 64:65], small[0:E_, 64:65], -1.0, float(CAP), MUL, ADD))
            link(V_.memset(TKR[5], 0.0))
            link(V_.tensor_tensor_scan(TKR[3], TKR[2], TKR[5], 0.0, ADD, ADD))
            link(V_.scalar_tensor_tensor(TKR[2], TKR[3], small[0:E_, 64:65], TKR[2], ALU.is_le, MUL))
            link(V_.tensor_tensor(TKR[1], TKR[1], TKR[2], ADD))
            link(V_.tensor_tensor_scan(TKR[3], TKR[1], TKR[5], 0.0, ADD, ADD))
            link(V_.tensor_tensor(TKR[3], TKR[3], TKR[1], MUL))
            V_.tensor_scalar(TKR[0], TKR[3], -1.0, None, ADD).then_inc(S("slots_ready"), 1)
            got(dve, "sl16")
            link(V_.tensor_copy(SLT[:, 0:4, :], PS[:, 0, 0:64].rearrange("p (c n) -> p c n", c=4)))
            free(V_.tensor_copy(SLT[0:META, 4, :], PS[0:META, 0, 64:80]), "sl16")
            dve.wait_ge(*freed("sl16"))
            dve.sem_inc(S("h_added"), 1)
            dve.sem_inc(S("sat_ready"), 1)
            dve.sem_inc(S("hg_ready"), 1)
            with dve.Fori(0, EXPERTS) as e:
                V_.tensor_copy(SLS[:, 0:4], SLT[:, 0:4, bass.ds(e, 1)].rearrange("p c n -> p (c n)")).then_inc(S("sel_cp"), 1)
                V_.tensor_copy(SLS[0:META, 4:5], SLT[0:META, 4, bass.ds(e, 1)]).then_inc(S("sel_cp"), 1)
                V_.tensor_copy(AFS[:, 0:4], AFF[:, 0:4, bass.ds(e, 1)].rearrange("p c n -> p (c n)")).then_inc(S("sel_cp"), 1)
                V_.tensor_copy(AFS[0:META, 4:5], AFF[0:META, 4, bass.ds(e, 1)]).then_inc(S("sel_cp"), 1)
                dve.wait_ge(S("sel_cp"), e * 4 + 4)
                dve.wait_ge(S("combined"), 1 + e * DT)
                for c, (t0, n) in enumerate(CHUNKS):
                    a = V_.tensor_scalar(SE[0:n, c, :], iota[0:n, :], SLS[0:n, c:c + 1], None, ALU.is_equal)
                    b = V_.tensor_scalar(SA[0:n, c, :], iota[0:n, :], SLS[0:n, c:c + 1], AFS[0:n, c:c + 1], ALU.is_equal, MUL)
                    if c == NC - 1:
                        a.then_inc(S("sel_ready"), 1)
                        b.then_inc(S("sel_ready"), 1)
                    else:
                        a.then_inc(S("sel_part"), 1)
                        b.then_inc(S("sel_part"), 1)
                dve.wait_ge(S("sel_part"), e * 8 + 8)
                dve.wait_ge(S("sel_ready"), e * 2 + 2)
                for b in range(4):
                    dve.wait_ge(S("up_done"), e * 4 + b + 1)
                    dve.wait_ge(S("gate_act"), e * 4 + b + 1)
                    V_.tensor_tensor(HG[:, 4 * b:4 * b + 4, :].rearrange("p k n -> p (k n)"), SIL[:, b % 2, :],
                                     PS[:, 4 + b % 2, 0:4 * CAP], MUL).then_inc(S("hg_ready"), 1)
                dve.wait_ge(S("sa_turned"), e + 1)
                V_.tensor_copy(SAT[0:CAP, 0:512], PS[0:CAP, 2, :]).then_inc(S("sat_part"), 1)
                V_.tensor_copy(SAT[0:CAP, 512:T2], PS[0:CAP, 3, 0:META]).then_inc(S("sat_ready"), 1)
                for m in range(DT):
                    dve.wait_ge(S("combined"), 1 + e * DT + m + 1)
                    b = 4 + 2 * (m % 2)
                    V_.tensor_tensor(tok(H[:, m, :], T2), tok(H[:, m, :], T2), PS[:, b:b + 2, 0:HT], ADD)\
                        .then_inc(S("h_added"), 1)
            dve.wait_ge(S("h_added"), 1 + EXPERTS * DT)
            norm_apply("n7", lambda k: H[:, k, :], lambda k: U[:, k, :], "y_out")

        @blk.gpsimd
        def _(pool):
            G_ = nc.gpsimd
            MUL, SUB = ALU.mult, ALU.subtract

            def mask(buf, fill):
                for kb in range(QB):
                    v = buf[:, ZO[kb]:ZO[kb] + P]
                    last = G_.affine_select(out=v, in_=v, compare_op=ALU.is_gt, fill=fill, base=0,
                                            pattern=[[1, P]], channel_multiplier=-1)
                return last

            pool.wait_ge(S("consts_in"), 48)
            for i in range(SB_HEADS + 1):
                if i < SB_HEADS:
                    if i == 0:
                        pool.wait_ge(S("rope_normed"), 8)
                    if i >= 2:
                        pool.wait_ge(S("rope_done"), i - 1)
                    G_.tensor_tensor(MIX[:, 6 + i % 2, :], QK[:, 8 + i, :], COS, MUL).then_inc(S("cos_part"), 1)
                    pool.wait_ge(S("sp_ready"), i + 1)
                    mask(SP[:, i % 2, :], 0.0).then_inc(S("sp_masked"), 1)
                if i >= 1:
                    pool.wait_ge(*freed(("c", i - 1)))
                    mask(Z[:, (i - 1) % 3, :], -BIG).then_inc(S("arg_masked"), 1)
            pool.wait_ge(*freed(("dn", DT - 1)))
            pool.dma_start(h_dram, H[:, :, :]).then_inc(S("h_saved"), 16)

            def bc(ap, n, w):
                return ap.unsqueeze(2).to_broadcast([n, GH, w])

            def scaled(dst, g, c, n, by, sem):
                G_.tensor_tensor(dst[0:n].rearrange("p (h w) -> p h w", h=GH),
                                 XS[0:n, c, :].rearrange("p (h w) -> p h w", h=GH), bc(by, n, HD), MUL)\
                    .then_inc(S(sem), 1)

            pool.wait_ge(S("w2_ready"), 1)
            for g in range(GROUPS):
                h8 = slice(GH * g, GH * g + GH)
                h8b = slice(32 + GH * g, 32 + GH * g + GH)
                pool.wait_ge(*freed(("tr", g, 4)))
                for s, c in enumerate(range(NC - 1, 0, -1)):
                    n = CHUNKS[c][1]
                    if s >= 2:
                        got(pool, ("sb", g, c + 2))
                    elif g > 0:
                        got(pool, ("sf", g - 1, 3))
                    scaled(XW[:, s % 2, :], g, c, n, W2[0:n, c, h8b], "xwb_ready")
                for c, (t0, n) in enumerate(CHUNKS):
                    i = NC * g + c
                    F = FR[i % 2]
                    pool.wait_ge(S(f"fr_in{i % 2}"), 32 * (i // 2 + 1))
                    G_.tensor_tensor(F[1][0:n, :, 0:n], F[1][0:n, :, 0:n], bc(FT[0:n, c, h8b], n, n), SUB)\
                        .then_inc(S("t2_ready"), 1)
                    if i >= 1:
                        pool.wait_ge(*freed(("yd", (i - 1) // NC, (i - 1) % NC)))
                    scaled(XD, g, c, n, par[0:n, PARAMS["ssm_d"] + GH * g:PARAMS["ssm_d"] + GH * g + GH], "xd_ready")
                    if c < 4:
                        if c >= 2:
                            got(pool, ("sf", g, c - 2))
                        else:
                            got(pool, ("sb", g, 1))
                        scaled(XW[:, c % 2, :], g, c, n, W2[0:n, c, h8], "xwf_ready")
                    pool.wait_ge(S("min_ready"), i + 1)
                    pool.wait_ge(*freed(("cb", g, c)))
                    G_.tensor_tensor(F[1][0:n, :, 0:n], CBM[0:n, 1, 0:n].unsqueeze(1).to_broadcast([n, GH, n]),
                                     bc(DTT[0:n, c, h8b], n, n), MUL).then_inc(S("n1_ready"), 1)
                    pool.wait_ge(S("m_sum"), i + 1)
                    pool.wait_ge(S("e_ready"), i + 1)
                    G_.tensor_tensor(M1[0:n, :, 0:n], M1[0:n, :, 0:n], F[0][0:n, :, 0:n], MUL).then_inc(S("m_ready"), 1)
            got(pool, ("co", DT - 1))
            pool.wait_ge(S("h_saved"), 16)
            pool.dma_start(H[:, :, :], h_dram).then_inc(S("h_back"), 16)

        @blk.sync
        def _(sp):
            sp.dma_start(consts[:, :], inp["consts"]).then_inc(S("consts_in"), 16)
            sp.dma_start(par[:, :], inp["params"]).then_inc(S("consts_in"), 16)
            sp.dma_start(arena[:, 16384:17408], inp["rope"]).then_inc(S("consts_in"), 16)

            def slot_free(n):
                tag = last_read[loads[n][0]]
                if tag[0] == "sem":
                    sp.wait_ge(S(tag[1]), tag[2])
                else:
                    got(sp, tag)

            for n, (name, put) in enumerate(loads):
                if n >= RING:
                    slot_free(n - RING)
                if name == ("g1", 0):
                    sp.wait_ge(S("m_ready"), NC * GROUPS)
                for at, k, cols, src in put:
                    sp.dma_start(ring[:, n % RING, at:at + k * cols].rearrange("p (k n) -> p k n", k=k), src)\
                        .then_inc(S(f"ring{n % RING}"), 16)

            def expert_load(e, i):
                s = (N_DENSE + i) % RING
                if i < 8:
                    w = inp[("w_exp_gate_2", "w_exp_up_2")[i % 2]]
                    src = w[bass.ds(e, 1), :, (i // 2) * 512:(i // 2) * 512 + 512]
                    k = DT
                else:
                    src = inp["w_exp_down_2"][bass.ds(e, 1), :, (i - 8) * 256:(i - 8) * 256 + 256]
                    k = EFT
                sp.dma_start(ring[:, s, :].rearrange("p (k n) -> p k n", k=k),
                             src.rearrange("o (k p) n -> p (o k) n", p=P)).then_inc(S(f"ring{s}"), 16)

            def expert_read(e, i):
                if i < 8:
                    sp.wait_ge(S(("gate_done", "up_done")[i % 2]), e * 4 + i // 2 + 1)
                else:
                    sp.wait_ge(S("down_done"), e * 4 + i - 8 + 1)
                sp.sem_inc(S("slots_turned"), 1)

            for i in range(RING):
                slot_free(N_DENSE - RING + i)
                expert_load(0, i)
            with sp.Fori(0, EXPERTS - 1) as e:
                for i in range(RING, 12):
                    expert_read(e, i - RING)
                    expert_load(e, i)
                for i in range(RING):
                    expert_read(e, 12 - RING + i)
                    expert_load(e + 1, i)
            for i in range(RING, 12):
                expert_read(EXPERTS - 1, i - RING)
                expert_load(EXPERTS - 1, i)
            for k in range(DT):
                sp.wait_ge(S("y_out"), k + 1)
                sp.dma_start(out[k * P:(k + 1) * P, :], U[:, k, META:T2]).then_inc(S("stored"), 16)
            sp.wait_ge(S("stored"), 16 * DT)


WEIGHTS = ["w_in", "w_o", "w_gate", "w_up", "w_down", "w_in_2", "w_conf_out_2", "w_ssm_out_2", "w_out_2",
           "w_exp_gate_2", "w_exp_up_2", "w_exp_down_2"]


def shape_constants():
    i = np.arange(P)
    c = np.zeros((P, N_CONSTS), np.float32)
    put = lambda name, a: c.__setitem__((slice(None), slice(CONSTS[name], CONSTS[name] + a.shape[1])), a)
    put("ident", np.eye(P))
    put("ones", np.ones((P, P)))
    put("upper", (i[:, None] <= i[None, :]).astype(float))
    put("lower", (i[:, None] >= i[None, :]).astype(float))
    put("heads", (i[:, None] // HD == i[None, :] // HD).astype(float))
    rot = np.zeros((P, P))
    for h0 in (0, HD):
        for r in range(HD // 2):
            rot[h0 + HD // 2 + r, h0 + r] = -1.0
            rot[h0 + r, h0 + HD // 2 + r] = 1.0
    put("rot", rot)
    put("iota", np.broadcast_to(np.arange(CAP), (P, CAP)))
    put("causal", np.where(i[None, :] > i[:, None], -BIG, 0.0))
    freq = (np.float32(10000.0) ** (-np.arange(HD // 2, dtype=np.float32) / np.float32(HD // 2))).astype(np.float32)
    ang = (np.arange(SEQ, dtype=np.float32)[None, :] * freq[i % (HD // 2), None]).astype(np.float32).astype(np.float64)
    return c, np.concatenate([np.cos(ang), np.sin(ang)], axis=1).astype(np.float32)


def kernel(**inputs):
    import numpy as np
    import concourse.bacc as bacc
    from concourse.bass_utils import run_bass_kernel_spmd

    x = {k: np.asarray(v) for k, v in inputs.items()}
    par = np.zeros((P, N_PARAMS), np.float32)

    def put(name, a):
        a = a.reshape(a.shape[0], -1)
        par[:a.shape[1], PARAMS[name]:PARAMS[name] + a.shape[0]] = a.T

    tiles = lambda v: v.reshape(-1, P)
    put("attn_g", tiles(x["attn_norm_g"]))
    put("ffn_g", tiles(x["ffn_norm_g"]))
    put("mix_g", tiles(x["w_norm_mix_2"]))
    put("ffn2_g", tiles(x["w_norm_ffn_2"]))
    put("final_g", tiles(x["w_norm_final_2"]))
    put("subln_g", tiles(x["diff_subln_g"]))
    for name in ("q_g", "k_g"):
        g = x[f"diff_{name[0]}_norm_g"].reshape(-1)
        put(name, np.concatenate([g, g])[None])
    put("lam", np.stack([x[f"lambda_{n}"].reshape(-1) for n in ("q1", "k1", "q2", "k2")]))
    put("conf_w", x["w_conf_dw_2"][0].reshape(CONF_TAPS, DT, P).transpose(1, 0, 2).reshape(-1, P))
    put("conf_b", tiles(x["b_conf_dw_2"]))
    put("ln_g", tiles(x["conf_ln_g_2"]))
    put("ln_b", tiles(x["conf_ln_b_2"]))
    put("ssm_w", x["w_ssm_conv_2"][0].reshape(SSM_TAPS, 24, P).transpose(1, 0, 2).reshape(-1, P))
    put("ssm_b", tiles(x["b_ssm_conv_2"]))
    put("ssm_norm_g", tiles(x["w_ssm_norm_2"]))
    put("dt_bias", x["ssm_dt_bias_2"].reshape(1, 64))
    put("a_log", x["ssm_a_log_2"].reshape(1, 64))
    par[:, PARAMS["ssm_d"]:PARAMS["ssm_d"] + HEADS] = x["ssm_d_2"].reshape(1, HEADS)
    par[:, PARAMS["router"]:PARAMS["router"] + DT * EXPERTS] = \
        x["w_router_2"][0].reshape(DT, P, EXPERTS).transpose(1, 0, 2).reshape(P, -1)
    par[:, PARAMS["eps"]] = EPS
    par[:, PARAMS["subln_eps"]] = SUBLN_EPS
    par[:, PARAMS["one"]] = 1.0
    consts, rope = shape_constants()
    arrays = {"params": par, "consts": consts, "rope": rope,
              "h_t": np.ascontiguousarray(np.concatenate([x["meta_tokens_2"], x["x"][0]], axis=0).T)}
    for name in WEIGHTS:
        arrays[name] = np.ascontiguousarray(x[name][0])

    nc = bacc.Bacc("TRN2", target_bir_lowering=False, num_devices=1)
    inp = {k: nc.dram_tensor(k, a.shape, mybir.dt.from_np(a.dtype), kind="ExternalInput").ap() for k, a in arrays.items()}
    out = nc.dram_tensor("out_t", (D, SEQ), F32, kind="ExternalOutput").ap()
    program(nc, inp, out)
    r = run_bass_kernel_spmd(nc, [arrays], core_ids=[0])
    return np.ascontiguousarray(np.asarray(r.results[0]["out_t"]).T)[None]
```

```python
import math
from contextlib import ExitStack

import concourse.bass as bass
import numpy as np
from concourse import mybir

F32, F32R = mybir.dt.float32, mybir.dt.float32r
ALU = mybir.AluOpType
ACT = mybir.ActivationFunctionType
AX_X = mybir.AxisListType.X

P = 128
D = 1024
DT = D // P
SEQ = 512
META = 16
T2 = SEQ + META
HT = T2 // 2
HD = 64
QB = SEQ // P
SB_HEADS, DIFF_HEADS = 8, 4
FF = 2816
FFT = FF // P
CONF_TAPS, SSM_TAPS = 31, 7
INNER, GROUPS, STATE, HEADS = 2048, 4, 128, 32
GH = HEADS // GROUPS
OFF_G, OFF_Z = 1024, 2048
OFF_X = OFF_Z + INNER
OFF_B = OFF_X + INNER
OFF_C = OFF_B + GROUPS * STATE
OFF_DT = OFF_C + GROUPS * STATE
OFF_GATE = OFF_DT + 2 * HEADS
EXPERTS, EFF = 16, 2048
EFT = EFF // P
CAP = 2 * T2 // EXPERTS
CHUNKS = [(c * P, min(P, T2 - c * P)) for c in range(-(-T2 // P))]
NC = len(CHUNKS)
SLOT = 4096
E_LOADS = 12
PIECE = 1024
PIECES = E_LOADS * SLOT // PIECE
PBUF = 4
RING = 4
BIG = 1e30
LAMBDA_INIT = 0.8 - 0.6 * math.exp(0.0)
EPS, SUBLN_EPS = 1e-6, 1e-5
TOPK_ROUNDS = -(-CAP // 8)

COMBINE_AT = [4 + 3 * m for m in range(DT)]
TURN_H_AT = [9, 17, 25, 33]
SLOTS_AT = 28
GATHER_AT = [35, 36]
TURN_X_AT = [38, 39]

PARAMS = {}
CONSTS = {}


def _columns(table, sizes):
    at = 0
    for name, n in sizes:
        table[name] = at
        at += n
    return at


N_PARAMS = _columns(PARAMS, [
    ("attn_g", DT), ("ffn_g", DT), ("mix_g", DT), ("ffn2_g", DT), ("final_g", DT), ("subln_g", 1),
    ("q_g", 1), ("k_g", 1), ("lam", 4), ("conf_w", DT * CONF_TAPS), ("conf_b", DT), ("ln_g", DT),
    ("ln_b", DT), ("ssm_w", 24 * SSM_TAPS), ("ssm_b", 24), ("ssm_norm_g", 16), ("dt_bias", 1),
    ("a_log", 1), ("ssm_d", HEADS), ("router", DT * EXPERTS), ("eps", 1), ("subln_eps", 1), ("one", 1)])
N_CONSTS = _columns(CONSTS, [
    ("ident", P), ("ones", P), ("upper", P), ("lower", P), ("heads", P), ("rot", P), ("iota", CAP),
    ("causal", P)])


def program(nc, inp, out):
    ctx = ExitStack()
    with ctx:
        def sb(name, shape):
            return ctx.enter_context(nc.sbuf_tensor(name, shape, F32))

        sems = {}

        def S(name):
            if name not in sems:
                sems[name] = ctx.enter_context(nc.semaphore(name))
            return sems[name]

        H = sb("H", [P, DT, T2])
        ring = sb("ring", [P, RING, SLOT])
        consts = sb("consts_sb", [P, N_CONSTS])
        par = sb("par", [P, N_PARAMS])
        SQ = sb("SQ", [P, 2, T2])
        RS = sb("RS", [P, T2])
        AR = 24200
        small = sb("small", [P, 256])
        before = ExitStack()
        U = before.enter_context(nc.sbuf_tensor("U", [P, DT, T2], F32))
        arena = before.enter_context(nc.sbuf_tensor("arena", [P, AR], F32))
        before.close()

        def parts(name, shape):
            return ctx.enter_context(nc.sbuf_tensor(name, shape, F32R))

        WS = parts("WS", [P, 2, PBUF, PIECE])
        XG = parts("XG", [P, 2, DT, CAP])
        SE = parts("SE", [P, NC, CAP])
        HG = parts("HG", [P, 2, EFT, CAP])
        YE = parts("YE", [P, 2, D])
        SAT = parts("SAT", [P, T2])
        XNT = parts("XNT", [P, 2, NC, D])
        XGS, SIL, HGS, AFF, SLT, _end = [arena[:, o:o + n] for o, n in (
            (20288, D), (21312, D), (22336, D), (23360, NC * EXPERTS), (23440, NC * EXPERTS), (23520, 8))]
        SIL, HGS = [v.rearrange("p (b n) -> p b n", b=2) for v in (SIL, HGS)]
        AFF, SLT = [v.rearrange("p (c n) -> p c n", c=NC) for v in (AFF, SLT)]
        assert 2 * PBUF * PIECE + 2 * CAP * (DT + EFT) + NC * CAP + 2 * D + T2 + 2 * NC * D <= DT * T2 + 20288
        ctx.enter_context(nc.sbuf_tensor("tail", [P, DT * T2 + AR - (2 * PBUF * PIECE + 2 * CAP * (DT + EFT) + NC * CAP
                                                                    + 2 * D + T2 + 2 * NC * D)], F32))
        PS = ctx.enter_context(nc.psum_tensor("PS", [P, 8, 512], F32))
        fr_dram = nc.dram_tensor("ssd_sums", [2 * HEADS, T2], F32).ap()
        h_dram = nc.dram_tensor("residual", [P, DT, T2], F32).ap()

        def area(sizes):
            at, views = 0, []
            for shape in sizes:
                n = int(np.prod(shape))
                v = arena[:, at:at + n]
                if len(shape) == 2:
                    v = v.rearrange("p (a b) -> p a b", a=shape[0])
                if len(shape) == 3:
                    v = v.rearrange("p (a b c) -> p a b c", a=shape[0], b=shape[1])
                views.append(v)
                at += n
            assert at <= AR, at
            return views

        def C(name, n=P):
            return consts[:, CONSTS[name]:CONSTS[name] + n]

        def pcol(name, i=0):
            return par[:, PARAMS[name] + i:PARAMS[name] + i + 1]

        ident, ones, upper, lower = C("ident"), C("ones"), C("upper"), C("lower")
        heads_ones, rot, iota, causal = C("heads"), C("rot"), C("iota", CAP), C("causal")

        def halves(T):
            return [(0, T)] if T <= 512 else [(0, HT), (HT, T2)]

        def ps(banks, T):
            return PS[:, banks[0], 0:T] if T <= 512 else PS[:, banks[0]:banks[0] + 2, 0:HT]

        def tok(ap, T):
            return ap if T <= 512 else ap.rearrange("p (h n) -> p h n", h=2)

        QK, V, MIX, COS, SIN, Z, SP = area([(16, SEQ), (QB, D), (DT, SEQ), (SEQ,), (SEQ,), (3, 1280), (2, 1280)])
        scr = arena[:, 17408:17408 + 6400]
        PR = scr[:, 0:2048].rearrange("p (b c n) -> p b c n", b=2, c=2)
        DA = scr[:, 2048:3072].rearrange("p (b n) -> p b n", b=2)
        DAT = scr[:, 3072:4096].rearrange("p (b n) -> p b n", b=2)
        DA2 = scr[:, 4096:5120].rearrange("p (b n) -> p b n", b=2)
        G, SG = area([(FFT, SEQ), (2, SEQ)])
        ZO = [0, 512, 1024, 896]
        (XS, BF, CF, BT, SNAP, YT, XP, CP, ST, M1, XW, YC, XD, YB, CBM, DTT, AAT, FT, EF, W2, ET) = area([
            (NC, 512), (T2,), (T2,), (NC, P), (4, 512), (16, T2), (2, T2 + SSM_TAPS - 1),
            (2, T2 + CONF_TAPS - 1), (2, 512), (GH, P), (2, 512), (512,), (512,), (512,), (2, P), (NC, 64),
            (NC, 64), (NC, 64), (NC, 64), (NC, 64), (NC, 64)])
        CACC = H
        CO = SQ
        SGB = RS
        FR = [[ring[:, 2 * b + d, 3072:4096].rearrange("p (h n) -> p h n", h=GH) for d in range(2)]
              for b in range(2)]
        MG = arena[:, 0:DT * T2].rearrange("p (a n) -> p a n", a=DT)
        GT = arena[:, 4224:4224 + 2 * T2].rearrange("p (a n) -> p a n", a=2)
        DTF = arena[:, 6304:6304 + 6 * T2].rearrange("p (a n) -> p a n", a=6)
        TK, TV = area([(8, T2), (8 * TOPK_ROUNDS,)])
        AFS, SLS = small[:, 128:129], small[:, 136:136 + NC]

        loads = []

        def rows(w, k, lo, hi):
            return w[0:k * P, lo:hi].rearrange("(k p) n -> p k n", p=P)

        def block(name, *parts):
            at, put = 0, []
            for src in parts:
                k, n = src.shape[1], src.shape[2]
                put.append((at, k, n, src))
                at += k * n
            assert at <= SLOT
            loads.append((name, put))

        w1, w2 = inp["w_in"], inp["w_in_2"]
        for b in range(6):
            block(("in", b), rows(w1, DT, b * 512, b * 512 + 512))
        for b in range(2):
            block(("wo", b), rows(inp["w_o"], DT, b * 512, b * 512 + 512))
        for b in range(FFT // 2):
            block(("gu", b), rows(inp["w_gate"], DT, b * 256, b * 256 + 256),
                  rows(inp["w_up"], DT, b * 256, b * 256 + 256))
        for b in range(4):
            for kh in range(2):
                block(("down", b, kh), inp["w_down"][kh * 11 * P:(kh + 1) * 11 * P, b * 256:b * 256 + 256]
                      .rearrange("(k p) n -> p k n", p=P))
        block(("dt",), rows(w2, DT, OFF_DT, OFF_DT + 64))
        for g in range(GROUPS):
            for i in range(2):
                bc = (OFF_B, OFF_C)[i] + g * P
                block(("xbc", g, i), rows(w2, DT, OFF_X + g * 512 + i * 256, OFF_X + g * 512 + i * 256 + 256),
                      rows(w2, DT, bc, bc + P))
            for i in range(2):
                block(("z", g, i), rows(w2, DT, OFF_Z + g * 512 + i * 256, OFF_Z + g * 512 + i * 256 + 256))
            for i in range(2):
                u = 2 * g + i
                block(("conf", u), rows(w2, DT, u * P, u * P + P), rows(w2, DT, OFF_G + u * P, OFF_G + u * P + P))
        for b in range(2):
            block(("g1", b), rows(w2, DT, OFF_GATE + b * 512, OFF_GATE + b * 512 + 512))
        for b in range(2):
            block(("co", b), rows(inp["w_conf_out_2"], DT, b * 512, b * 512 + 512))
        for b in range(4):
            block(("g2", b), rows(w2, DT, OFF_GATE + D + b * 256, OFF_GATE + D + b * 256 + 256))
            block(("so", b), rows(inp["w_ssm_out_2"], 16, b * 256, b * 256 + 256))
        for b in range(2):
            block(("out", b), rows(inp["w_out_2"], DT, b * 512, b * 512 + 512))
        N_DENSE = len(loads)
        where = {name: n for n, (name, _) in enumerate(loads)}
        landed, count = {}, [0] * RING
        for n, (name, put) in enumerate(loads):
            count[n % RING] += 16 * len(put)
            landed[name] = count[n % RING]
        RING0 = list(count)
        last_read = {}

        def landed_e(eng, e, i):
            s = (N_DENSE + i) % RING
            eng.wait_ge(S(f"ring{s}"), e * (16 * E_LOADS // RING) + RING0[s] + 16 * (i // RING + 1))

        def slot(name, part=0):
            at, k, n, _ = loads[where[name]][1][part]
            return ring[:, where[name] % RING, at:at + k * n].rearrange("p (k n) -> p k n", k=k)

        uses, last_tag, order, filled_n, freed_n = [0] * 8, [None] * 8, {}, [0] * 8, [0] * 8

        def filled(tag):
            b, n = order[tag]
            return S(f"filled{b}"), n

        def freed(tag):
            b, n = order[tag]
            return S(f"freed{b}"), n

        def got(eng, tag):
            eng.wait_ge(*filled(tag))

        def free(ins, tag):
            return ins.then_inc(S(f"freed{order[tag][0]}"), 1)

        def bank(tag):
            return order[tag][0]

        def chain(eng, name):
            n = [0]

            def link(ins):
                n[0] += 1
                ins.then_inc(S(name), 1)
                eng.wait_ge(S(name), n[0])
            return link

        NORMS = [("n1", DT, SEQ, 1 / D, "eps", "attn_g"), ("n2", DT, SEQ, 1 / D, "eps", "ffn_g"),
                 ("n3", DT, T2, 1 / D, "eps", "mix_g"), ("ny", 16, T2, 1 / INNER, "eps", "ssm_norm_g"),
                 ("lnv", DT, T2, 1 / D, "eps", "ln_g"), ("n6", DT, T2, 1 / D, "eps", "ffn2_g"),
                 ("n7", DT, T2, 1 / D, "eps", "final_g")]
        sq_base, used_base = {}, {}
        a = b_ = 0
        for nm, K, *_ in NORMS:
            sq_base[nm], used_base[nm] = a, b_
            a += K
            b_ += K - 1
        NORM = {x[0]: x for x in NORMS}
        u_base = {"n1": 0, "n2": DT, "n3": 2 * DT, "n6": 3 * DT}

        blk = ctx.enter_context(nc.Block())

        @blk.tensor
        def _(pe):
            def open_(tag, *banks):
                for b in banks:
                    if last_tag[b] is not None:
                        pe.wait_ge(*freed(last_tag[b]))
                    last_tag[b] = tag
                uses[banks[0]] += 1
                order[tag] = (banks[0], uses[banks[0]])

            def fill(ins, tag):
                ins.then_inc(S(f"filled{order[tag][0]}"), 1)

            def arrived(name):
                pe.wait_ge(S(f"ring{where[name] % RING}"), landed[name])

            def dense(tag, banks, K, T, lhs, rhs, M=P, reads=None):
                open_(tag, *banks)
                for k in range(K):
                    for i, (lo, hi) in enumerate(halves(T)):
                        last = nc.tensor.matmul(PS[0:M, banks[i], 0:hi - lo], lhs(k), rhs(k)[:, lo:hi],
                                                start=(k == 0), stop=(k == K - 1))
                fill(last, tag)
                if reads:
                    last_read[reads] = tag

            def norm_sum(nm, banks):
                _, K, T, *_ = NORM[nm]
                open_(nm, *banks)
                for k in range(K):
                    pe.wait_ge(S("sq_ready"), sq_base[nm] + k + 1)
                    for i, (lo, hi) in enumerate(halves(T)):
                        last = nc.tensor.matmul(PS[:, banks[i], 0:hi - lo], ones, SQ[:, k % 2, lo:hi],
                                                start=(k == 0), stop=(k == K - 1))
                    if k < K - 1:
                        last.then_inc(S("sq_used"), 1)
                fill(last, nm)

            pe.wait_ge(S("consts_in"), 48)
            pe.wait_ge(S("lam_prod"), 1)
            open_("lam", 7)
            fill(nc.tensor.matmul(PS[:, 7, 0:2], ones[0:HD, :], small[0:HD, 0:2], start=True, stop=True), "lam")
            norm_sum("n1", (6,))
            pe.wait_ge(S("u_ready"), DT)
            n = 0
            for b, kind in enumerate(("q", "k", "v", "q", "k", "v")):
                arrived(("in", b))
                w = slot(("in", b))
                for m in range(4):
                    tag = ("in", b, m)
                    if kind == "v":
                        dense(tag, (n % 4,), DT, SEQ, lambda k: U[:, k, m * P:m * P + P], lambda k: w[:, k, :],
                              reads=("in", b))
                    else:
                        dense(tag, (n % 4,), DT, SEQ, lambda k: w[:, k, m * P:m * P + P],
                              lambda k: U[:, k, 0:SEQ], reads=("in", b))
                    n += 1
            for j in range(8):
                pe.wait_ge(S("rope_sq"), j + 1)
                open_(("rn", j), 6 + j % 2)
                fill(nc.tensor.matmul(PS[:, 6 + j % 2, :], heads_ones, SQ[:, j % 2, 0:SEQ], start=True, stop=True),
                     ("rn", j))
            for i in range(SB_HEADS + 2):
                if i < SB_HEADS:
                    j, r = i // 2, HD * (i % 2)
                    if i == 0:
                        for b in (0, 1):
                            for m in range(4):
                                pe.wait_ge(*freed(("in", b, m)))
                    open_(("z", i), 0, 1, 2)
                    for kb in range(QB):
                        o = ZO[kb]
                        last = nc.tensor.matmul(PS[:, o // 512, o % 512:o % 512 + SEQ - kb * P],
                                                QK[r:r + HD, 4 + j, kb * P:kb * P + P], QK[r:r + HD, j, kb * P:SEQ],
                                                start=True, stop=True)
                    fill(last, ("z", i))
                    pe.wait_ge(S("rope_normed"), i + 1)
                    open_(("rot", i), 7)
                    fill(nc.tensor.matmul(PS[:, 7, :], rot, QK[:, 8 + i, :], start=True, stop=True), ("rot", i))
                if 1 <= i <= SB_HEADS:
                    h = i - 1
                    pe.wait_ge(S("sp_masked"), h + 1)
                    open_(("c", h), 3, 4, 5)
                    for kb in range(QB):
                        for k2 in range(kb, QB):
                            o = ZO[kb] + (k2 - kb) * P
                            last = nc.tensor.matmul(PS[:, 3 + o // 512, o % 512:o % 512 + SEQ - k2 * P],
                                                    lower if k2 == kb else ones,
                                                    SP[:, h % 2, ZO[k2]:ZO[k2] + SEQ - k2 * P],
                                                    start=(k2 == kb), stop=(k2 == QB - 1))
                    fill(last, ("c", h))
                if i >= 2:
                    h = i - 2
                    r = HD * (h % 2)
                    pe.wait_ge(S("w_ready"), h + 1)
                    if h == 0:
                        for b in (2, 5):
                            for m in range(4):
                                pe.wait_ge(*freed(("in", b, m)))
                    open_(("o", h), 6)
                    for kb in range(QB):
                        last = nc.tensor.matmul(PS[r:r + HD, 6, kb * P:SEQ], V[:, kb, h * HD:h * HD + HD],
                                                Z[:, h % 3, ZO[kb]:ZO[kb] + SEQ - kb * P],
                                                start=(kb == 0), stop=(kb == QB - 1))
                    fill(last, ("o", h))
            pe.wait_ge(S("rope_done"), 8)
            steps = [(h, qb) for h in range(DIFF_HEADS) for qb in range(QB)]
            for n in range(len(steps) + 2):
                if n < len(steps):
                    h, qb = steps[n]
                    b0 = 2 * (n % 2)
                    open_(("s", n), b0, b0 + 1)
                    for c in range(2):
                        last = nc.tensor.matmul(PS[:, b0 + c, 0:(qb + 1) * P],
                                                QK[HD * c:HD * c + HD, 8 + h, qb * P:qb * P + P],
                                                QK[HD * c:HD * c + HD, 12 + h, 0:(qb + 1) * P], start=True, stop=True)
                    fill(last, ("s", n))
                if 1 <= n <= len(steps):
                    m = n - 1
                    pe.wait_ge(S("diff_map"), m + 1)
                    open_(("at", m), 4 + m % 2)
                    for kb in range(steps[m][1] + 1):
                        last = nc.tensor.transpose(PS[:, 4 + m % 2, kb * P:kb * P + P],
                                                   DA[:, m % 2, kb * P:kb * P + P], ident)
                    fill(last, ("at", m))
                if n >= 2:
                    m = n - 2
                    h, qb = steps[m]
                    pe.wait_ge(*freed(("at", m)))
                    if qb == 0:
                        open_(("do", h), 6 + h % 2)
                    for kb in range(qb + 1):
                        last = nc.tensor.matmul(PS[:, 6 + h % 2, qb * P:qb * P + P],
                                                V[:, kb, 512 + h * P:512 + h * P + P],
                                                DAT[:, m % 2, kb * P:kb * P + P], start=(kb == 0), stop=(kb == qb))
                    if qb == QB - 1:
                        fill(last, ("do", h))
                    else:
                        last.then_inc(S("diff_o"), 1)
            def subln_sum(h):
                pe.wait_ge(S("subln_sq"), h + 1)
                open_(("sl", h), 6 + h % 2)
                fill(nc.tensor.matmul(PS[:, 6 + h % 2, :], ones, SQ[:, h % 2, 0:SEQ], start=True, stop=True), ("sl", h))

            pe.wait_ge(*freed(("o", SB_HEADS - 1)))
            def wo(m, ks):
                name = ("wo", m // 4)
                w = slot(name)
                if ks.start == 0:
                    open_(("wo", m), m % 4)
                for k in ks:
                    last = nc.tensor.matmul(PS[:, m % 4, :], w[:, k, (m % 4) * P:(m % 4) * P + P], MIX[:, k, :],
                                            start=(k == 0), stop=(k == DT - 1))
                if ks.stop == DT:
                    fill(last, ("wo", m))
                    last_read[name] = ("wo", m)

            for m in range(DT):
                if m in (0, 4):
                    arrived(("wo", m // 4))
                if m < 4:
                    subln_sum(m)
                wo(m, range(0, 4 if m < 4 else DT))
                if m == 3:
                    pe.wait_ge(S("mix_ready"), DIFF_HEADS)
                    for j in range(4):
                        wo(j, range(4, DT))
            norm_sum("n2", (6,))
            pe.wait_ge(S("u_ready"), u_base["n2"] + DT)
            for m in range(FFT):
                name = ("gu", m // 2)
                arrived(name)
                cols = slice((m % 2) * P, (m % 2) * P + P)
                for part, kind in enumerate(("ga", "up")):
                    w = slot(name, part)
                    dense((kind, m), (2 * (m % 3) + part,), DT, SEQ, lambda k: w[:, k, cols],
                          lambda k: U[:, k, 0:SEQ], reads=name)
            for b in range(4):
                banks = [2 * (b % 3), 2 * (b % 3) + 1]
                for kh in range(2):
                    name = ("down", b, kh)
                    arrived(name)
                    w = slot(name)
                    for mm in range(2):
                        tag = ("dn", 2 * b + mm)
                        if kh == 0:
                            open_(tag, banks[mm])
                        if kh == 1 and b == 0 and mm == 0:
                            pe.wait_ge(*freed(("up", FFT - 1)))
                        if kh == 0 and b == 0 and mm == 0:
                            pe.wait_ge(*freed(("up", FFT // 2 - 1)))
                        for k in range(11):
                            last = nc.tensor.matmul(PS[:, banks[mm], :], w[:, k, mm * P:mm * P + P],
                                                    G[:, 11 * kh + k, :], start=(kh == 0 and k == 0),
                                                    stop=(kh == 1 and k == 10))
                        if kh == 1:
                            fill(last, tag)
                            last_read[name] = tag
                        elif mm == 1:
                            last.then_inc(S("down_half"), 1)
                            last_read[name] = ("sem", "down_half", b + 1)
            norm_sum("n3", (6, 7))
            pe.wait_ge(S("u_ready"), u_base["n3"] + DT)
            arrived(("dt",))
            w = slot(("dt",))
            dense("dt", (6, 7), DT, T2, lambda k: w[:, k, :], lambda k: U[:, k, :], M=64, reads=("dt",))
            pair = [0]

            def proj(tag, w, cols, name):
                b = 2 * (pair[0] % 2)
                pair[0] += 1
                dense(tag, (b, b + 1), DT, T2, lambda k: w[:, k, cols], lambda k: U[:, k, :], reads=name)

            def xbc(g, i, j):
                name = ("xbc", g, i)
                arrived(name)
                if j < 2:
                    proj(("xb", g, 3 * i + j), slot(name, 0), slice(j * P, j * P + P), name)
                else:
                    proj(("xb", g, 3 * i + 2), slot(name, 1), slice(0, P), name)

            xbc(0, 0, 0)
            xbc(0, 0, 1)
            pe.wait_ge(S("dt_done"), 2)
            for part, src in enumerate((0, 5)):
                open_(("dtT", part), 4 + part)
                for c, (t0, n) in enumerate(CHUNKS):
                    last = nc.tensor.transpose(PS[0:n, 4 + part, c * 64:c * 64 + 64], DTF[0:64, src, t0:t0 + n],
                                               ident[0:64, 0:64])
                fill(last, ("dtT", part))
            pe.wait_ge(*freed(("dtT", 0)))
            pe.wait_ge(*freed(("dtT", 1)))
            open_("F", 6)
            for c, (t0, n) in enumerate(CHUNKS):
                for d, tri in enumerate((upper, lower)):
                    last = nc.tensor.matmul(PS[0:n, 6, c * 64 + 32 * d:c * 64 + 32 * d + 32], tri[0:n, 0:n],
                                            AAT[0:n, c, 32 * d:32 * d + 32], start=True, stop=True)
            fill(last, "F")
            open_("TOT", 7)
            for c, (t0, n) in enumerate(CHUNKS):
                last = nc.tensor.matmul(PS[:, 7, c * 64:c * 64 + 64], ones[0:n, :], AAT[0:n, c, :], start=True, stop=True)
            fill(last, "TOT")
            open_("FR", 4, 5)
            for c, (t0, n) in enumerate(CHUNKS):
                for d, tri in enumerate((upper, lower)):
                    last = nc.tensor.matmul(PS[32 * d:32 * d + 32, 4 + c // 4, (c % 4) * P:(c % 4) * P + n],
                                            AAT[0:n, c, 32 * d:32 * d + 32], tri[0:n, 0:n], start=True, stop=True)
            fill(last, "FR")

            def conf(u, part):
                arrived(("conf", u))
                proj((("ca", "cg")[part], u), slot(("conf", u), part), slice(0, P), ("conf", u))

            def turn(g, t):
                src = CO[:, (6 * g + t) % 2, :] if t != 2 else BF[:, :]
                pe.wait_ge(S("conv_ready"), 6 * g + t + 1)
                open_(("tr", g, t), 4, 5)
                for c, (t0, n) in enumerate(CHUNKS):
                    last = nc.tensor.transpose(PS[0:n, 4 + c // 4, (c % 4) * P:(c % 4) * P + P], src[:, t0:t0 + n], ident)
                fill(last, ("tr", g, t))

            for g in range(GROUPS):
                tiles = [(i, j) for i in range(2) for j in range(3)]
                for t, (i, j) in enumerate(tiles):
                    if g > 0 or t >= 2:
                        xbc(g, i, j)
                    if t >= 2:
                        turn(g, t - 2)
                turn(g, 4)
                pe.wait_ge(S("conv_ready"), 6 * g + 6)
                pe.wait_ge(*freed(("tr", g, 2)))
                pe.wait_ge(*freed(("tr", g, 4)))
                for s, c in enumerate(range(NC - 1, 0, -1)):
                    t0, n = CHUNKS[c]
                    pe.wait_ge(S("xwb_ready"), 4 * g + s + 1)
                    open_(("sb", g, c), 6)
                    fill(nc.tensor.matmul(PS[:, 6, :], BT[0:n, c, :], XW[0:n, s % 2, :], start=True, stop=True),
                         ("sb", g, c))
                    name = ("z", g, s // 2)
                    arrived(name)
                    proj(("zt", 4 * g + s), slot(name), slice((s % 2) * P, (s % 2) * P + P), name)
                for c, (t0, n) in enumerate(CHUNKS):
                    if c == 0:
                        open_(("cb", g, 0), 4)
                        fill(nc.tensor.matmul(PS[0:n, 4, 0:n], BF[:, 0:n], CF[:, 0:n], start=True, stop=True), ("cb", g, 0))
                    if c < 4:
                        conf(2 * g + c // 2, c % 2)
                        pe.wait_ge(*freed(("sb", g, c + 1)))
                        open_(("ob", g, c), 7)
                        fill(nc.tensor.matmul(PS[0:n, 7, :], CF[:, t0:t0 + n], SNAP[:, c, :], start=True, stop=True),
                             ("ob", g, c))
                    if c > 0:
                        pe.wait_ge(*freed(("sf", g, c - 1)))
                        open_(("of", g, c), 6)
                        fill(nc.tensor.matmul(PS[0:n, 6, :], CF[:, t0:t0 + n], ST[:, (c - 1) % 2, :], start=True, stop=True),
                             ("of", g, c))
                    pe.wait_ge(S("m_ready"), NC * g + c + 1)
                    open_(("yd", g, c), 5)
                    for h in range(GH):
                        last = nc.tensor.matmul(PS[0:n, 5, h * HD:h * HD + HD], M1[0:n, h, 0:n],
                                                XS[0:n, c, h * HD:h * HD + HD], start=True, stop=True)
                    fill(last, ("yd", g, c))
                    if c < 4:
                        pe.wait_ge(S("xwf_ready"), 4 * g + c + 1)
                        open_(("sf", g, c), 6)
                        fill(nc.tensor.matmul(PS[:, 6, :], BT[0:n, c, :], XW[0:n, c % 2, :], start=True, stop=True),
                             ("sf", g, c))
                        t1, n1 = CHUNKS[c + 1]
                        open_(("cb", g, c + 1), 4)
                        fill(nc.tensor.matmul(PS[0:n1, 4, 0:n1], BF[:, t1:t1 + n1], CF[:, t1:t1 + n1], start=True,
                                              stop=True), ("cb", g, c + 1))
                    pe.wait_ge(*freed(("yd", g, c)))
                    open_(("yt", g, c), 5)
                    for j in range(4):
                        last = nc.tensor.transpose(PS[:, 5, j * P:j * P + n], YC[0:n, j * P:j * P + P], ident[0:n, 0:n])
                    fill(last, ("yt", g, c))
            triple = [0]

            def out_dense(kind, m, src, K, per):
                name = (kind, m // per)
                arrived(name)
                w = slot(name)
                n = triple[0] % 3
                triple[0] += 1
                dense((kind, m), (2 * n, 2 * n + 1), K, T2, lambda k: w[:, k, (m % per) * P:(m % per) * P + P],
                      lambda k: src[:, k, :], reads=name)

            norm_sum("ny", (6, 7))
            for m in range(4):
                out_dense("g1", m, U, DT, 4)
            pe.wait_ge(S("cacc_done"), DT)
            open_("lnm", 6, 7)
            for k in range(DT):
                for i, (lo, hi) in enumerate(halves(T2)):
                    last = nc.tensor.matmul(PS[:, 6 + i, 0:HT], ones, CACC[:, k, lo:hi], start=(k == 0), stop=(k == DT - 1))
            fill(last, "lnm")
            for m in (4, 5):
                out_dense("g1", m, U, DT, 4)
            norm_sum("lnv", (6, 7))
            for m in (6, 7):
                out_dense("g1", m, U, DT, 4)
            pe.wait_ge(S("conf_ready"), DT)
            for m in range(DT):
                out_dense("co", m, CACC, DT, 4)
            pe.wait_ge(S("y_ready"), 16)
            for m in range(DT):
                out_dense("g2", m, U, DT, 2)
                out_dense("so", m, YT, 16, 2)
            pe.wait_ge(S("merged"), DT)
            for m in range(DT):
                out_dense("out", m, MG, DT, 4)
            norm_sum("n6", (6, 7))
            pe.wait_ge(S("u_ready"), u_base["n6"] + DT)
            open_("lg", 0)
            for c, (t0, n) in enumerate(CHUNKS):
                for k in range(DT):
                    r0 = PARAMS["router"] + k * EXPERTS
                    last = nc.tensor.matmul(PS[0:n, 0, c * EXPERTS:(c + 1) * EXPERTS], U[:, k, t0:t0 + n],
                                            par[:, r0:r0 + EXPERTS], start=(k == 0), stop=(k == DT - 1))
            fill(last, "lg")
            for c, (t0, n) in enumerate(CHUNKS):
                for hf in range(2):
                    b = 2 + (2 * c + hf) % 2
                    open_(("xn", c, hf), b)
                    for k in range(4):
                        last = nc.tensor.transpose(PS[0:n, b, k * P:k * P + P], U[:, 4 * hf + k, t0:t0 + n], ident)
                    fill(last, ("xn", c, hf))
            pe.wait_ge(S("aff_ready"), 2)
            open_("af", 4, 5)
            for c, (t0, n) in enumerate(CHUNKS):
                last = nc.tensor.transpose(PS[0:EXPERTS, 4 + c // 4, (c % 4) * P:(c % 4) * P + n], AFF[0:n, c, :],
                                           ident[0:n, 0:n])
            fill(last, "af")
            pe.wait_ge(S("slots_ready"), 1)
            open_("sl16", 0)
            for c, (t0, n) in enumerate(CHUNKS):
                last = nc.tensor.transpose(PS[0:n, 0, c * EXPERTS:(c + 1) * EXPERTS], TK[0:EXPERTS, 0, t0:t0 + n],
                                           ident[0:EXPERTS, 0:EXPERTS])
            fill(last, "sl16")
            for b in range(8):
                if last_tag[b] is not None:
                    pe.wait_ge(*freed(last_tag[b]))

            def gather(e, hf):
                if hf == 0:
                    pe.wait_ge(S("sel_ready"), e * NC + NC)
                for c, (t0, n) in enumerate(CHUNKS):
                    for part in range(2):
                        last = nc.tensor.matmul(PS[0:CAP, 6 + hf, :], SE[0:n, c, :], XNT[0:n, part, c, 512 * hf:512 * hf + 512],
                                                start=(c == 0 and part == 0), stop=(c == NC - 1 and part == 1))
                last.then_inc(S("x_gathered"), 1)

            def turn_x(e, hf):
                pe.wait_ge(S("xgs_ready"), e * 2 + hf + 1)
                for k in range(4):
                    last = nc.tensor.transpose(PS[:, 6 + hf, k * CAP:(k + 1) * CAP],
                                               XGS[0:CAP, (4 * hf + k) * P:(4 * hf + k + 1) * P], ident[0:CAP, 0:CAP])
                last.then_inc(S("x_turned"), 1)

            def turn_h(e, b):
                pe.wait_ge(S("hgs_ready"), e * 4 + b + 1)
                for k in range(4):
                    last = nc.tensor.transpose(PS[:, 6 + b % 2, k * CAP:(k + 1) * CAP], HGS[0:CAP, b % 2, k * P:k * P + P],
                                               ident[0:CAP, 0:CAP])
                last.then_inc(S("h_turned"), 1)

            def combine(e, m):
                pe.wait_ge(S("yel_ready"), e * 2 + m // 4 + 1)
                if m == 0:
                    pe.wait_ge(S("yel_ready"), e * 2 + 2)
                else:
                    pe.wait_ge(S("h_added"), e * DT + m)
                for i, (lo, hi) in enumerate(halves(T2)):
                    for part in range(2):
                        last = nc.tensor.matmul(PS[:, 4 + i, 0:HT], YE[0:CAP, part, m * P:m * P + P], SAT[0:CAP, lo:hi],
                                                start=(part == 0), stop=(part == 1))
                last.then_inc(S("combined"), 1)

            def turn_slots(e):
                pe.wait_ge(S("hgl_ready"), e * 4 + 3)
                for c, (t0, n) in enumerate(CHUNKS):
                    nc.tensor.transpose(PS[0:CAP, 6 + c // 4, (c % 4) * P:(c % 4) * P + n], SE[0:n, c, :].bitcast(F32),
                                        ident[0:n, 0:n])
                pe.wait_ge(S("aff_copied"), e * 2 + 2)
                for c, (t0, n) in enumerate(CHUNKS):
                    last = nc.tensor.matmul(PS[0:CAP, 7, 256:257], SE[0:n, c, :].bitcast(F32), small[0:n, 144 + c:145 + c],
                                            start=(c == 0), stop=(c == NC - 1))
                last.then_inc(S("sat_turned"), 1)

            def expert(e, first=False, last=False):
                for q in range(PIECES):
                    i, kk = q // 4, q % 4
                    if i < 8:
                        b, part = i // 2, i % 2
                        bank, stat, k0 = 2 * (b % 2) + part, XG, 2 * kk
                        if kk == 0 and not (first and b < 2):
                            pe.wait_ge(S(("gate_act", "hgs_ready")[part]), e * 4 + b - 1)
                        if q in (0, 2):
                            pe.wait_ge(S("xgl_ready"), e * 2 + q // 2 + 1)
                        start, stop = kk == 0, kk == 3
                    else:
                        kh, bank = (i - 8) // 2, 4 + i % 2
                        stat, k0 = HG, 8 * kh + 2 * kk
                        if i == 8 and kk == 0 and not first:
                            pe.wait_ge(S("h_added"), e * DT)
                        if i in (8, 10) and kk in (0, 2):
                            pe.wait_ge(S("hgl_ready"), e * 4 + 2 * kh + kk // 2 + 1)
                        start, stop = kh == 0 and kk == 0, kh == 1 and kk == 3
                    pe.wait_ge(S("wh_ready"), e * PIECES + q + 1)
                    for j in range(2):
                        k = k0 + j
                        w = WS[:, :, q % PBUF, 512 * j:512 * j + 512]
                        nc.tensor.matmul(PS[0:CAP, bank, :], stat[:, 0, k, :], w[:, 0, :], start=(start and j == 0), stop=False)
                        nc.tensor.matmul(PS[0:CAP, bank, :], stat[:, 1, k, :], w[:, 0, :], start=False, stop=False)
                    pe.wait_ge(S("wl_ready"), e * PIECES + q + 1)
                    for j in range(2):
                        mm = nc.tensor.matmul(PS[0:CAP, bank, :], stat[:, 0, k0 + j, :], WS[:, 1, q % PBUF, 512 * j:512 * j + 512],
                                              start=False, stop=(stop and j == 1))
                    mm.then_inc(S("w_used"), 1)
                    if not first and q in COMBINE_AT:
                        combine(e - 1, COMBINE_AT.index(q))
                    if q in TURN_H_AT:
                        b = TURN_H_AT.index(q)
                        if b == 3:
                            pe.wait_ge(S("sat_ready"), e * 3 + 3)
                        turn_h(e, b)
                    if q == SLOTS_AT:
                        turn_slots(e)
                    if not last and q in GATHER_AT:
                        hf = GATHER_AT.index(q)
                        if hf == 1:
                            pe.wait_ge(S("hgl_ready"), e * 4 + 4)
                        gather(e + 1, hf)
                    if not last and q in TURN_X_AT:
                        turn_x(e + 1, TURN_X_AT.index(q))

            for hf in range(2):
                gather(0, hf)
            for hf in range(2):
                turn_x(0, hf)
            expert(0, first=True)
            with pe.Fori(1, EXPERTS - 1) as e:
                expert(e)
            expert(EXPERTS - 1, last=True)
            for m in range(DT):
                combine(EXPERTS - 1, m)
            pe.wait_ge(S("h_added"), EXPERTS * DT)
            for b in range(8):
                last_tag[b] = None
            norm_sum("n7", (6, 7))

        @blk.scalar
        def _(act):
            A = nc.scalar.activation
            link = chain(act, "act_chain")

            def squares(nm, src):
                _, K, T, *_ = NORM[nm]
                for k in range(K):
                    if k >= 2:
                        act.wait_ge(S("sq_used"), used_base[nm] + k - 1)
                    A(SQ[:, k % 2, 0:T], src(k), ACT.Square).then_inc(S("sq_ready"), 1)

            def root(nm, banks, R=RS):
                _, K, T, scale, eps, _ = NORM[nm]
                got(act, nm)
                free(A(tok(R[:, 0:T], T), ps(banks, T), ACT.Sqrt, bias=pcol(eps), scale=scale), nm)

            act.dma_start(H[:, :, :], inp["h_t"].rearrange("(k p) n -> p k n", p=P)).then_inc(S("h_in"), 16)
            act.wait_ge(S("consts_in"), 48)
            act.wait_ge(S("h_in"), 16)
            squares("n1", lambda k: H[:, k, META:T2])
            root("n1", (6,))
            got(act, "lam")
            free(A(small[:, 2:4], PS[:, 7, 0:2], ACT.Exp), "lam")
            for b in (0, 1, 3, 4):
                for m in range(4):
                    got(act, ("in", b, m))
                    at = {0: 0, 1: 4, 3: 8, 4: 12}[b] + m
                    free(A(QK[:, at, :], PS[:, (4 * b + m) % 4, :], ACT.Copy, scale=HD ** -0.5 if b == 0 else 1.0),
                         ("in", b, m))
            def rope_root(j):
                got(act, ("rn", j))
                free(A(MIX[:, j, :], PS[:, bank(("rn", j)), :], ACT.Sqrt, bias=pcol("eps"), scale=1.0 / HD), ("rn", j))

            for j in range(8):
                act.wait_ge(*freed(("in", 3 + j // 4, j % 4)))
                if j >= 2:
                    got(act, ("rn", j - 2))
                A(SQ[:, j % 2, 0:SEQ], QK[:, 8 + j, :], ACT.Square).then_inc(S("rope_sq"), 1)
                if j >= 1:
                    rope_root(j - 1)
            rope_root(7)
            nc.scalar.preload_act_table_set("natural_log_exp_and_others")
            for i in range(SB_HEADS + 1):
                if i < SB_HEADS:
                    got(act, ("z", i))
                    if i >= 3:
                        got(act, ("o", i - 3))
                    free(A(Z[:, i % 3, :], PS[:, 0:3, :].rearrange("p a n -> p (a n)")[:, 0:1280], ACT.Copy), ("z", i))
                    act.wait_ge(*freed(("z", i)))
                    if i >= 2:
                        got(act, ("c", i - 2))
                    link(A(SP[:, i % 2, :], Z[:, i % 3, :], ACT.Abs))
                    link(A(SP[:, i % 2, :], SP[:, i % 2, :], ACT.Exp, scale=-1.0))
                    A(SP[:, i % 2, :], SP[:, i % 2, :], ACT.Ln, bias=pcol("one")).then_inc(S("ln_ready"), 1)
                if i >= 1:
                    act.wait_ge(S("arg_masked"), i)
                    A(Z[:, (i - 1) % 3, :], Z[:, (i - 1) % 3, :], ACT.Exp).then_inc(S("w_ready"), 1)
            for n in range(DIFF_HEADS * QB + 1):
                if n < DIFF_HEADS * QB:
                    qb, b0 = n % QB, 2 * (n % 2)
                    act.wait_ge(S("diff_max"), n + 1)
                    if n == 0:
                        got(act, ("o", SB_HEADS - 1))
                    if n >= 2:
                        act.wait_ge(S("diff_map"), n - 1)
                    for c in range(2):
                        ins = A(PR[:, n % 2, c, 0:(qb + 1) * P], PS[:, b0 + c, 0:(qb + 1) * P], ACT.Exp,
                                bias=small[:, 16 + 2 * (n % 2) + c:17 + 2 * (n % 2) + c], scale=HD ** -0.5,
                                accum_out=small[:, 24 + 2 * (n % 2) + c:25 + 2 * (n % 2) + c])
                        if c == 0:
                            ins.then_inc(S("diff_exp0"), 1)
                    free(ins, ("s", n))
                if n >= 1:
                    m = n - 1
                    got(act, ("at", m))
                    if m >= 2 and (m - 2) % QB == QB - 1:
                        got(act, ("do", (m - 2) // QB))
                    elif m >= 2:
                        act.wait_ge(S("diff_o"), (QB - 1) * ((m - 2) // QB) + (m - 2) % QB + 1)
                    free(A(DAT[:, m % 2, 0:(m % QB + 1) * P], PS[:, 4 + m % 2, 0:(m % QB + 1) * P], ACT.Copy), ("at", m))
            def subln_root(h):
                got(act, ("sl", h))
                free(A(QK[:, h, :], PS[:, bank(("sl", h)), :], ACT.Sqrt, bias=pcol("subln_eps"), scale=1.0 / P), ("sl", h))

            for h in range(DIFF_HEADS):
                act.wait_ge(*freed(("do", h)))
                if h >= 2:
                    got(act, ("sl", h - 2))
                A(SQ[:, h % 2, 0:SEQ], MIX[:, 4 + h, :], ACT.Square).then_inc(S("subln_sq"), 1)
                if h >= 1:
                    subln_root(h - 1)
            subln_root(DIFF_HEADS - 1)
            for m in range(DT):
                act.wait_ge(*freed(("wo", m)))
                if m >= 2:
                    act.wait_ge(S("sq_used"), used_base["n2"] + m - 1)
                A(SQ[:, m % 2, 0:SEQ], H[:, m, META:T2], ACT.Square).then_inc(S("sq_ready"), 1)
            root("n2", (6,))
            for m in range(FFT):
                got(act, ("ga", m))
                if m >= 2:
                    act.wait_ge(*freed(("up", m - 2)))
                free(A(SG[:, m % 2, :], PS[:, 2 * (m % 3), :], ACT.Silu), ("ga", m))
            for m in range(DT):
                act.wait_ge(*freed(("dn", m)))
                if m >= 2:
                    act.wait_ge(S("sq_used"), used_base["n3"] + m - 1)
                A(SQ[:, m % 2, :], H[:, m, :], ACT.Square).then_inc(S("sq_ready"), 1)
            root("n3", (6, 7))
            got(act, "dt")
            free(A(tok(DTF[0:64, 1, :], T2), PS[0:64, 6:8, 0:HT], ACT.Identity, bias=par[0:64, PARAMS["dt_bias"]:PARAMS["dt_bias"] + 1]), "dt")
            act.wait_ge(*freed("dt"))
            nc.scalar.preload_act_table_set("natural_log_exp_and_others")
            link(A(DTF[0:64, 2, :], DTF[0:64, 1, :], ACT.Abs))
            link(A(DTF[0:64, 2, :], DTF[0:64, 2, :], ACT.Exp, scale=-1.0))
            A(small[0:64, 32:33], par[0:64, PARAMS["a_log"]:PARAMS["a_log"] + 1], ACT.Exp).then_inc(S("dt_parts"), 1)
            A(DTF[0:64, 2, :], DTF[0:64, 2, :], ACT.Ln, bias=par[0:64, PARAMS["one"]:PARAMS["one"] + 1]).then_inc(S("dt_parts"), 1)
            def conv_tile(g, t):
                got(act, ("xb", g, t))
                i = 6 * g + t
                if i >= 2:
                    act.wait_ge(S("conv_done"), i - 1)
                b = bank(("xb", g, t))
                free(A(tok(XP[:, i % 2, 3:3 + T2], T2), PS[:, b:b + 2, 0:HT], ACT.Copy), ("xb", g, t))

            conv_tile(0, 0)
            conv_tile(0, 1)
            got(act, "FR")
            link(A(DTF[0:64, 3, 0:512], PS[0:64, 4, :], ACT.Copy))
            free(A(DTF[0:64, 3, 512:T2], PS[0:64, 5, 0:META], ACT.Copy), "FR")
            act.wait_ge(*freed("FR"))
            act.dma_start(fr_dram, DTF[0:64, 3, :]).then_inc(S("fr_out"), 16)
            act.wait_ge(S("w2_arg"), 2)
            for i, (n, cs) in enumerate(((P, slice(0, 4)), (META, slice(4, 5)))):
                A(EF[0:n, cs, :], FT[0:n, cs, :], ACT.Exp).then_inc(S("ssd_exp"), 1)
                A(W2[0:n, cs, :], W2[0:n, cs, :], ACT.Exp).then_inc(S("ssd_exp"), 1)
            A(ET[:, :, :], ET[:, :, :], ACT.Exp).then_inc(S("ssd_exp"), 1)
            act.wait_ge(S("fr_out"), 16)

            def fr_load(g, c):
                i = NC * g + c
                t0, n = CHUNKS[c]
                if i >= 2:
                    act.wait_ge(S("m_ready"), i - 1)
                for d in range(2):
                    src = fr_dram[32 * d + GH * g:32 * d + GH * (g + 1), t0:t0 + n]
                    act.dma_start(FR[i % 2][d][:, :, 0:n], src.partition_broadcast(P)).then_inc(S(f"fr_in{i % 2}"), 16)

            def conv_silu(g, t):
                i = 6 * g + t
                act.wait_ge(S("conv_done"), i + 1)
                j = 16 + (0 if t == 2 else 4) + g if t in (2, 5) else 4 * g + (t if t < 2 else t - 1)
                co = CO[:, (6 * g + t) % 2, :]
                if t in (2, 5):
                    if g > 0:
                        got(act, ("of", g - 1, NC - 1))
                        act.wait_ge(S("m_ready"), NC * g)
                    ins = A(BF if t == 2 else CF, CO[:, (6 * g + t) % 2, :], ACT.Silu, bias=pcol("ssm_b", j))
                else:
                    ins = A(co, co, ACT.Silu, bias=pcol("ssm_b", j))
                ins.then_inc(S("conv_ready"), 1)

            def take_turned(g, t):
                tag = ("tr", g, t)
                got(act, tag)
                if g > 0:
                    got(act, ("yt", g - 1, NC - 1))
                dst = BT if t == 2 else XS[:, :, XS_AT[t] * P:XS_AT[t] * P + P]
                link(A(dst[:, 0:4, :], PS[:, 4, :].rearrange("p (c n) -> p c n", c=4), ACT.Copy))
                free(A(dst[0:META, 4, :], PS[0:META, 5, 0:P], ACT.Copy), tag)

            XS_AT = {0: 0, 1: 1, 3: 2, 4: 3}
            for g in range(GROUPS):
                for t in range(6):
                    if g > 0 or t >= 2:
                        conv_tile(g, t)
                    if t >= 1:
                        conv_silu(g, t - 1)
                    if t >= 3:
                        take_turned(g, t - 3)
                conv_silu(g, 5)
                take_turned(g, 3)
                take_turned(g, 4)
                fr_load(g, 0)
                fr_load(g, 1)
                for s in range(4):
                    tag = ("zt", 4 * g + s)
                    got(act, tag)
                    b = bank(tag)
                    free(A(tok(YT[:, 4 * g + s, :], T2), PS[:, b:b + 2, 0:HT], ACT.Silu), tag)
                for c, (t0, n) in enumerate(CHUNKS):
                    i = NC * g + c
                    act.wait_ge(S("min_ready"), i + 1)
                    A(FR[i % 2][0][0:n, :, 0:n], FR[i % 2][0][0:n, :, 0:n], ACT.Exp).then_inc(S("e_ready"), 1)
                    if c % 2 == 1:
                        u = 2 * g + c // 2
                        got(act, ("cg", u))
                        if u >= 1:
                            act.wait_ge(*freed(("ca", u - 1)))
                        b = bank(("cg", u))
                        free(A(tok(SGB[:, :], T2), PS[:, b:b + 2, 0:HT], ACT.Sigmoid), ("cg", u))
                    if c + 2 < NC:
                        fr_load(g, c + 2)
            act.wait_ge(*freed(("yt", GROUPS - 1, NC - 1)))
            squares("ny", lambda k: YT[:, k, :])
            root("ny", (6, 7), GT[:, 1, :])

            def first_gate(m):
                got(act, ("g1", m))
                b = bank(("g1", m))
                free(A(tok(MG[:, m, :], T2), PS[:, b:b + 2, 0:HT], ACT.Sigmoid), ("g1", m))

            for m in range(4):
                first_gate(m)
            for k in range(DT):
                act.wait_ge(S("ln_centred"), k + 1)
                if k >= 2:
                    act.wait_ge(S("sq_used"), used_base["lnv"] + k - 1)
                A(SQ[:, k % 2, :], CACC[:, k, :], ACT.Square).then_inc(S("sq_ready"), 1)
            root("lnv", (6, 7))
            for m in (4, 5):
                first_gate(m)
            for k in range(DT):
                act.wait_ge(S("ln_scaled"), k + 1)
                A(CACC[:, k, :], CACC[:, k, :], ACT.Silu, bias=pcol("ln_b", k)).then_inc(S("conf_ready"), 1)
            for m in (6, 7):
                first_gate(m)
            for m in range(DT):
                got(act, ("g2", m))
                if m == 0:
                    act.wait_ge(S("y_ready"), 16)
                if m >= 2:
                    act.wait_ge(S("merged"), m - 1)
                else:
                    act.wait_ge(*freed(("co", DT - 1)))
                b = bank(("g2", m))
                free(A(tok(GT[:, m % 2, :], T2), PS[:, b:b + 2, 0:HT], ACT.Sigmoid), ("g2", m))
            for m in range(DT):
                act.wait_ge(*freed(("out", m)))
                if m >= 2:
                    act.wait_ge(S("sq_used"), used_base["n6"] + m - 1)
                A(SQ[:, m % 2, :], H[:, m, :], ACT.Square).then_inc(S("sq_ready"), 1)
            root("n6", (6, 7))
            for c, (t0, n) in enumerate(CHUNKS):
                act.wait_ge(S("lg_max"), NC)
                ins = A(AFF[0:n, c, :], PS[0:n, 0, c * EXPERTS:(c + 1) * EXPERTS], ACT.Exp,
                        bias=small[0:n, 48 + c:49 + c], accum_out=small[0:n, 56 + c:57 + c])
                if c < NC - 1:
                    ins.then_inc(S("aff_exp"), 1)
            free(ins, "lg")
            for c, (t0, n) in enumerate(CHUNKS):
                for hf in range(2):
                    got(act, ("xn", c, hf))
                    A(XNT[0:n, 0, c, 512 * hf:512 * hf + 512], PS[0:n, 2 + hf, :], ACT.Copy).then_inc(S("xnt_high"), 1)
            nc.scalar.preload_act_table_set("silu_and_others")

            def x_rows(e, hf):
                act.wait_ge(S("x_gathered"), e * 2 + hf + 1)
                A(XGS[0:CAP, 512 * hf:512 * hf + 512], PS[0:CAP, 6 + hf, :], ACT.Copy).then_inc(S("xgs_ready"), 1)

            def x_high(e, hf):
                act.wait_ge(S("x_turned"), e * 2 + hf + 1)
                A(XG[:, 0, 4 * hf:4 * hf + 4, :], PS[:, 6 + hf, 0:4 * CAP].rearrange("p (k n) -> p k n", k=4),
                  ACT.Copy).then_inc(S("xgh_ready"), 1)

            def y_high(e, hf):
                act.wait_ge(S("w_used"), e * PIECES + 44 + 4 * hf)
                act.wait_ge(S("sat_ready"), e * 3 + 3)
                A(YE[0:CAP, 0, 512 * hf:512 * hf + 512], PS[0:CAP, 4 + hf, :], ACT.Copy, scale=AFS[0:CAP])\
                    .then_inc(S("yeh_ready"), 1)

            def expert(e, first=False, last=False):
                for q in range(PIECES):
                    i, kk = q // 4, q % 4
                    if kk == 0:
                        landed_e(act, e, i)
                    if first and q < PBUF:
                        if q == 0:
                            act.wait_ge(S("sel_ready"), NC)
                    else:
                        act.wait_ge(S("w_used"), e * PIECES + q - PBUF + 1)
                    at = q - PBUF
                    if at == -1 and not first:
                        y_high(e - 1, 1)
                    if at >= 0 and at < 32 and at % 8 == 3:
                        b = at // 8
                        if not (first and b < 2):
                            act.wait_ge(S("hgs_ready"), e * 4 + b - 1)
                        A(SIL[0:CAP, b % 2, :], PS[0:CAP, 2 * (b % 2), :], ACT.Silu).then_inc(S("gate_act"), 1)
                    if at in TURN_H_AT:
                        b = TURN_H_AT.index(at)
                        act.wait_ge(S("h_turned"), e * 4 + b + 1)
                        A(HG[:, 0, 4 * b:4 * b + 4, :], PS[:, 6 + b % 2, 0:4 * CAP].rearrange("p (k n) -> p k n", k=4),
                          ACT.Copy).then_inc(S("hgh_ready"), 1)
                    if at in GATHER_AT and not last:
                        x_rows(e + 1, GATHER_AT.index(at))
                    if at in TURN_X_AT and not last:
                        x_high(e + 1, TURN_X_AT.index(at))
                    if at == 43:
                        y_high(e, 0)
                    A(WS[:, 0, q % PBUF, :], ring[:, (N_DENSE + i) % RING, PIECE * kk:PIECE * (kk + 1)], ACT.Copy)\
                        .then_inc(S("wh_ready"), 1)

            for hf in range(2):
                x_rows(0, hf)
            for hf in range(2):
                x_high(0, hf)
            expert(0, first=True)
            with act.Fori(1, EXPERTS - 1) as e:
                expert(e)
            expert(EXPERTS - 1, last=True)
            y_high(EXPERTS - 1, 1)
            act.wait_ge(S("h_added"), EXPERTS * DT)
            squares("n7", lambda k: H[:, k, :])
            root("n7", (6, 7))

        @blk.vector
        def _(dve):
            V_ = nc.vector
            link = chain(dve, "dve_chain")
            MUL, ADD, SUB = ALU.mult, ALU.add, ALU.subtract

            def norm_apply(nm, src, dst, sem, R=RS):
                _, K, T, _, _, gain = NORM[nm]
                dve.wait_ge(*freed(nm))
                link(V_.reciprocal(R[:, 0:T], R[:, 0:T]))
                for k in range(K):
                    V_.scalar_tensor_tensor(dst(k), src(k), pcol(gain, k), R[:, 0:T], MUL, MUL).then_inc(S(sem), 1)

            dve.wait_ge(S("consts_in"), 48)
            l0 = PARAMS["lam"]
            V_.tensor_tensor(small[0:HD, 0:2], par[0:HD, l0:l0 + 4:2], par[0:HD, l0 + 1:l0 + 4:2], MUL).then_inc(S("lam_prod"), 1)
            norm_apply("n1", lambda k: H[:, k, META:T2], lambda k: U[:, k, 0:SEQ], "u_ready")
            dve.wait_ge(*freed("lam"))
            link(V_.tensor_tensor(small[:, 4:5], small[:, 3:4], small[:, 2:3], SUB))
            link(V_.tensor_scalar(small[:, 4:5], small[:, 4:5], LAMBDA_INIT, None, SUB))
            link(V_.tensor_scalar(small[:, 5:6], pcol("subln_g"), 1.0 - LAMBDA_INIT, None, MUL))
            for i, b in enumerate((2, 5)):
                for m in range(4):
                    got(dve, ("in", b, m))
                    tag = ("in", b, m)
                    free(V_.tensor_copy(V[:, m, 512 * i:512 * i + 512], PS[:, bank(tag), :]), tag)
            def rope_norm(j):
                dve.wait_ge(*freed(("rn", j)))
                R = MIX[:, j, :]
                link(V_.reciprocal(R, R))
                gain = pcol("q_g") if j < 4 else pcol("k_g")
                V_.scalar_tensor_tensor(QK[:, 8 + j, :], QK[:, 8 + j, :], gain, R, MUL, MUL).then_inc(S("rope_normed"), 1)

            def stick_out(h):
                r0 = HD * (h % 2)
                got(dve, ("o", h))
                free(V_.tensor_copy(MIX[r0:r0 + HD, h // 2, :], PS[r0:r0 + HD, 6, :]), ("o", h))

            def diff_out(h):
                got(dve, ("do", h))
                free(V_.tensor_copy(MIX[:, 4 + h, :], PS[:, bank(("do", h)), :]), ("do", h))

            rope_norm(0)
            for i in range(SB_HEADS + 1):
                if i < SB_HEADS:
                    dve.wait_ge(S("ln_ready"), i + 1)
                    V_.scalar_tensor_tensor(SP[:, i % 2, :], Z[:, i % 3, :], 0.0, SP[:, i % 2, :], ALU.max, ADD)\
                        .then_inc(S("sp_ready"), 1)
                    got(dve, ("rot", i))
                    dve.wait_ge(S("cos_part"), i + 1)
                    RB = U[:, i % 2, 0:SEQ]
                    if i >= 2:
                        dve.wait_ge(S("rope_done"), i - 1)
                    free(V_.tensor_tensor(RB, PS[:, 7, :], SIN, MUL), ("rot", i))
                    dve.wait_ge(*freed(("rot", i)))
                    V_.tensor_tensor(QK[:, 8 + i, :], RB, U[:, 2 + i % 2, 0:SEQ], ADD).then_inc(S("rope_done"), 1)
                if i >= 1:
                    h = i - 1
                    got(dve, ("c", h))
                    free(V_.tensor_tensor(Z[:, h % 3, :], Z[:, h % 3, :],
                                          PS[:, 3:6, :].rearrange("p a n -> p (a n)")[:, 0:1280], SUB), ("c", h))
                if i + 1 < SB_HEADS:
                    rope_norm(i + 1)
                if i >= 2:
                    stick_out(i - 2)
            stick_out(SB_HEADS - 1)
            dve.wait_ge(S("rope_done"), 8)
            for n in range(DIFF_HEADS * QB + 1):
                if n < DIFF_HEADS * QB:
                    qb, b0 = n % QB, 2 * (n % 2)
                    N = (qb + 1) * P
                    got(dve, ("s", n))
                    link(V_.tensor_tensor(PS[:, b0:b0 + 2, qb * P:N], PS[:, b0:b0 + 2, qb * P:N],
                                          causal.unsqueeze(1).to_broadcast([P, 2, P]), ADD))
                    link(V_.tensor_reduce(small[:, 8:10], PS[:, b0:b0 + 2, 0:N], AX_X, ALU.max))
                    V_.tensor_scalar(small[:, 16 + 2 * (n % 2):18 + 2 * (n % 2)], small[:, 8:10], -HD ** -0.5, None, MUL)\
                        .then_inc(S("diff_max"), 1)
                    dve.wait_ge(S("diff_max"), n + 1)
                if n >= 1:
                    m = n - 1
                    N = (m % QB + 1) * P
                    s0 = 24 + 2 * (m % 2)
                    dve.wait_ge(*freed(("s", m)))
                    dve.wait_ge(S("diff_exp0"), m + 1)
                    link(V_.reciprocal(small[:, s0:s0 + 2], small[:, s0:s0 + 2]))
                    link(V_.tensor_tensor(small[:, s0 + 1:s0 + 2], small[:, s0 + 1:s0 + 2], small[:, 4:5], MUL))
                    link(V_.tensor_scalar(DA2[:, m % 2, 0:N], PR[:, m % 2, 1, 0:N], small[:, s0 + 1:s0 + 2], None, MUL))
                    if m >= 2:
                        got(dve, ("at", m - 2))
                    V_.scalar_tensor_tensor(DA[:, m % 2, 0:N], PR[:, m % 2, 0, 0:N], small[:, s0:s0 + 1],
                                            DA2[:, m % 2, 0:N], MUL, ADD).then_inc(S("diff_map"), 1)
                    dve.wait_ge(S("diff_map"), m + 1)
                if n >= QB + 2 and (n - 2) % QB == 0:
                    diff_out((n - 2) // QB - 1)
            diff_out(DIFF_HEADS - 1)
            for h in range(DIFF_HEADS):
                dve.wait_ge(*freed(("sl", h)))
                R = QK[:, h, :]
                link(V_.reciprocal(R, R))
                V_.scalar_tensor_tensor(MIX[:, 4 + h, :], MIX[:, 4 + h, :], small[:, 5:6], R, MUL, MUL).then_inc(S("mix_ready"), 1)
            for m in range(DT):
                got(dve, ("wo", m))
                free(V_.tensor_tensor(H[:, m, META:T2], H[:, m, META:T2], PS[:, m % 4, :], ADD), ("wo", m))
            norm_apply("n2", lambda k: H[:, k, META:T2], lambda k: U[:, k, 0:SEQ], "u_ready")
            for m in range(FFT):
                got(dve, ("up", m))
                dve.wait_ge(*freed(("ga", m)))
                free(V_.tensor_tensor(G[:, m, :], SG[:, m % 2, :], PS[:, 2 * (m % 3) + 1, :], MUL), ("up", m))
            for m in range(DT):
                got(dve, ("dn", m))
                b = 2 * ((m // 2) % 3) + m % 2
                free(V_.tensor_tensor(H[:, m, META:T2], H[:, m, META:T2], PS[:, b, :], ADD), ("dn", m))
            norm_apply("n3", lambda k: H[:, k, :], lambda k: U[:, k, :], "u_ready")
            for v in (XP[:, :, 0:3], XP[:, :, 3 + T2:6 + T2], CP[:, :, 0:15], CP[:, :, 15 + T2:30 + T2]):
                V_.memset(v, 0.0).then_inc(S("pads"), 1)
            dve.wait_ge(S("dt_parts"), 2)
            V_.scalar_tensor_tensor(DTF[0:64, 0, :], DTF[0:64, 1, :], 0.0, DTF[0:64, 2, :], ALU.max, ADD).then_inc(S("dt_done"), 1)
            dve.wait_ge(S("dt_done"), 1)
            V_.tensor_scalar(DTF[0:64, 5, :], DTF[0:64, 0, :], small[0:64, 32:33], -1.0, MUL, MUL).then_inc(S("dt_done"), 1)
            for part, dst in enumerate((DTT, AAT)):
                got(dve, ("dtT", part))
                link(V_.tensor_copy(dst[:, 0:4, :], PS[:, 4 + part, 0:256].rearrange("p (c n) -> p c n", c=4)))
                free(V_.tensor_copy(dst[0:META, 4, :], PS[0:META, 4 + part, 256:320]), ("dtT", part))
            dve.wait_ge(*freed(("dtT", 1)))
            got(dve, "F")
            got(dve, "TOT")
            free(V_.tensor_copy(ET[:, :, :], PS[:, 7, 0:320].rearrange("p (c n) -> p c n", c=NC)), "TOT")
            dve.wait_ge(*freed("TOT"))
            for n, cs in ((P, slice(0, 4)), (META, slice(4, 5))):
                lo, hi = cs.start * 64, cs.stop * 64
                k = cs.stop - cs.start
                ins = V_.tensor_copy(FT[0:n, cs, :], PS[0:n, 6, lo:hi].rearrange("p (c n) -> p c n", c=k))
                if n == P:
                    link(ins)
                else:
                    free(ins, "F")
                    dve.wait_ge(*freed("F"))
                ins = V_.tensor_tensor(W2[0:n, cs, :], ET[0:n, cs, :], FT[0:n, cs, :], SUB)
                ins.then_inc(S("w2_arg"), 1)
            dve.wait_ge(S("ssd_exp"), 5)
            link(V_.tensor_tensor(W2[:, 0:4, :], W2[:, 0:4, :], DTT[:, 0:4, :], MUL))
            V_.tensor_tensor(W2[0:META, 4, :], W2[0:META, 4, :], DTT[0:META, 4, :], MUL).then_inc(S("w2_ready"), 1)
            dve.wait_ge(S("w2_ready"), 1)
            dve.wait_ge(S("pads"), 4)

            def conv(out_, src, taps, w0, done, bias=None):
                if bias is None:
                    link(V_.tensor_scalar(out_, src[:, 0:T2], par[:, w0:w0 + 1], None, MUL))
                else:
                    link(V_.tensor_scalar(out_, src[:, 0:T2], par[:, w0:w0 + 1], bias, MUL, ADD))
                for j in range(1, taps):
                    ins = V_.scalar_tensor_tensor(out_, src[:, j:j + T2], par[:, w0 + j:w0 + j + 1], out_, MUL, ADD)
                    if j < taps - 1:
                        link(ins)
                    else:
                        ins.then_inc(S(done), 1)

            def bc(ap, n, w):
                return ap.unsqueeze(2).to_broadcast([n, GH, w])

            tap = [0]

            def conf_taps(upto):
                while tap[0] < upto:
                    u, j = divmod(tap[0], CONF_TAPS)
                    w0 = PARAMS["conf_w"] + u * CONF_TAPS
                    acc = CACC[:, u, :]
                    if u == 0 and j == 0:
                        dve.wait_ge(S("h_saved"), 16)
                    if j == 0:
                        dve.wait_ge(*freed(("ca", u)))
                        link(V_.tensor_scalar(acc, CP[:, u % 2, 0:T2], par[:, w0:w0 + 1], pcol("conf_b", u), MUL, ADD))
                    else:
                        ins = V_.scalar_tensor_tensor(acc, CP[:, u % 2, j:j + T2], par[:, w0 + j:w0 + j + 1], acc, MUL, ADD)
                        if j < CONF_TAPS - 1:
                            link(ins)
                        else:
                            ins.then_inc(S("cacc_done"), 1)
                    tap[0] += 1

            def some_taps(n, tiles):
                conf_taps(min(tap[0] + n, tiles * CONF_TAPS))

            for g in range(GROUPS):
                h8 = slice(GH * g, GH * g + GH)
                h8b = slice(32 + GH * g, 32 + GH * g + GH)
                for t in range(6):
                    i = 6 * g + t
                    dve.wait_ge(*freed(("xb", g, t)))
                    j = 16 + (0 if t == 2 else 4) + g if t in (2, 5) else 4 * g + (t if t < 2 else t - 1)
                    if i >= 2:
                        g2, t2 = divmod(i - 2, 6)
                        if t2 in (2, 5):
                            dve.wait_ge(S("conv_ready"), i - 1)
                        else:
                            got(dve, ("tr", g2, t2))
                    conv(CO[:, (6 * g + t) % 2, :], XP[:, i % 2, :], SSM_TAPS, PARAMS["ssm_w"] + j * SSM_TAPS, "conv_done")
                    some_taps(6, 2 * g)
                for s, c in enumerate(range(NC - 1, 0, -1)):
                    t0, n = CHUNKS[c]
                    got(dve, ("sb", g, c))
                    dst = SNAP[:, c - 1, :]
                    if g > 0 and s == 0:
                        got(dve, ("ob", g - 1, 3))
                    if c == NC - 1:
                        ins = V_.tensor_copy(dst, PS[:, 6, :])
                    else:
                        link(V_.tensor_tensor(dst.rearrange("p (h w) -> p h w", h=GH),
                                              SNAP[:, c, :].rearrange("p (h w) -> p h w", h=GH),
                                              bc(ET[:, c, h8b], P, HD), MUL))
                        ins = V_.tensor_tensor(dst, dst, PS[:, 6, :], ADD)
                    free(ins, ("sb", g, c))
                    dve.wait_ge(*freed(("sb", g, c)))
                    some_taps(8, 2 * g)
                for c, (t0, n) in enumerate(CHUNKS):
                    i = NC * g + c
                    F = FR[i % 2]
                    got(dve, ("cb", g, c))
                    link(V_.tensor_tensor(CBM[0:n, 0, 0:n], PS[0:n, 4, 0:n], upper[0:n, 0:n], MUL))
                    free(V_.tensor_tensor(CBM[0:n, 1, 0:n], PS[0:n, 4, 0:n], lower[0:n, 0:n], MUL), ("cb", g, c))
                    dve.wait_ge(S(f"fr_in{i % 2}"), 32 * (i // 2 + 1))
                    link(V_.tensor_tensor(F[0][0:n, :, 0:n], F[0][0:n, :, 0:n], bc(FT[0:n, c, h8], n, n), SUB))
                    dve.wait_ge(S("t2_ready"), i + 1)
                    V_.tensor_tensor(F[0][0:n, :, 0:n], F[0][0:n, :, 0:n], F[1][0:n, :, 0:n], ALU.min).then_inc(S("min_ready"), 1)
                    if i >= 1:
                        got(dve, ("yd", (i - 1) // NC, (i - 1) % NC))
                    link(V_.tensor_tensor(M1[0:n, :, 0:n], CBM[0:n, 0, 0:n].unsqueeze(1).to_broadcast([n, GH, n]),
                                          bc(DTT[0:n, c, h8], n, n), MUL))
                    dve.wait_ge(S("n1_ready"), i + 1)
                    V_.tensor_tensor(M1[0:n, :, 0:n], M1[0:n, :, 0:n], F[1][0:n, :, 0:n], ADD).then_inc(S("m_sum"), 1)
                    if i >= 1:
                        got(dve, ("yt", (i - 1) // NC, (i - 1) % NC))
                    dve.wait_ge(S("xd_ready"), i + 1)
                    yc = YC[0:n, :]
                    yh = yc.rearrange("p (h w) -> p h w", h=GH)
                    if c > 0:
                        got(dve, ("of", g, c))
                        link(V_.tensor_tensor(yh, PS[0:n, 6, :].rearrange("p (h w) -> p h w", h=GH),
                                              bc(EF[0:n, c, h8], n, HD), MUL))
                        free(V_.tensor_tensor(yc, yc, XD[0:n, :], ADD), ("of", g, c))
                        dve.wait_ge(*freed(("of", g, c)))
                        base = yc
                    else:
                        base = XD[0:n, :]
                    if c < 4:
                        got(dve, ("ob", g, c))
                        tmp = YB[0:n, :]
                        free(V_.tensor_tensor(tmp.rearrange("p (h w) -> p h w", h=GH),
                                              PS[0:n, 7, :].rearrange("p (h w) -> p h w", h=GH),
                                              bc(EF[0:n, c, h8b], n, HD), MUL), ("ob", g, c))
                        dve.wait_ge(*freed(("ob", g, c)))
                        link(V_.tensor_tensor(yc, base, tmp, ADD))
                        base = yc
                    got(dve, ("yd", g, c))
                    free(V_.tensor_tensor(yc, base, PS[0:n, 5, :], ADD), ("yd", g, c))
                    if c < 4:
                        got(dve, ("sf", g, c))
                        st = ST[:, c % 2, :]
                        if c == 0:
                            ins = V_.tensor_copy(st, PS[:, 6, :])
                        else:
                            link(V_.tensor_tensor(st.rearrange("p (h w) -> p h w", h=GH),
                                                  ST[:, (c - 1) % 2, :].rearrange("p (h w) -> p h w", h=GH),
                                                  bc(ET[:, c, h8], P, HD), MUL))
                            ins = V_.tensor_tensor(st, st, PS[:, 6, :], ADD)
                        free(ins, ("sf", g, c))
                        dve.wait_ge(*freed(("sf", g, c)))
                    if c % 2 == 1:
                        u = 2 * g + c // 2
                        got(dve, ("ca", u))
                        dve.wait_ge(*freed(("cg", u)))
                        b = bank(("ca", u))
                        if u >= 2:
                            conf_taps((u - 1) * CONF_TAPS)
                            dve.wait_ge(S("cacc_done"), u - 1)
                        free(V_.tensor_tensor(tok(CP[:, u % 2, 15:15 + T2], T2), tok(SGB[:, :], T2), PS[:, b:b + 2, 0:HT],
                                              MUL), ("ca", u))
                    got(dve, ("yt", g, c))
                    if c == 0:
                        dve.wait_ge(*freed(("zt", 4 * g + 3)))
                    yv = YT[:, 4 * g:4 * g + 4, t0:t0 + n]
                    free(V_.tensor_tensor(yv, yv, PS[:, 5, :].rearrange("p (j n) -> p j n", j=4)[:, :, 0:n], MUL), ("yt", g, c))
                    dve.wait_ge(*freed(("yt", g, c)))
                    some_taps(0, 2 * g + c // 2)
            conf_taps(DT * CONF_TAPS)
            got(dve, "lnm")
            mean = GT[:, 0, :]
            free(V_.tensor_scalar(tok(mean, T2), PS[:, 6:8, 0:HT], 1.0 / D, None, MUL), "lnm")
            dve.wait_ge(*freed("lnm"))
            for k in range(DT):
                V_.tensor_tensor(CACC[:, k, :], CACC[:, k, :], mean, SUB).then_inc(S("ln_centred"), 1)
            dve.wait_ge(S("ln_centred"), DT)
            norm_apply("lnv", lambda k: CACC[:, k, :], lambda k: CACC[:, k, :], "ln_scaled")
            norm_apply("ny", lambda k: YT[:, k, :], lambda k: YT[:, k, :], "y_ready", GT[:, 1, :])
            for m in range(DT):
                got(dve, ("co", m))
                dve.wait_ge(*freed(("g1", m)))
                b = bank(("co", m))
                free(V_.tensor_tensor(tok(MG[:, m, :], T2), tok(MG[:, m, :], T2), PS[:, b:b + 2, 0:HT], MUL), ("co", m))
            for m in range(DT):
                got(dve, ("so", m))
                dve.wait_ge(*freed(("g2", m)))
                b = bank(("so", m))
                free(V_.tensor_tensor(tok(GT[:, m % 2, :], T2), tok(GT[:, m % 2, :], T2), PS[:, b:b + 2, 0:HT], MUL),
                     ("so", m))
                dve.wait_ge(*freed(("so", m)))
                V_.tensor_tensor(MG[:, m, :], MG[:, m, :], GT[:, m % 2, :], ADD).then_inc(S("merged"), 1)
            dve.wait_ge(S("h_back"), 16)
            for m in range(DT):
                got(dve, ("out", m))
                b = bank(("out", m))
                free(V_.tensor_tensor(tok(H[:, m, :], T2), tok(H[:, m, :], T2), PS[:, b:b + 2, 0:HT], ADD), ("out", m))
            norm_apply("n6", lambda k: H[:, k, :], lambda k: U[:, k, :], "u_ready")
            got(dve, "lg")
            for c, (t0, n) in enumerate(CHUNKS):
                V_.tensor_reduce(small[0:n, 48 + c:49 + c], PS[0:n, 0, c * EXPERTS:(c + 1) * EXPERTS], AX_X, ALU.max,
                                 negate=True).then_inc(S("lg_max"), 1)
            dve.wait_ge(*freed("lg"))
            dve.wait_ge(S("aff_exp"), NC - 1)
            link(V_.reciprocal(small[:, 56:60], small[:, 56:60]))
            link(V_.reciprocal(small[0:META, 60:61], small[0:META, 60:61]))
            for n, cs in ((P, slice(0, 4)), (META, slice(4, 5))):
                k = cs.stop - cs.start
                V_.tensor_tensor(AFF[0:n, cs, :], AFF[0:n, cs, :],
                                 small[0:n, 56 + cs.start:56 + cs.stop].unsqueeze(2).to_broadcast([n, k, EXPERTS]),
                                 MUL).then_inc(S("aff_ready"), 1)
            for c, (t0, n) in enumerate(CHUNKS):
                for hf in range(2):
                    dve.wait_ge(S("xnt_high"), 2 * c + hf + 1)
                    free(V_.tensor_tensor(XNT[0:n, 1, c, 512 * hf:512 * hf + 512], PS[0:n, 2 + hf, :],
                                          XNT[0:n, 0, c, 512 * hf:512 * hf + 512].bitcast(F32), SUB), ("xn", c, hf))
            E_ = EXPERTS
            TKR = [TK[0:E_, r, :] for r in range(8)]
            got(dve, "af")
            link(V_.tensor_copy(TKR[0][:, 0:512], PS[0:E_, 4, :]))
            free(V_.tensor_copy(TKR[0][:, 512:T2], PS[0:E_, 5, 0:META]), "af")
            dve.wait_ge(*freed("af"))
            src = TKR[0]
            for r in range(TOPK_ROUNDS):
                v8 = TV[0:E_, 8 * r:8 * r + 8]
                link(V_.max(v8, src))
                if r < TOPK_ROUNDS - 1:
                    link(V_.match_replace(TKR[1 + r % 2], v8, src, -1.0))
                    src = TKR[1 + r % 2]
            least = TV[0:E_, CAP - 1:CAP]
            link(V_.tensor_scalar(TKR[1], TKR[0], least, None, ALU.is_gt))
            link(V_.tensor_scalar(TKR[2], TKR[0], least, None, ALU.is_equal))
            link(V_.tensor_reduce(small[0:E_, 64:65], TKR[1], AX_X, ADD))
            link(V_.tensor_scalar(small[0:E_, 64:65], small[0:E_, 64:65], -1.0, float(CAP), MUL, ADD))
            link(V_.memset(TKR[5], 0.0))
            link(V_.tensor_tensor_scan(TKR[3], TKR[2], TKR[5], 0.0, ADD, ADD))
            link(V_.scalar_tensor_tensor(TKR[2], TKR[3], small[0:E_, 64:65], TKR[2], ALU.is_le, MUL))
            link(V_.tensor_tensor(TKR[1], TKR[1], TKR[2], ADD))
            link(V_.tensor_tensor_scan(TKR[3], TKR[1], TKR[5], 0.0, ADD, ADD))
            link(V_.tensor_tensor(TKR[3], TKR[3], TKR[1], MUL))
            V_.tensor_scalar(TKR[0], TKR[3], -1.0, None, ADD).then_inc(S("slots_ready"), 1)
            got(dve, "sl16")
            link(V_.tensor_copy(SLT[:, 0:4, :], PS[:, 0, 0:64].rearrange("p (c n) -> p c n", c=4)))
            free(V_.tensor_copy(SLT[0:META, 4, :], PS[0:META, 0, 64:80]), "sl16")
            dve.wait_ge(*freed("sl16"))
            def select(e):
                V_.tensor_copy(SLS[:, 0:4], SLT[:, 0:4, bass.ds(e, 1)].rearrange("p c n -> p (c n)")).then_inc(S("sel_cp"), 1)
                V_.tensor_copy(SLS[0:META, 4:5], SLT[0:META, 4, bass.ds(e, 1)]).then_inc(S("sel_cp"), 1)
                dve.wait_ge(S("sel_cp"), e * 2 + 2)
                for c, (t0, n) in enumerate(CHUNKS):
                    V_.tensor_scalar(SE[0:n, c, :], iota[0:n, :], SLS[0:n, c:c + 1], None, ALU.is_equal)\
                        .then_inc(S("sel_ready"), 1)
                V_.tensor_copy(small[:, 144:148], AFF[:, 0:4, bass.ds(e, 1)].rearrange("p c n -> p (c n)")).then_inc(S("aff_copied"), 1)
                V_.tensor_copy(small[0:META, 148:149], AFF[0:META, 4, bass.ds(e, 1)]).then_inc(S("aff_copied"), 1)

            def x_low(e, hf):
                dve.wait_ge(S("xgh_ready"), e * 2 + hf + 1)
                V_.tensor_tensor(XG[:, 1, 4 * hf:4 * hf + 4, :], PS[:, 6 + hf, 0:4 * CAP].rearrange("p (k n) -> p k n", k=4),
                                 XG[:, 0, 4 * hf:4 * hf + 4, :].bitcast(F32), SUB).then_inc(S("xgl_ready"), 1)

            def y_low(e, hf):
                dve.wait_ge(S("yeh_ready"), e * 2 + hf + 1)
                cols = slice(512 * hf, 512 * hf + 512)
                V_.scalar_tensor_tensor(YE[0:CAP, 1, cols], PS[0:CAP, 4 + hf, :], AFS[0:CAP], YE[0:CAP, 0, cols].bitcast(F32),
                                        MUL, SUB).then_inc(S("yel_ready"), 1)

            def add(e, m):
                dve.wait_ge(S("combined"), e * DT + m + 1)
                V_.tensor_tensor(tok(H[:, m, :], T2), tok(H[:, m, :], T2), PS[:, 4:6, 0:HT], ADD).then_inc(S("h_added"), 1)

            def expert(e, first=False, last=False):
                for q in range(PIECES):
                    i, kk = q // 4, q % 4
                    at = q - PBUF
                    if at == -1 and not first:
                        y_low(e - 1, 1)
                    if at - 1 in COMBINE_AT and not first:
                        add(e - 1, COMBINE_AT.index(at - 1))
                    if at >= 0 and at < 32 and at % 8 == 7:
                        b = at // 8
                        dve.wait_ge(S("w_used"), e * PIECES + at + 1)
                        dve.wait_ge(S("gate_act"), e * 4 + b + 1)
                        if not (first and b < 2):
                            dve.wait_ge(S("h_turned"), e * 4 + b - 1)
                        V_.tensor_tensor(HGS[0:CAP, b % 2, :], SIL[0:CAP, b % 2, :], PS[0:CAP, 2 * (b % 2) + 1, :], MUL)\
                            .then_inc(S("hgs_ready"), 1)
                    if at in TURN_H_AT:
                        b = TURN_H_AT.index(at)
                        dve.wait_ge(S("hgh_ready"), e * 4 + b + 1)
                        V_.tensor_tensor(HG[:, 1, 4 * b:4 * b + 4, :],
                                         PS[:, 6 + b % 2, 0:4 * CAP].rearrange("p (k n) -> p k n", k=4),
                                         HG[:, 0, 4 * b:4 * b + 4, :].bitcast(F32), SUB).then_inc(S("hgl_ready"), 1)
                    if at == SLOTS_AT:
                        dve.wait_ge(S("sat_turned"), e + 1)
                        if not first:
                            dve.wait_ge(S("yel_ready"), e * 2)
                        V_.tensor_copy(SAT[0:CAP, 0:512], PS[0:CAP, 6, :]).then_inc(S("sat_ready"), 1)
                        V_.tensor_copy(SAT[0:CAP, 512:T2], PS[0:CAP, 7, 0:META]).then_inc(S("sat_ready"), 1)
                        V_.tensor_copy(AFS[0:CAP], PS[0:CAP, 7, 256:257]).then_inc(S("sat_ready"), 1)
                        dve.wait_ge(S("sat_ready"), e * 3 + 3)
                    if at == SLOTS_AT + 1 and not last:
                        select(e + 1)
                    if at in TURN_X_AT and not last:
                        x_low(e + 1, TURN_X_AT.index(at))
                    if at == 43:
                        y_low(e, 0)
                    dve.wait_ge(S("wh_ready"), e * PIECES + q + 1)
                    V_.tensor_tensor(WS[:, 1, q % PBUF, :], ring[:, (N_DENSE + i) % RING, PIECE * kk:PIECE * (kk + 1)],
                                     WS[:, 0, q % PBUF, :].bitcast(F32), SUB).then_inc(S("wl_ready"), 1)

            select(0)
            for hf in range(2):
                x_low(0, hf)
            expert(0, first=True)
            with dve.Fori(1, EXPERTS - 1) as e:
                expert(e)
            expert(EXPERTS - 1, last=True)
            y_low(EXPERTS - 1, 1)
            for m in range(DT):
                add(EXPERTS - 1, m)
            dve.wait_ge(S("h_added"), EXPERTS * DT)
            norm_apply("n7", lambda k: H[:, k, :], lambda k: H[:, k, :], "y_out")

        @blk.gpsimd
        def _(pool):
            G_ = nc.gpsimd
            MUL, SUB = ALU.mult, ALU.subtract

            def mask(buf, fill):
                for kb in range(QB):
                    v = buf[:, ZO[kb]:ZO[kb] + P]
                    last = G_.affine_select(out=v, in_=v, compare_op=ALU.is_gt, fill=fill, base=0,
                                            pattern=[[1, P]], channel_multiplier=-1)
                return last

            pool.wait_ge(S("consts_in"), 48)
            for i in range(SB_HEADS + 1):
                if i < SB_HEADS:
                    pool.wait_ge(S("rope_normed"), i + 1)
                    if i >= 2:
                        pool.wait_ge(S("rope_done"), i - 1)
                    G_.tensor_tensor(U[:, 2 + i % 2, 0:SEQ], QK[:, 8 + i, :], COS, MUL).then_inc(S("cos_part"), 1)
                    pool.wait_ge(S("sp_ready"), i + 1)
                    mask(SP[:, i % 2, :], 0.0).then_inc(S("sp_masked"), 1)
                if i >= 1:
                    pool.wait_ge(*freed(("c", i - 1)))
                    mask(Z[:, (i - 1) % 3, :], -BIG).then_inc(S("arg_masked"), 1)
            pool.wait_ge(*freed(("dn", DT - 1)))
            pool.dma_start(h_dram, H[:, :, :]).then_inc(S("h_saved"), 16)

            def bc(ap, n, w):
                return ap.unsqueeze(2).to_broadcast([n, GH, w])

            def scaled(dst, g, c, n, by, sem):
                G_.tensor_tensor(dst[0:n].rearrange("p (h w) -> p h w", h=GH),
                                 XS[0:n, c, :].rearrange("p (h w) -> p h w", h=GH), bc(by, n, HD), MUL)\
                    .then_inc(S(sem), 1)

            pool.wait_ge(S("h_saved"), 16)
            pool.wait_ge(S("w2_ready"), 1)
            for g in range(GROUPS):
                h8 = slice(GH * g, GH * g + GH)
                h8b = slice(32 + GH * g, 32 + GH * g + GH)
                pool.wait_ge(*freed(("tr", g, 4)))
                for s, c in enumerate(range(NC - 1, 0, -1)):
                    n = CHUNKS[c][1]
                    if s >= 2:
                        got(pool, ("sb", g, c + 2))
                    elif g > 0:
                        got(pool, ("sf", g - 1, 3))
                    scaled(XW[:, s % 2, :], g, c, n, W2[0:n, c, h8b], "xwb_ready")
                for c, (t0, n) in enumerate(CHUNKS):
                    i = NC * g + c
                    F = FR[i % 2]
                    pool.wait_ge(S(f"fr_in{i % 2}"), 32 * (i // 2 + 1))
                    G_.tensor_tensor(F[1][0:n, :, 0:n], F[1][0:n, :, 0:n], bc(FT[0:n, c, h8b], n, n), SUB)\
                        .then_inc(S("t2_ready"), 1)
                    if i >= 1:
                        pool.wait_ge(*freed(("yd", (i - 1) // NC, (i - 1) % NC)))
                    scaled(XD, g, c, n, par[0:n, PARAMS["ssm_d"] + GH * g:PARAMS["ssm_d"] + GH * g + GH], "xd_ready")
                    if c < 4:
                        if c >= 2:
                            got(pool, ("sf", g, c - 2))
                        else:
                            got(pool, ("sb", g, 1))
                        scaled(XW[:, c % 2, :], g, c, n, W2[0:n, c, h8], "xwf_ready")
                    pool.wait_ge(S("min_ready"), i + 1)
                    pool.wait_ge(*freed(("cb", g, c)))
                    G_.tensor_tensor(F[1][0:n, :, 0:n], CBM[0:n, 1, 0:n].unsqueeze(1).to_broadcast([n, GH, n]),
                                     bc(DTT[0:n, c, h8b], n, n), MUL).then_inc(S("n1_ready"), 1)
                    pool.wait_ge(S("m_sum"), i + 1)
                    pool.wait_ge(S("e_ready"), i + 1)
                    G_.tensor_tensor(M1[0:n, :, 0:n], M1[0:n, :, 0:n], F[0][0:n, :, 0:n], MUL).then_inc(S("m_ready"), 1)
            got(pool, ("co", DT - 1))
            pool.wait_ge(S("h_saved"), 16)
            pool.dma_start(H[:, :, :], h_dram).then_inc(S("h_back"), 16)

        @blk.sync
        def _(sp):
            sp.dma_start(consts[:, :], inp["consts"]).then_inc(S("consts_in"), 16)
            sp.dma_start(par[:, :], inp["params"]).then_inc(S("consts_in"), 16)
            sp.dma_start(arena[:, 16384:17408], inp["rope"]).then_inc(S("consts_in"), 16)

            def slot_free(n):
                tag = last_read[loads[n][0]]
                if tag[0] == "sem":
                    sp.wait_ge(S(tag[1]), tag[2])
                else:
                    got(sp, tag)

            for n, (name, put) in enumerate(loads):
                if n >= RING:
                    slot_free(n - RING)
                if name == ("g1", 0):
                    sp.wait_ge(S("m_ready"), NC * GROUPS)
                for at, k, cols, src in put:
                    sp.dma_start(ring[:, n % RING, at:at + k * cols].rearrange("p (k n) -> p k n", k=k), src)\
                        .then_inc(S(f"ring{n % RING}"), 16)

            def expert_load(e, i):
                s = (N_DENSE + i) % RING
                if i < 8:
                    w = inp[("w_exp_gate_2", "w_exp_up_2")[i % 2]]
                    src = w[bass.ds(e, 1), :, (i // 2) * 512:(i // 2) * 512 + 512]
                else:
                    kh, ch = (i - 8) // 2, i % 2
                    src = inp["w_exp_down_2"][bass.ds(e, 1), kh * D:(kh + 1) * D, ch * 512:ch * 512 + 512]
                sp.dma_start(ring[:, s, :].rearrange("p (k n) -> p k n", k=DT),
                             src.rearrange("o (k p) n -> p (o k) n", p=P)).then_inc(S(f"ring{s}"), 16)

            def expert_read(e, i):
                sp.wait_ge(S("wh_ready"), e * PIECES + 4 * i + 4)
                sp.wait_ge(S("wl_ready"), e * PIECES + 4 * i + 4)
                sp.sem_inc(S("slots_turned"), 1)

            for i in range(RING):
                slot_free(N_DENSE - RING + i)
                expert_load(0, i)
            with sp.Fori(0, EXPERTS - 1) as e:
                for i in range(RING, 12):
                    expert_read(e, i - RING)
                    expert_load(e, i)
                for i in range(RING):
                    expert_read(e, 12 - RING + i)
                    expert_load(e + 1, i)
            for i in range(RING, 12):
                expert_read(EXPERTS - 1, i - RING)
                expert_load(EXPERTS - 1, i)
            for k in range(DT):
                sp.wait_ge(S("y_out"), k + 1)
                sp.dma_start(out[k * P:(k + 1) * P, :], H[:, k, META:T2]).then_inc(S("stored"), 16)
            sp.wait_ge(S("stored"), 16 * DT)


WEIGHTS = ["w_in", "w_o", "w_gate", "w_up", "w_down", "w_in_2", "w_conf_out_2", "w_ssm_out_2", "w_out_2",
           "w_exp_gate_2", "w_exp_up_2", "w_exp_down_2"]


def shape_constants():
    i = np.arange(P)
    c = np.zeros((P, N_CONSTS), np.float32)
    put = lambda name, a: c.__setitem__((slice(None), slice(CONSTS[name], CONSTS[name] + a.shape[1])), a)
    put("ident", np.eye(P))
    put("ones", np.ones((P, P)))
    put("upper", (i[:, None] <= i[None, :]).astype(float))
    put("lower", (i[:, None] >= i[None, :]).astype(float))
    put("heads", (i[:, None] // HD == i[None, :] // HD).astype(float))
    rot = np.zeros((P, P))
    for h0 in (0, HD):
        for r in range(HD // 2):
            rot[h0 + HD // 2 + r, h0 + r] = -1.0
            rot[h0 + r, h0 + HD // 2 + r] = 1.0
    put("rot", rot)
    put("iota", np.broadcast_to(np.arange(CAP), (P, CAP)))
    put("causal", np.where(i[None, :] > i[:, None], -BIG, 0.0))
    freq = (np.float32(10000.0) ** (-np.arange(HD // 2, dtype=np.float32) / np.float32(HD // 2))).astype(np.float32)
    ang = (np.arange(SEQ, dtype=np.float32)[None, :] * freq[i % (HD // 2), None]).astype(np.float32).astype(np.float64)
    return c, np.concatenate([np.cos(ang), np.sin(ang)], axis=1).astype(np.float32)


def kernel(**inputs):
    import numpy as np
    import concourse.bacc as bacc
    from concourse.bass_utils import run_bass_kernel_spmd

    x = {k: np.asarray(v) for k, v in inputs.items()}
    par = np.zeros((P, N_PARAMS), np.float32)

    def put(name, a):
        a = a.reshape(a.shape[0], -1)
        par[:a.shape[1], PARAMS[name]:PARAMS[name] + a.shape[0]] = a.T

    tiles = lambda v: v.reshape(-1, P)
    put("attn_g", tiles(x["attn_norm_g"]))
    put("ffn_g", tiles(x["ffn_norm_g"]))
    put("mix_g", tiles(x["w_norm_mix_2"]))
    put("ffn2_g", tiles(x["w_norm_ffn_2"]))
    put("final_g", tiles(x["w_norm_final_2"]))
    put("subln_g", tiles(x["diff_subln_g"]))
    for name in ("q_g", "k_g"):
        g = x[f"diff_{name[0]}_norm_g"].reshape(-1)
        put(name, np.concatenate([g, g])[None])
    put("lam", np.stack([x[f"lambda_{n}"].reshape(-1) for n in ("q1", "k1", "q2", "k2")]))
    put("conf_w", x["w_conf_dw_2"][0].reshape(CONF_TAPS, DT, P).transpose(1, 0, 2).reshape(-1, P))
    put("conf_b", tiles(x["b_conf_dw_2"]))
    put("ln_g", tiles(x["conf_ln_g_2"]))
    put("ln_b", tiles(x["conf_ln_b_2"]))
    put("ssm_w", x["w_ssm_conv_2"][0].reshape(SSM_TAPS, 24, P).transpose(1, 0, 2).reshape(-1, P))
    put("ssm_b", tiles(x["b_ssm_conv_2"]))
    put("ssm_norm_g", tiles(x["w_ssm_norm_2"]))
    put("dt_bias", x["ssm_dt_bias_2"].reshape(1, 64))
    put("a_log", x["ssm_a_log_2"].reshape(1, 64))
    par[:, PARAMS["ssm_d"]:PARAMS["ssm_d"] + HEADS] = x["ssm_d_2"].reshape(1, HEADS)
    par[:, PARAMS["router"]:PARAMS["router"] + DT * EXPERTS] = \
        x["w_router_2"][0].reshape(DT, P, EXPERTS).transpose(1, 0, 2).reshape(P, -1)
    par[:, PARAMS["eps"]] = EPS
    par[:, PARAMS["subln_eps"]] = SUBLN_EPS
    par[:, PARAMS["one"]] = 1.0
    consts, rope = shape_constants()
    arrays = {"params": par, "consts": consts, "rope": rope,
              "h_t": np.ascontiguousarray(np.concatenate([x["meta_tokens_2"], x["x"][0]], axis=0).T)}
    for name in WEIGHTS:
        arrays[name] = np.ascontiguousarray(x[name][0])

    nc = bacc.Bacc("TRN2", target_bir_lowering=False, num_devices=1)
    inp = {k: nc.dram_tensor(k, a.shape, mybir.dt.from_np(a.dtype), kind="ExternalInput").ap() for k, a in arrays.items()}
    out = nc.dram_tensor("out_t", (D, SEQ), F32, kind="ExternalOutput").ap()
    program(nc, inp, out)
    r = run_bass_kernel_spmd(nc, [arrays], core_ids=[0])
    return np.ascontiguousarray(np.asarray(r.results[0]["out_t"]).T)[None]
```

```python
import math
from contextlib import ExitStack

import concourse.bass as bass
import numpy as np
from concourse import mybir

F32, F32R = mybir.dt.float32, mybir.dt.float32r
ALU = mybir.AluOpType
ACT = mybir.ActivationFunctionType
AX_X = mybir.AxisListType.X

P = 128
D = 1024
DT = D // P
SEQ = 512
META = 16
T2 = SEQ + META
HT = T2 // 2
HD = 64
QB = SEQ // P
SB_HEADS, DIFF_HEADS = 8, 4
FF = 2816
FFT = FF // P
CONF_TAPS, SSM_TAPS = 31, 7
INNER, GROUPS, STATE, HEADS = 2048, 4, 128, 32
GH = HEADS // GROUPS
OFF_G, OFF_Z = 1024, 2048
OFF_X = OFF_Z + INNER
OFF_B = OFF_X + INNER
OFF_C = OFF_B + GROUPS * STATE
OFF_DT = OFF_C + GROUPS * STATE
OFF_GATE = OFF_DT + 2 * HEADS
EXPERTS, EFF = 16, 2048
EFT = EFF // P
CAP = 2 * T2 // EXPERTS
CHUNKS = [(c * P, min(P, T2 - c * P)) for c in range(-(-T2 // P))]
NC = len(CHUNKS)
SLOT = 4096
E_LOADS = 12
PIECE = 1024
PIECES = E_LOADS * SLOT // PIECE
IBUF = 4
FBUF = 3
PBUF = 4
RING = 4
BIG = 1e30
LAMBDA_INIT = 0.8 - 0.6 * math.exp(0.0)
EPS, SUBLN_EPS = 1e-6, 1e-5
TOPK_ROUNDS = -(-CAP // 8)

COMBINE_AT = [4 + 3 * m for m in range(DT)]
TURN_H_AT = [9, 17, 25, 33]
SLOTS_AT = 28
GATHER_AT = [35, 36]
TURN_X_AT = [38, 39]

PARAMS = {}
CONSTS = {}


def _columns(table, sizes):
    at = 0
    for name, n in sizes:
        table[name] = at
        at += n
    return at


N_PARAMS = _columns(PARAMS, [
    ("attn_g", DT), ("ffn_g", DT), ("mix_g", DT), ("ffn2_g", DT), ("final_g", DT), ("subln_g", 1),
    ("q_g", 1), ("k_g", 1), ("lam", 4), ("conf_w", DT * CONF_TAPS), ("conf_b", DT), ("ln_g", DT),
    ("ln_b", DT), ("ssm_w", 24 * SSM_TAPS), ("ssm_b", 24), ("ssm_norm_g", 16), ("dt_bias", 1),
    ("a_log", 1), ("ssm_d", HEADS), ("router", DT * EXPERTS), ("eps", 1), ("subln_eps", 1), ("one", 1)])
N_CONSTS = _columns(CONSTS, [
    ("ident", P), ("ones", P), ("upper", P), ("lower", P), ("heads", P), ("rot", P), ("iota", CAP),
    ("causal", P)])


def program(nc, inp, out):
    ctx = ExitStack()
    with ctx:
        def sb(name, shape):
            return ctx.enter_context(nc.sbuf_tensor(name, shape, F32))

        sems = {}

        def S(name):
            if name not in sems:
                sems[name] = ctx.enter_context(nc.semaphore(name))
            return sems[name]

        H = sb("H", [P, DT, T2])
        consts = sb("consts_sb", [P, N_CONSTS])
        par = sb("par", [P, N_PARAMS])
        SQ = sb("SQ", [P, 2, T2])
        RS = sb("RS", [P, T2])
        AR = 24448
        small = sb("small", [P, 256])
        before = ExitStack()
        U = before.enter_context(nc.sbuf_tensor("U", [P, DT, T2], F32))
        arena = before.enter_context(nc.sbuf_tensor("arena", [P, AR], F32))
        ring = before.enter_context(nc.sbuf_tensor("ring", [P, RING, SLOT], F32))
        before.close()
        ffn = ExitStack()
        UX = ffn.enter_context(nc.sbuf_tensor("UX", [P, 2, DT, SEQ], F32R))
        WF = ffn.enter_context(nc.sbuf_tensor("WF", [P, 2, FBUF, PIECE], F32R))
        GX = ffn.enter_context(nc.sbuf_tensor("GX", [P, 2, FFT, SEQ], F32R))
        assert 2 * (DT + FFT) * SEQ + 2 * FBUF * PIECE <= DT * T2 + AR + 2 * SLOT
        ffn.close()
        proj_ = ExitStack()
        proj_.enter_context(nc.sbuf_tensor("below_slot_0", [P, DT * T2 + AR], F32))
        WI = proj_.enter_context(nc.sbuf_tensor("WI", [P, 2, IBUF, PIECE], F32R))
        proj_.close()

        def parts(name, shape):
            return ctx.enter_context(nc.sbuf_tensor(name, shape, F32R))

        WS = parts("WS", [P, 2, PBUF, PIECE])
        XG = parts("XG", [P, 2, DT, CAP])
        SE = parts("SE", [P, NC, CAP])
        HG = parts("HG", [P, 2, EFT, CAP])
        YE = parts("YE", [P, 2, D])
        SAT = parts("SAT", [P, T2])
        XNT = parts("XNT", [P, 2, NC, D])
        XGS, SIL, HGS, AFF, SLT = [arena[:, o:o + n] for o, n in (
            (20288, D), (21312, D), (22336, D), (23360, NC * EXPERTS), (23440, NC * EXPERTS))]
        SIL, HGS = [v.rearrange("p (b n) -> p b n", b=2) for v in (SIL, HGS)]
        AFF, SLT = [v.rearrange("p (c n) -> p c n", c=NC) for v in (AFF, SLT)]
        assert 2 * PBUF * PIECE + 2 * CAP * (DT + EFT) + NC * CAP + 2 * D + T2 + 2 * NC * D <= DT * T2 + 20288
        ctx.enter_context(nc.sbuf_tensor("tail", [P, DT * T2 + AR - (2 * PBUF * PIECE + 2 * CAP * (DT + EFT) + NC * CAP
                                                                    + 2 * D + T2 + 2 * NC * D)], F32))
        ctx.enter_context(nc.sbuf_tensor("ring_place", [P, RING, SLOT], F32))
        PS = ctx.enter_context(nc.psum_tensor("PS", [P, 8, 512], F32))
        fr_dram = nc.dram_tensor("ssd_sums", [2 * HEADS, T2], F32).ap()
        h_dram = nc.dram_tensor("residual", [P, DT, T2], F32).ap()

        def area(sizes):
            at, views = 0, []
            for shape in sizes:
                n = int(np.prod(shape))
                v = arena[:, at:at + n]
                if len(shape) == 2:
                    v = v.rearrange("p (a b) -> p a b", a=shape[0])
                if len(shape) == 3:
                    v = v.rearrange("p (a b c) -> p a b c", a=shape[0], b=shape[1])
                views.append(v)
                at += n
            assert at <= AR, at
            return views

        def C(name, n=P):
            return consts[:, CONSTS[name]:CONSTS[name] + n]

        def pcol(name, i=0):
            return par[:, PARAMS[name] + i:PARAMS[name] + i + 1]

        ident, ones, upper, lower = C("ident"), C("ones"), C("upper"), C("lower")
        heads_ones, rot, iota, causal = C("heads"), C("rot"), C("iota", CAP), C("causal")

        def halves(T):
            return [(0, T)] if T <= 512 else [(0, HT), (HT, T2)]

        def ps(banks, T):
            return PS[:, banks[0], 0:T] if T <= 512 else PS[:, banks[0]:banks[0] + 2, 0:HT]

        def tok(ap, T):
            return ap if T <= 512 else ap.rearrange("p (h n) -> p h n", h=2)

        Z, SP, QK, V, MIX, ROPE = area([(3, 1280), (2, 1280), (16, SEQ), (QB, D), (DT, SEQ), (2, SEQ)])
        COS, SIN = ROPE[:, 0, :], ROPE[:, 1, :]
        scr = arena[:, 0:6400]
        PR = scr[:, 0:2048].rearrange("p (b c n) -> p b c n", b=2, c=2)
        DA = scr[:, 2048:3072].rearrange("p (b n) -> p b n", b=2)
        DAT = scr[:, 3072:4096].rearrange("p (b n) -> p b n", b=2)
        DA2 = scr[:, 4096:5120].rearrange("p (b n) -> p b n", b=2)
        ZO = [0, 512, 1024, 896]
        (XS, BF, CF, BT, SNAP, YT, XP, CP, ST, M1, XW, YC, XD, YB, CBM, DTT, AAT, FT, EF, W2, ET) = area([
            (NC, 512), (T2,), (T2,), (NC, P), (4, 512), (16, T2), (2, T2 + SSM_TAPS - 1),
            (2, T2 + CONF_TAPS - 1), (2, 512), (GH, P), (2, 512), (512,), (512,), (512,), (2, P), (NC, 64),
            (NC, 64), (NC, 64), (NC, 64), (NC, 64), (NC, 64)])
        CACC = H
        CO = SQ
        SGB = RS
        FR = [[ring[:, 2 * b + d, 3072:4096].rearrange("p (h n) -> p h n", h=GH) for d in range(2)]
              for b in range(2)]
        MG = arena[:, 0:DT * T2].rearrange("p (a n) -> p a n", a=DT)
        GT = arena[:, 4224:4224 + 2 * T2].rearrange("p (a n) -> p a n", a=2)
        DTF = arena[:, 6304:6304 + 6 * T2].rearrange("p (a n) -> p a n", a=6)
        TK, TV = area([(8, T2), (8 * TOPK_ROUNDS,)])
        AFS, SLS = small[:, 128:129], small[:, 136:136 + NC]

        loads = []

        def rows(w, k, lo, hi):
            return w[0:k * P, lo:hi].rearrange("(k p) n -> p k n", p=P)

        def block(name, *parts):
            at, put = 0, []
            for src in parts:
                k, n = src.shape[1], src.shape[2]
                put.append((at, k, n, src))
                at += k * n
            assert at <= SLOT
            loads.append((name, put))

        w1, w2 = inp["w_in"], inp["w_in_2"]
        for b in range(6):
            block(("in", b), rows(w1, DT, b * 512, b * 512 + 512))
        for b in range(2):
            block(("wo", b), rows(inp["w_o"], DT, b * 512, b * 512 + 512))
        for b in range(FFT // 2):
            block(("gu", b), rows(inp["w_gate"], DT, b * 256, b * 256 + 256),
                  rows(inp["w_up"], DT, b * 256, b * 256 + 256))
        for b in range(4):
            for kh in range(2):
                block(("down", b, kh), inp["w_down"][kh * 11 * P:(kh + 1) * 11 * P, b * 256:b * 256 + 256]
                      .rearrange("(k p) n -> p k n", p=P))
        block(("dt",), rows(w2, DT, OFF_DT, OFF_DT + 64))
        for g in range(GROUPS):
            for i in range(2):
                bc = (OFF_B, OFF_C)[i] + g * P
                block(("xbc", g, i), rows(w2, DT, OFF_X + g * 512 + i * 256, OFF_X + g * 512 + i * 256 + 256),
                      rows(w2, DT, bc, bc + P))
            for i in range(2):
                block(("z", g, i), rows(w2, DT, OFF_Z + g * 512 + i * 256, OFF_Z + g * 512 + i * 256 + 256))
            for i in range(2):
                u = 2 * g + i
                block(("conf", u), rows(w2, DT, u * P, u * P + P), rows(w2, DT, OFF_G + u * P, OFF_G + u * P + P))
        for b in range(2):
            block(("g1", b), rows(w2, DT, OFF_GATE + b * 512, OFF_GATE + b * 512 + 512))
        for b in range(2):
            block(("co", b), rows(inp["w_conf_out_2"], DT, b * 512, b * 512 + 512))
        for b in range(4):
            block(("g2", b), rows(w2, DT, OFF_GATE + D + b * 256, OFF_GATE + D + b * 256 + 256))
            block(("so", b), rows(inp["w_ssm_out_2"], 16, b * 256, b * 256 + 256))
        for b in range(2):
            block(("out", b), rows(inp["w_out_2"], DT, b * 512, b * 512 + 512))
        N_DENSE = len(loads)
        where = {name: n for n, (name, _) in enumerate(loads)}
        order_of = [2, 3, 0, 1]
        slot_of, turn_ = [], 0
        for name, _ in loads:
            if name[0] in ("in", "wo", "gu", "down"):
                slot_of.append(2 + turn_ % 2)
            elif name == ("dt",):
                turn_ = 1
                slot_of.append(order_of[turn_ % RING])
            else:
                slot_of.append(order_of[turn_ % RING])
            turn_ += 1
        EXP0 = (slot_of[-1] + 1) % RING
        prev = [max([j for j in range(n) if slot_of[j] == slot_of[n]], default=None) for n in range(len(loads))]
        landed, count = {}, [0] * RING
        for n, (name, put) in enumerate(loads):
            count[slot_of[n]] += 16 * len(put)
            landed[name] = count[slot_of[n]]
        RING0 = list(count)
        AFTER_FFN = [loads[min(n for n in range(where[("dt",)], N_DENSE) if slot_of[n] == b)][0] for b in (0, 1)]
        last_read = {}

        def landed_e(eng, e, i):
            s = (EXP0 + i) % RING
            eng.wait_ge(S(f"ring{s}"), e * (16 * E_LOADS // RING) + RING0[s] + 16 * (i // RING + 1))

        def slot(name, part=0):
            at, k, n, _ = loads[where[name]][1][part]
            return ring[:, slot_of[where[name]], at:at + k * n].rearrange("p (k n) -> p k n", k=k)

        pieces = []
        for m in range(FFT):
            for part in range(2):
                pieces.append((("gu", m // 2), part, 0, DT, m % 2))
        for b in range(4):
            for kh in range(2):
                for mm in range(2):
                    pieces.append((("down", b, kh), 0, 0, 6, mm))
                    pieces.append((("down", b, kh), 0, 6, 5, mm))

        IN_KINDS = ("q", "k", "v", "q", "k", "v")

        def in_raw(p):
            b, j = divmod(p, 4)
            w = slot(("in", b))
            return w[:, 2 * j:2 * j + 2, :] if IN_KINDS[b] == "v" else w[:, :, j * P:j * P + P]

        def in_split(which, p):
            return WI[:, which, p % IBUF, :].rearrange("p (k n) -> p k n", k=2 if IN_KINDS[p // 4] == "v" else DT)

        in_used = []

        def raw(p):
            name, part, k0, n, m = pieces[p]
            return slot(name, part)[:, k0:k0 + n, m * P:m * P + P]

        def split(which, p):
            n = pieces[p][3]
            return WF[:, which, p % FBUF, 0:n * P].rearrange("p (k n) -> p k n", k=n)

        piece_used = []

        uses, last_tag, order, filled_n, freed_n = [0] * 8, [None] * 8, {}, [0] * 8, [0] * 8

        def filled(tag):
            b, n = order[tag]
            return S(f"filled{b}"), n

        def freed(tag):
            b, n = order[tag]
            return S(f"freed{b}"), n

        def got(eng, tag):
            eng.wait_ge(*filled(tag))

        def free(ins, tag):
            return ins.then_inc(S(f"freed{order[tag][0]}"), 1)

        def bank(tag):
            return order[tag][0]

        def chain(eng, name):
            n = [0]

            def link(ins):
                n[0] += 1
                ins.then_inc(S(name), 1)
                eng.wait_ge(S(name), n[0])
            return link

        NORMS = [("n1", DT, SEQ, 1 / D, "eps", "attn_g"), ("n2", DT, SEQ, 1 / D, "eps", "ffn_g"),
                 ("n3", DT, T2, 1 / D, "eps", "mix_g"), ("ny", 16, T2, 1 / INNER, "eps", "ssm_norm_g"),
                 ("lnv", DT, T2, 1 / D, "eps", "ln_g"), ("n6", DT, T2, 1 / D, "eps", "ffn2_g"),
                 ("n7", DT, T2, 1 / D, "eps", "final_g")]
        sq_base, used_base = {}, {}
        a = b_ = 0
        for nm, K, *_ in NORMS:
            sq_base[nm], used_base[nm] = a, b_
            a += K
            b_ += K - 1
        NORM = {x[0]: x for x in NORMS}
        u_base = {"n3": 0, "n6": DT}

        blk = ctx.enter_context(nc.Block())

        @blk.tensor
        def _(pe):
            def open_(tag, *banks):
                for b in banks:
                    if last_tag[b] is not None:
                        pe.wait_ge(*freed(last_tag[b]))
                    last_tag[b] = tag
                uses[banks[0]] += 1
                order[tag] = (banks[0], uses[banks[0]])

            def fill(ins, tag):
                ins.then_inc(S(f"filled{order[tag][0]}"), 1)

            def arrived(name):
                pe.wait_ge(S(f"ring{slot_of[where[name]]}"), landed[name])

            def dense(tag, banks, K, T, lhs, rhs, M=P, reads=None):
                open_(tag, *banks)
                for k in range(K):
                    for i, (lo, hi) in enumerate(halves(T)):
                        last = nc.tensor.matmul(PS[0:M, banks[i], 0:hi - lo], lhs(k), rhs(k)[:, lo:hi],
                                                start=(k == 0), stop=(k == K - 1))
                fill(last, tag)
                if reads:
                    last_read[reads] = tag

            def norm_sum(nm, banks):
                _, K, T, *_ = NORM[nm]
                open_(nm, *banks)
                for k in range(K):
                    pe.wait_ge(S("sq_ready"), sq_base[nm] + k + 1)
                    for i, (lo, hi) in enumerate(halves(T)):
                        last = nc.tensor.matmul(PS[:, banks[i], 0:hi - lo], ones, SQ[:, k % 2, lo:hi],
                                                start=(k == 0), stop=(k == K - 1))
                    if k < K - 1:
                        last.then_inc(S("sq_used"), 1)
                fill(last, nm)

            pe.wait_ge(S("consts_in"), 48)
            pe.wait_ge(S("lam_prod"), 1)
            open_("lam", 7)
            fill(nc.tensor.matmul(PS[:, 7, 0:2], ones[0:HD, :], small[0:HD, 0:2], start=True, stop=True), "lam")
            norm_sum("n1", (6,))
            partial_in = 0
            for b, kind in enumerate(IN_KINDS):
                for j in range(4):
                    p = 4 * b + j
                    hi, lo = in_split(0, p), in_split(1, p)
                    pe.wait_ge(S("iw_high"), p + 1)
                    if kind == "v":
                        pe.wait_ge(S("iw_low"), p + 1)
                        for m in range(4):
                            if j == 0:
                                open_(("in", b, m), m)
                            for k in range(2):
                                kk = 2 * j + k
                                x = UX[:, :, kk, m * P:m * P + P]
                                nc.tensor.matmul(PS[:, m, :], x[:, 0, :], hi[:, k, :], start=(kk == 0), stop=False)
                                nc.tensor.matmul(PS[:, m, :], x[:, 0, :], lo[:, k, :], start=False, stop=False)
                                last = nc.tensor.matmul(PS[:, m, :], x[:, 1, :], hi[:, k, :], start=False, stop=(kk == DT - 1))
                            if j == 3:
                                fill(last, ("in", b, m))
                        if j == 3:
                            in_used.append(filled(("in", b, 3)))
                        else:
                            partial_in += 1
                            last.then_inc(S("iw_used"), 1)
                            in_used.append((S("iw_used"), partial_in))
                    else:
                        open_(("in", b, j), j)
                        for k in range(DT):
                            if p == 0:
                                pe.wait_ge(S("ux_low"), k + 1)
                            nc.tensor.matmul(PS[:, j, :], hi[:, k, :], UX[:, 0, k, :], start=(k == 0), stop=False)
                            nc.tensor.matmul(PS[:, j, :], hi[:, k, :], UX[:, 1, k, :], start=False, stop=False)
                        pe.wait_ge(S("iw_low"), p + 1)
                        for k in range(DT):
                            last = nc.tensor.matmul(PS[:, j, :], lo[:, k, :], UX[:, 0, k, :], start=False, stop=(k == DT - 1))
                        fill(last, ("in", b, j))
                        in_used.append(filled(("in", b, j)))
                last_read[("in", b)] = ("sem", [("iw_high", 4 * b + 4), ("iw_low", 4 * b + 4)])
            for j in range(8):
                pe.wait_ge(S("rope_sq"), j + 1)
                open_(("rn", j), 6 + j % 2)
                fill(nc.tensor.matmul(PS[:, 6 + j % 2, :], heads_ones, SQ[:, j % 2, 0:SEQ], start=True, stop=True),
                     ("rn", j))
            for i in range(SB_HEADS + 2):
                if i < SB_HEADS:
                    j, r = i // 2, HD * (i % 2)
                    if i == 0:
                        for b in (0, 1):
                            for m in range(4):
                                pe.wait_ge(*freed(("in", b, m)))
                    open_(("z", i), 0, 1, 2)
                    for kb in range(QB):
                        o = ZO[kb]
                        last = nc.tensor.matmul(PS[:, o // 512, o % 512:o % 512 + SEQ - kb * P],
                                                QK[r:r + HD, 4 + j, kb * P:kb * P + P], QK[r:r + HD, j, kb * P:SEQ],
                                                start=True, stop=True)
                    fill(last, ("z", i))
                    pe.wait_ge(S("rope_normed"), i + 1)
                    open_(("rot", i), 7)
                    fill(nc.tensor.matmul(PS[:, 7, :], rot, QK[:, 8 + i, :], start=True, stop=True), ("rot", i))
                if 1 <= i <= SB_HEADS:
                    h = i - 1
                    pe.wait_ge(S("sp_masked"), h + 1)
                    open_(("c", h), 3, 4, 5)
                    for kb in range(QB):
                        for k2 in range(kb, QB):
                            o = ZO[kb] + (k2 - kb) * P
                            last = nc.tensor.matmul(PS[:, 3 + o // 512, o % 512:o % 512 + SEQ - k2 * P],
                                                    lower if k2 == kb else ones,
                                                    SP[:, h % 2, ZO[k2]:ZO[k2] + SEQ - k2 * P],
                                                    start=(k2 == kb), stop=(k2 == QB - 1))
                    fill(last, ("c", h))
                if i >= 2:
                    h = i - 2
                    r = HD * (h % 2)
                    pe.wait_ge(S("w_ready"), h + 1)
                    if h == 0:
                        for b in (2, 5):
                            for m in range(4):
                                pe.wait_ge(*freed(("in", b, m)))
                    open_(("o", h), 6)
                    for kb in range(QB):
                        last = nc.tensor.matmul(PS[r:r + HD, 6, kb * P:SEQ], V[:, kb, h * HD:h * HD + HD],
                                                Z[:, h % 3, ZO[kb]:ZO[kb] + SEQ - kb * P],
                                                start=(kb == 0), stop=(kb == QB - 1))
                    fill(last, ("o", h))
            pe.wait_ge(S("rope_done"), 8)
            steps = [(h, qb) for h in range(DIFF_HEADS) for qb in range(QB)]
            for n in range(len(steps) + 3):
                if n < len(steps):
                    h, qb = steps[n]
                    b0 = 2 * (n % 2)
                    open_(("s", n), b0, b0 + 1)
                    for c in range(2):
                        last = nc.tensor.matmul(PS[:, b0 + c, 0:(qb + 1) * P],
                                                QK[HD * c:HD * c + HD, 8 + h, qb * P:qb * P + P],
                                                QK[HD * c:HD * c + HD, 12 + h, 0:(qb + 1) * P], start=True, stop=True)
                    fill(last, ("s", n))
                if 2 <= n <= len(steps) + 1:
                    m = n - 2
                    pe.wait_ge(S("diff_map"), m + 1)
                    open_(("at", m), 4 + m % 2)
                    for kb in range(steps[m][1] + 1):
                        last = nc.tensor.transpose(PS[:, 4 + m % 2, kb * P:kb * P + P],
                                                   DA[:, m % 2, kb * P:kb * P + P], ident)
                    fill(last, ("at", m))
                if n >= 3:
                    m = n - 3
                    h, qb = steps[m]
                    pe.wait_ge(*freed(("at", m)))
                    if qb == 0:
                        open_(("do", h), 6 + h % 2)
                    for kb in range(qb + 1):
                        last = nc.tensor.matmul(PS[:, 6 + h % 2, qb * P:qb * P + P],
                                                V[:, kb, 512 + h * P:512 + h * P + P],
                                                DAT[:, m % 2, kb * P:kb * P + P], start=(kb == 0), stop=(kb == qb))
                    if qb == QB - 1:
                        fill(last, ("do", h))
                    else:
                        last.then_inc(S("diff_o"), 1)
            def subln_sum(h):
                pe.wait_ge(S("subln_sq"), h + 1)
                open_(("sl", h), 6 + h % 2)
                fill(nc.tensor.matmul(PS[:, 6 + h % 2, :], ones, SQ[:, h % 2, 0:SEQ], start=True, stop=True), ("sl", h))

            pe.wait_ge(*freed(("o", SB_HEADS - 1)))
            def wo(m, ks):
                name = ("wo", m // 4)
                w = slot(name)
                if ks.start == 0:
                    open_(("wo", m), m % 4)
                for k in ks:
                    last = nc.tensor.matmul(PS[:, m % 4, :], w[:, k, (m % 4) * P:(m % 4) * P + P], MIX[:, k, :],
                                            start=(k == 0), stop=(k == DT - 1))
                if ks.stop == DT:
                    fill(last, ("wo", m))
                    last_read[name] = ("wo", m)

            for m in range(DT):
                if m in (0, 4):
                    arrived(("wo", m // 4))
                if m < 4:
                    subln_sum(m)
                wo(m, range(0, 4 if m < 4 else DT))
                if m == 3:
                    pe.wait_ge(S("mix_ready"), DIFF_HEADS)
                    for j in range(4):
                        wo(j, range(4, DT))
            norm_sum("n2", (6,))

            def split_piece(tag, p, bank, src, k0, start, stop):
                n = pieces[p][3]
                hi, lo = split(0, p), split(1, p)
                pe.wait_ge(S("fw_high"), p + 1)
                for k in range(n):
                    if p == 0:
                        pe.wait_ge(S("ux_low"), DT + k + 1)
                    nc.tensor.matmul(PS[:, bank, :], hi[:, k, :], src[:, 0, k0 + k, :], start=(start and k == 0), stop=False)
                    nc.tensor.matmul(PS[:, bank, :], hi[:, k, :], src[:, 1, k0 + k, :], start=False, stop=False)
                pe.wait_ge(S("fw_low"), p + 1)
                for k in range(n):
                    last = nc.tensor.matmul(PS[:, bank, :], lo[:, k, :], src[:, 0, k0 + k, :], start=False,
                                            stop=(stop and k == n - 1))
                if stop:
                    fill(last, tag)
                    piece_used.append(filled(tag))
                else:
                    partial[0] += 1
                    last.then_inc(S("fw_used"), 1)
                    piece_used.append((S("fw_used"), partial[0]))

            partial = [0]

            for m in range(FFT):
                for part, kind in enumerate(("ga", "up")):
                    open_((kind, m), 2 * (m % 3) + part)
                    split_piece((kind, m), 2 * m + part, 2 * (m % 3) + part, UX, 0, True, True)
                last_read[("gu", m // 2)] = ("sem", [("fw_high", 4 * (m // 2) + 4), ("fw_low", 4 * (m // 2) + 4)])
            p = 2 * FFT
            for b in range(4):
                for kh in range(2):
                    for mm in range(2):
                        tag = ("dn", 2 * b + mm)
                        bank = 2 * (b % 3) + mm
                        if kh == 0:
                            open_(tag, bank)
                        for half in range(2):
                            if b == 0 and mm == 0:
                                pe.wait_ge(S("gx_low"), 11 * kh + (6, 11)[half])
                            split_piece(tag, p, bank, GX, 11 * kh + 6 * half, kh == 0 and half == 0, kh == 1 and half == 1)
                            p += 1
                    last_read[("down", b, kh)] = ("sem", [("fw_high", p), ("fw_low", p)])
            norm_sum("n3", (6, 7))
            pe.wait_ge(S("u_ready"), u_base["n3"] + DT)
            arrived(("dt",))
            w = slot(("dt",))
            dense("dt", (6, 7), DT, T2, lambda k: w[:, k, :], lambda k: U[:, k, :], M=64, reads=("dt",))
            pair = [0]

            def proj(tag, w, cols, name):
                b = 2 * (pair[0] % 2)
                pair[0] += 1
                dense(tag, (b, b + 1), DT, T2, lambda k: w[:, k, cols], lambda k: U[:, k, :], reads=name)

            def xbc(g, i, j):
                name = ("xbc", g, i)
                arrived(name)
                if j < 2:
                    proj(("xb", g, 3 * i + j), slot(name, 0), slice(j * P, j * P + P), name)
                else:
                    proj(("xb", g, 3 * i + 2), slot(name, 1), slice(0, P), name)

            xbc(0, 0, 0)
            xbc(0, 0, 1)
            pe.wait_ge(S("dt_done"), 2)
            for part, src in enumerate((0, 5)):
                open_(("dtT", part), 4 + part)
                for c, (t0, n) in enumerate(CHUNKS):
                    last = nc.tensor.transpose(PS[0:n, 4 + part, c * 64:c * 64 + 64], DTF[0:64, src, t0:t0 + n],
                                               ident[0:64, 0:64])
                fill(last, ("dtT", part))
            pe.wait_ge(*freed(("dtT", 0)))
            pe.wait_ge(*freed(("dtT", 1)))
            open_("F", 6)
            for c, (t0, n) in enumerate(CHUNKS):
                for d, tri in enumerate((upper, lower)):
                    last = nc.tensor.matmul(PS[0:n, 6, c * 64 + 32 * d:c * 64 + 32 * d + 32], tri[0:n, 0:n],
                                            AAT[0:n, c, 32 * d:32 * d + 32], start=True, stop=True)
            fill(last, "F")
            open_("TOT", 7)
            for c, (t0, n) in enumerate(CHUNKS):
                last = nc.tensor.matmul(PS[:, 7, c * 64:c * 64 + 64], ones[0:n, :], AAT[0:n, c, :], start=True, stop=True)
            fill(last, "TOT")
            open_("FR", 4, 5)
            for c, (t0, n) in enumerate(CHUNKS):
                for d, tri in enumerate((upper, lower)):
                    last = nc.tensor.matmul(PS[32 * d:32 * d + 32, 4 + c // 4, (c % 4) * P:(c % 4) * P + n],
                                            AAT[0:n, c, 32 * d:32 * d + 32], tri[0:n, 0:n], start=True, stop=True)
            fill(last, "FR")

            def conf(u, part):
                arrived(("conf", u))
                proj((("ca", "cg")[part], u), slot(("conf", u), part), slice(0, P), ("conf", u))

            def turn(g, t):
                src = CO[:, (6 * g + t) % 2, :] if t != 2 else BF[:, :]
                pe.wait_ge(S("conv_ready"), 6 * g + t + 1)
                open_(("tr", g, t), 4, 5)
                for c, (t0, n) in enumerate(CHUNKS):
                    last = nc.tensor.transpose(PS[0:n, 4 + c // 4, (c % 4) * P:(c % 4) * P + P], src[:, t0:t0 + n], ident)
                fill(last, ("tr", g, t))

            def turn_y(g, c):
                n = CHUNKS[c][1]
                pe.wait_ge(*freed(("yd", g, c)))
                open_(("yt", g, c), 5)
                for j in range(4):
                    last = nc.tensor.transpose(PS[:, 5, j * P:j * P + n], YC[0:n, j * P:j * P + P], ident[0:n, 0:n])
                fill(last, ("yt", g, c))

            for g in range(GROUPS):
                tiles = [(i, j) for i in range(2) for j in range(3)]
                for t, (i, j) in enumerate(tiles):
                    if t >= 2 or (g > 0 and t == 1):
                        xbc(g, i, j)
                    if t >= 2:
                        turn(g, t - 2)
                turn(g, 4)
                pe.wait_ge(S("conv_ready"), 6 * g + 6)
                pe.wait_ge(*freed(("tr", g, 2)))
                pe.wait_ge(*freed(("tr", g, 4)))
                for s, c in enumerate(range(NC - 1, 0, -1)):
                    t0, n = CHUNKS[c]
                    pe.wait_ge(S("xwb_ready"), 4 * g + s + 1)
                    open_(("sb", g, c), 6)
                    fill(nc.tensor.matmul(PS[:, 6, :], BT[0:n, c, :], XW[0:n, s % 2, :], start=True, stop=True),
                         ("sb", g, c))
                    name = ("z", g, s // 2)
                    arrived(name)
                    proj(("zt", 4 * g + s), slot(name), slice((s % 2) * P, (s % 2) * P + P), name)
                for c, (t0, n) in enumerate(CHUNKS):
                    if c == 0:
                        open_(("cb", g, 0), 4)
                        fill(nc.tensor.matmul(PS[0:n, 4, 0:n], BF[:, 0:n], CF[:, 0:n], start=True, stop=True), ("cb", g, 0))
                    if c < 4:
                        conf(2 * g + c // 2, c % 2)
                    elif g < GROUPS - 1:
                        xbc(g + 1, 0, 0)
                    if c > 0:
                        turn_y(g, c - 1)
                    if c < 4:
                        pe.wait_ge(*freed(("sb", g, c + 1)))
                        open_(("ob", g, c), 7)
                        fill(nc.tensor.matmul(PS[0:n, 7, :], CF[:, t0:t0 + n], SNAP[:, c, :], start=True, stop=True),
                             ("ob", g, c))
                    if c > 0:
                        pe.wait_ge(*freed(("sf", g, c - 1)))
                        open_(("of", g, c), 6)
                        fill(nc.tensor.matmul(PS[0:n, 6, :], CF[:, t0:t0 + n], ST[:, (c - 1) % 2, :], start=True, stop=True),
                             ("of", g, c))
                    pe.wait_ge(S("m_ready"), NC * g + c + 1)
                    open_(("yd", g, c), 5)
                    for h in range(GH):
                        last = nc.tensor.matmul(PS[0:n, 5, h * HD:h * HD + HD], M1[0:n, h, 0:n],
                                                XS[0:n, c, h * HD:h * HD + HD], start=True, stop=True)
                    fill(last, ("yd", g, c))
                    if c < 4:
                        pe.wait_ge(S("xwf_ready"), 4 * g + c + 1)
                        open_(("sf", g, c), 6)
                        fill(nc.tensor.matmul(PS[:, 6, :], BT[0:n, c, :], XW[0:n, c % 2, :], start=True, stop=True),
                             ("sf", g, c))
                        t1, n1 = CHUNKS[c + 1]
                        open_(("cb", g, c + 1), 4)
                        fill(nc.tensor.matmul(PS[0:n1, 4, 0:n1], BF[:, t1:t1 + n1], CF[:, t1:t1 + n1], start=True,
                                              stop=True), ("cb", g, c + 1))
                turn_y(g, NC - 1)
            triple = [0]

            def out_dense(kind, m, src, K, per):
                name = (kind, m // per)
                arrived(name)
                w = slot(name)
                n = triple[0] % 3
                triple[0] += 1
                dense((kind, m), (2 * n, 2 * n + 1), K, T2, lambda k: w[:, k, (m % per) * P:(m % per) * P + P],
                      lambda k: src[:, k, :], reads=name)

            norm_sum("ny", (6, 7))
            for m in range(4):
                out_dense("g1", m, U, DT, 4)
            pe.wait_ge(S("conf_tap"), DT * CONF_TAPS)
            open_("lnm", 6, 7)
            for k in range(DT):
                for i, (lo, hi) in enumerate(halves(T2)):
                    last = nc.tensor.matmul(PS[:, 6 + i, 0:HT], ones, CACC[:, k, lo:hi], start=(k == 0), stop=(k == DT - 1))
            fill(last, "lnm")
            for m in (4, 5):
                out_dense("g1", m, U, DT, 4)
            norm_sum("lnv", (6, 7))
            for m in (6, 7):
                out_dense("g1", m, U, DT, 4)
            pe.wait_ge(S("conf_ready"), DT)
            for m in range(DT):
                out_dense("co", m, CACC, DT, 4)
            pe.wait_ge(S("y_ready"), 16)
            for m in range(DT):
                out_dense("g2", m, U, DT, 2)
                out_dense("so", m, YT, 16, 2)
            pe.wait_ge(S("merged"), DT)
            for m in range(DT):
                out_dense("out", m, MG, DT, 4)
            norm_sum("n6", (6, 7))
            pe.wait_ge(S("u_ready"), u_base["n6"] + DT)
            open_("lg", 0)
            for c, (t0, n) in enumerate(CHUNKS):
                for k in range(DT):
                    r0 = PARAMS["router"] + k * EXPERTS
                    last = nc.tensor.matmul(PS[0:n, 0, c * EXPERTS:(c + 1) * EXPERTS], U[:, k, t0:t0 + n],
                                            par[:, r0:r0 + EXPERTS], start=(k == 0), stop=(k == DT - 1))
            fill(last, "lg")
            pe.wait_ge(S("aff_ready"), 2)
            open_("af", 4, 5)
            for c, (t0, n) in enumerate(CHUNKS):
                last = nc.tensor.transpose(PS[0:EXPERTS, 4 + c // 4, (c % 4) * P:(c % 4) * P + n], AFF[0:n, c, :],
                                           ident[0:n, 0:n])
            fill(last, "af")
            for c, (t0, n) in enumerate(CHUNKS):
                for hf in range(2):
                    b = 2 + (2 * c + hf) % 2
                    open_(("xn", c, hf), b)
                    for k in range(4):
                        last = nc.tensor.transpose(PS[0:n, b, k * P:k * P + P], U[:, 4 * hf + k, t0:t0 + n], ident)
                    fill(last, ("xn", c, hf))
            pe.wait_ge(S("slots_ready"), 1)
            open_("sl16", 0)
            for c, (t0, n) in enumerate(CHUNKS):
                last = nc.tensor.transpose(PS[0:n, 0, c * EXPERTS:(c + 1) * EXPERTS], TK[0:EXPERTS, 0, t0:t0 + n],
                                           ident[0:EXPERTS, 0:EXPERTS])
            fill(last, "sl16")
            for b in range(8):
                if last_tag[b] is not None:
                    pe.wait_ge(*freed(last_tag[b]))

            def gather(e, hf):
                if hf == 0:
                    pe.wait_ge(S("sel_ready"), e * NC + NC)
                for c, (t0, n) in enumerate(CHUNKS):
                    for part in range(2):
                        last = nc.tensor.matmul(PS[0:CAP, 6 + hf, :], SE[0:n, c, :], XNT[0:n, part, c, 512 * hf:512 * hf + 512],
                                                start=(c == 0 and part == 0), stop=(c == NC - 1 and part == 1))
                last.then_inc(S("x_gathered"), 1)

            def turn_x(e, hf):
                pe.wait_ge(S("xgs_ready"), e * 2 + hf + 1)
                for k in range(4):
                    last = nc.tensor.transpose(PS[:, 6 + hf, k * CAP:(k + 1) * CAP],
                                               XGS[0:CAP, (4 * hf + k) * P:(4 * hf + k + 1) * P], ident[0:CAP, 0:CAP])
                last.then_inc(S("x_turned"), 1)

            def turn_h(e, b):
                pe.wait_ge(S("hgs_ready"), e * 4 + b + 1)
                for k in range(4):
                    last = nc.tensor.transpose(PS[:, 6 + b % 2, k * CAP:(k + 1) * CAP], HGS[0:CAP, b % 2, k * P:k * P + P],
                                               ident[0:CAP, 0:CAP])
                last.then_inc(S("h_turned"), 1)

            def combine(e, m):
                pe.wait_ge(S("yel_ready"), e * 2 + m // 4 + 1)
                if m == 0:
                    pe.wait_ge(S("yel_ready"), e * 2 + 2)
                else:
                    pe.wait_ge(S("h_added"), e * DT + m)
                for i, (lo, hi) in enumerate(halves(T2)):
                    for part in range(2):
                        last = nc.tensor.matmul(PS[:, 4 + i, 0:HT], YE[0:CAP, part, m * P:m * P + P], SAT[0:CAP, lo:hi],
                                                start=(part == 0), stop=(part == 1))
                last.then_inc(S("combined"), 1)

            def turn_slots(e):
                pe.wait_ge(S("hgl_ready"), e * 4 + 3)
                for c, (t0, n) in enumerate(CHUNKS):
                    nc.tensor.transpose(PS[0:CAP, 6 + c // 4, (c % 4) * P:(c % 4) * P + n], SE[0:n, c, :].bitcast(F32),
                                        ident[0:n, 0:n])
                pe.wait_ge(S("aff_copied"), e * 2 + 2)
                for c, (t0, n) in enumerate(CHUNKS):
                    last = nc.tensor.matmul(PS[0:CAP, 7, 256:257], SE[0:n, c, :].bitcast(F32), small[0:n, 144 + c:145 + c],
                                            start=(c == 0), stop=(c == NC - 1))
                last.then_inc(S("sat_turned"), 1)

            def expert(e, first=False, last=False):
                for q in range(PIECES):
                    i, kk = q // 4, q % 4
                    if i < 8:
                        b, part = i // 2, i % 2
                        bank, stat, k0 = 2 * (b % 2) + part, XG, 2 * kk
                        if kk == 0 and not (first and b < 2):
                            pe.wait_ge(S(("gate_act", "hgs_ready")[part]), e * 4 + b - 1)
                        if q in (0, 2):
                            pe.wait_ge(S("xgl_ready"), e * 2 + q // 2 + 1)
                        start, stop = kk == 0, kk == 3
                    else:
                        kh, bank = (i - 8) // 2, 4 + i % 2
                        stat, k0 = HG, 8 * kh + 2 * kk
                        if i == 8 and kk == 0 and not first:
                            pe.wait_ge(S("h_added"), e * DT)
                        if i in (8, 10) and kk in (0, 2):
                            pe.wait_ge(S("hgl_ready"), e * 4 + 2 * kh + kk // 2 + 1)
                        start, stop = kh == 0 and kk == 0, kh == 1 and kk == 3
                    pe.wait_ge(S("wh_ready"), e * PIECES + q + 1)
                    for j in range(2):
                        k = k0 + j
                        w = WS[:, :, q % PBUF, 512 * j:512 * j + 512]
                        nc.tensor.matmul(PS[0:CAP, bank, :], stat[:, 0, k, :], w[:, 0, :], start=(start and j == 0), stop=False)
                        nc.tensor.matmul(PS[0:CAP, bank, :], stat[:, 1, k, :], w[:, 0, :], start=False, stop=False)
                    pe.wait_ge(S("wl_ready"), e * PIECES + q + 1)
                    for j in range(2):
                        mm = nc.tensor.matmul(PS[0:CAP, bank, :], stat[:, 0, k0 + j, :], WS[:, 1, q % PBUF, 512 * j:512 * j + 512],
                                              start=False, stop=(stop and j == 1))
                    mm.then_inc(S("w_used"), 1)
                    if not first and q in COMBINE_AT:
                        combine(e - 1, COMBINE_AT.index(q))
                    if q in TURN_H_AT:
                        b = TURN_H_AT.index(q)
                        if b == 3:
                            pe.wait_ge(S("sat_ready"), e * 3 + 3)
                        turn_h(e, b)
                    if q == SLOTS_AT:
                        turn_slots(e)
                    if not last and q in GATHER_AT:
                        hf = GATHER_AT.index(q)
                        if hf == 1:
                            pe.wait_ge(S("hgl_ready"), e * 4 + 4)
                        gather(e + 1, hf)
                    if not last and q in TURN_X_AT:
                        turn_x(e + 1, TURN_X_AT.index(q))

            pe.wait_ge(S("xnt_low"), 2 * NC)
            for hf in range(2):
                gather(0, hf)
            for hf in range(2):
                turn_x(0, hf)
            expert(0, first=True)
            with pe.Fori(1, EXPERTS - 1) as e:
                expert(e)
            expert(EXPERTS - 1, last=True)
            for m in range(DT):
                combine(EXPERTS - 1, m)
            pe.wait_ge(S("h_added"), EXPERTS * DT)
            for b in range(8):
                last_tag[b] = None
            norm_sum("n7", (6, 7))

        @blk.scalar
        def _(act):
            A = nc.scalar.activation
            link = chain(act, "act_chain")

            def squares(nm, src):
                _, K, T, *_ = NORM[nm]
                for k in range(K):
                    if k >= 2:
                        act.wait_ge(S("sq_used"), used_base[nm] + k - 1)
                    A(SQ[:, k % 2, 0:T], src(k), ACT.Square).then_inc(S("sq_ready"), 1)

            def root(nm, banks, R=RS):
                _, K, T, scale, eps, _ = NORM[nm]
                got(act, nm)
                free(A(tok(R[:, 0:T], T), ps(banks, T), ACT.Sqrt, bias=pcol(eps), scale=scale), nm)

            act.dma_start(H[:, :, :], inp["h_t"].rearrange("(k p) n -> p k n", p=P)).then_inc(S("h_in"), 16)
            act.wait_ge(S("consts_in"), 48)
            act.wait_ge(S("h_in"), 16)
            squares("n1", lambda k: H[:, k, META:T2])
            root("n1", (6,))
            got(act, "lam")
            free(A(small[:, 2:4], PS[:, 7, 0:2], ACT.Exp), "lam")
            def x_parts(base):
                for k in range(DT):
                    act.wait_ge(S("x_normed"), base + k + 1)
                    A(UX[:, 0, k, :], SQ[:, k % 2, 0:SEQ], ACT.Copy).then_inc(S("ux_high"), 1)

            def in_high(p):
                act.wait_ge(S(f"ring{slot_of[where['in', p // 4]]}"), landed["in", p // 4])
                if p >= IBUF:
                    act.wait_ge(*in_used[p - IBUF])
                A(in_split(0, p), in_raw(p), ACT.Copy).then_inc(S("iw_high"), 1)

            for p in range(IBUF):
                in_high(p)
            x_parts(0)
            for p in range(24):
                b, m = divmod(p, 4)
                if IN_KINDS[b] != "v":
                    got(act, ("in", b, m))
                    at = {0: 0, 1: 4, 3: 8, 4: 12}[b] + m
                    free(A(QK[:, at, :], PS[:, m, :], ACT.Copy, scale=HD ** -0.5 if b == 0 else 1.0), ("in", b, m))
                if p + IBUF < 24:
                    in_high(p + IBUF)

            def rope_root(j):
                got(act, ("rn", j))
                free(A(MIX[:, j, :], PS[:, bank(("rn", j)), :], ACT.Sqrt, bias=pcol("eps"), scale=1.0 / HD), ("rn", j))

            act.wait_ge(S("ux_low"), DT)
            for j in range(8):
                act.wait_ge(*freed(("in", 3 + j // 4, j % 4)))
                if j >= 2:
                    got(act, ("rn", j - 2))
                A(SQ[:, j % 2, 0:SEQ], QK[:, 8 + j, :], ACT.Square).then_inc(S("rope_sq"), 1)
                if j >= 1:
                    rope_root(j - 1)
            rope_root(7)
            nc.scalar.preload_act_table_set("natural_log_exp_and_others")
            for i in range(SB_HEADS + 1):
                if i < SB_HEADS:
                    got(act, ("z", i))
                    if i >= 3:
                        got(act, ("o", i - 3))
                    free(A(Z[:, i % 3, :], PS[:, 0:3, :].rearrange("p a n -> p (a n)")[:, 0:1280], ACT.Copy), ("z", i))
                    act.wait_ge(*freed(("z", i)))
                    if i >= 2:
                        got(act, ("c", i - 2))
                    link(A(SP[:, i % 2, :], Z[:, i % 3, :], ACT.Abs))
                    link(A(SP[:, i % 2, :], SP[:, i % 2, :], ACT.Exp, scale=-1.0))
                    A(SP[:, i % 2, :], SP[:, i % 2, :], ACT.Ln, bias=pcol("one")).then_inc(S("ln_ready"), 1)
                if i >= 1:
                    act.wait_ge(S("arg_masked"), i)
                    A(Z[:, (i - 1) % 3, :], Z[:, (i - 1) % 3, :], ACT.Exp).then_inc(S("w_ready"), 1)
            for n in range(DIFF_HEADS * QB + 2):
                if n < DIFF_HEADS * QB:
                    qb, b0 = n % QB, 2 * (n % 2)
                    act.wait_ge(S("diff_max"), n + 1)
                    if n == 0:
                        got(act, ("o", SB_HEADS - 1))
                    if n >= 2:
                        act.wait_ge(S("diff_map"), n - 1)
                    for c in range(2):
                        ins = A(PR[:, n % 2, c, 0:(qb + 1) * P], PS[:, b0 + c, 0:(qb + 1) * P], ACT.Exp,
                                bias=small[:, 16 + 2 * (n % 2) + c:17 + 2 * (n % 2) + c], scale=HD ** -0.5,
                                accum_out=small[:, 24 + 2 * (n % 2) + c:25 + 2 * (n % 2) + c])
                        if c == 0:
                            ins.then_inc(S("diff_exp0"), 1)
                    free(ins, ("s", n))
                if n >= 2:
                    m = n - 2
                    got(act, ("at", m))
                    if m >= 2 and (m - 2) % QB == QB - 1:
                        got(act, ("do", (m - 2) // QB))
                    elif m >= 2:
                        act.wait_ge(S("diff_o"), (QB - 1) * ((m - 2) // QB) + (m - 2) % QB + 1)
                    free(A(DAT[:, m % 2, 0:(m % QB + 1) * P], PS[:, 4 + m % 2, 0:(m % QB + 1) * P], ACT.Copy), ("at", m))
            def subln_root(h):
                got(act, ("sl", h))
                free(A(QK[:, h, :], PS[:, bank(("sl", h)), :], ACT.Sqrt, bias=pcol("subln_eps"), scale=1.0 / P), ("sl", h))

            for h in range(DIFF_HEADS):
                act.wait_ge(*freed(("do", h)))
                if h >= 2:
                    got(act, ("sl", h - 2))
                A(SQ[:, h % 2, 0:SEQ], MIX[:, 4 + h, :], ACT.Square).then_inc(S("subln_sq"), 1)
                if h >= 1:
                    subln_root(h - 1)
            subln_root(DIFF_HEADS - 1)
            for m in range(DT):
                act.wait_ge(*freed(("wo", m)))
                if m >= 2:
                    act.wait_ge(S("sq_used"), used_base["n2"] + m - 1)
                A(SQ[:, m % 2, 0:SEQ], H[:, m, META:T2], ACT.Square).then_inc(S("sq_ready"), 1)
            root("n2", (6,))
            def ffn_high(p):
                name = pieces[p][0]
                act.wait_ge(S(f"ring{slot_of[where[name]]}"), landed[name])
                if p >= FBUF:
                    act.wait_ge(*piece_used[p - FBUF])
                A(split(0, p), raw(p), ACT.Copy).then_inc(S("fw_high"), 1)

            def hidden_high(m):
                act.wait_ge(*freed(("up", m)))
                A(GX[:, 0, m, :], RS[:, 0:SEQ], ACT.Copy).then_inc(S("gx_high"), 1)

            act.wait_ge(*freed(("wo", DT - 1)))
            for p in range(FBUF):
                ffn_high(p)
            x_parts(DT)
            for m in range(FFT):
                got(act, ("ga", m))
                if m >= 2:
                    act.wait_ge(*freed(("up", m - 2)))
                else:
                    act.wait_ge(S("ux_low"), 2 * DT)
                free(A(SQ[:, m % 2, 0:SEQ], PS[:, 2 * (m % 3), :], ACT.Silu), ("ga", m))
                ffn_high(2 * m + 3)
                if m >= 1:
                    hidden_high(m - 1)
                ffn_high(2 * m + 4)
            hidden_high(FFT - 1)
            for p in range(2 * FFT + 3, len(pieces)):
                ffn_high(p)
            for m in range(DT):
                act.wait_ge(*freed(("dn", m)))
                if m >= 2:
                    act.wait_ge(S("sq_used"), used_base["n3"] + m - 1)
                A(SQ[:, m % 2, :], H[:, m, :], ACT.Square).then_inc(S("sq_ready"), 1)
            root("n3", (6, 7))
            got(act, "dt")
            free(A(tok(DTF[0:64, 1, :], T2), PS[0:64, 6:8, 0:HT], ACT.Identity, bias=par[0:64, PARAMS["dt_bias"]:PARAMS["dt_bias"] + 1]), "dt")
            act.wait_ge(*freed("dt"))
            nc.scalar.preload_act_table_set("natural_log_exp_and_others")
            link(A(DTF[0:64, 2, :], DTF[0:64, 1, :], ACT.Abs))
            link(A(DTF[0:64, 2, :], DTF[0:64, 2, :], ACT.Exp, scale=-1.0))
            A(small[0:64, 32:33], par[0:64, PARAMS["a_log"]:PARAMS["a_log"] + 1], ACT.Exp).then_inc(S("dt_parts"), 1)
            A(DTF[0:64, 2, :], DTF[0:64, 2, :], ACT.Ln, bias=par[0:64, PARAMS["one"]:PARAMS["one"] + 1]).then_inc(S("dt_parts"), 1)
            def conv_tile(g, t):
                got(act, ("xb", g, t))
                i = 6 * g + t
                if i >= 2:
                    act.wait_ge(S("conv_done"), i - 1)
                b = bank(("xb", g, t))
                free(A(tok(XP[:, i % 2, 3:3 + T2], T2), PS[:, b:b + 2, 0:HT], ACT.Copy), ("xb", g, t))

            conv_tile(0, 0)
            conv_tile(0, 1)
            got(act, "FR")
            link(A(DTF[0:64, 3, 0:512], PS[0:64, 4, :], ACT.Copy))
            free(A(DTF[0:64, 3, 512:T2], PS[0:64, 5, 0:META], ACT.Copy), "FR")
            act.wait_ge(*freed("FR"))
            act.dma_start(fr_dram, DTF[0:64, 3, :]).then_inc(S("fr_out"), 16)
            act.wait_ge(S("w2_arg"), 2)
            for i, (n, cs) in enumerate(((P, slice(0, 4)), (META, slice(4, 5)))):
                A(EF[0:n, cs, :], FT[0:n, cs, :], ACT.Exp).then_inc(S("ssd_exp"), 1)
                A(W2[0:n, cs, :], W2[0:n, cs, :], ACT.Exp).then_inc(S("ssd_exp"), 1)
            A(ET[:, :, :], ET[:, :, :], ACT.Exp).then_inc(S("ssd_exp"), 1)
            act.wait_ge(S("fr_out"), 16)

            def fr_load(g, c):
                i = NC * g + c
                t0, n = CHUNKS[c]
                if i >= 2:
                    act.wait_ge(S("m_ready"), i - 1)
                for d in range(2):
                    src = fr_dram[32 * d + GH * g:32 * d + GH * (g + 1), t0:t0 + n]
                    act.dma_start(FR[i % 2][d][:, :, 0:n], src.partition_broadcast(P)).then_inc(S(f"fr_in{i % 2}"), 16)

            def conv_silu(g, t):
                i = 6 * g + t
                act.wait_ge(S("conv_done"), i + 1)
                j = 16 + (0 if t == 2 else 4) + g if t in (2, 5) else 4 * g + (t if t < 2 else t - 1)
                co = CO[:, (6 * g + t) % 2, :]
                if t in (2, 5):
                    if g > 0:
                        got(act, ("of", g - 1, NC - 1))
                        act.wait_ge(S("m_ready"), NC * g)
                    ins = A(BF if t == 2 else CF, CO[:, (6 * g + t) % 2, :], ACT.Silu, bias=pcol("ssm_b", j))
                else:
                    ins = A(co, co, ACT.Silu, bias=pcol("ssm_b", j))
                ins.then_inc(S("conv_ready"), 1)

            def take_turned(g, t):
                tag = ("tr", g, t)
                got(act, tag)
                if g > 0:
                    got(act, ("yt", g - 1, NC - 1))
                dst = BT if t == 2 else XS[:, :, XS_AT[t] * P:XS_AT[t] * P + P]
                link(A(dst[:, 0:4, :], PS[:, 4, :].rearrange("p (c n) -> p c n", c=4), ACT.Copy))
                free(A(dst[0:META, 4, :], PS[0:META, 5, 0:P], ACT.Copy), tag)

            XS_AT = {0: 0, 1: 1, 3: 2, 4: 3}
            for g in range(GROUPS):
                for t in range(6):
                    if g > 0 or t >= 2:
                        conv_tile(g, t)
                    if t >= 1:
                        conv_silu(g, t - 1)
                    if t >= 3:
                        take_turned(g, t - 3)
                conv_silu(g, 5)
                take_turned(g, 3)
                take_turned(g, 4)
                fr_load(g, 0)
                fr_load(g, 1)
                for s in range(4):
                    tag = ("zt", 4 * g + s)
                    got(act, tag)
                    b = bank(tag)
                    free(A(tok(YT[:, 4 * g + s, :], T2), PS[:, b:b + 2, 0:HT], ACT.Silu), tag)
                for c, (t0, n) in enumerate(CHUNKS):
                    i = NC * g + c
                    act.wait_ge(S("min_ready"), i + 1)
                    A(FR[i % 2][0][0:n, :, 0:n], FR[i % 2][0][0:n, :, 0:n], ACT.Exp).then_inc(S("e_ready"), 1)
                    if c % 2 == 1:
                        u = 2 * g + c // 2
                        got(act, ("cg", u))
                        if u >= 1:
                            act.wait_ge(*freed(("ca", u - 1)))
                        b = bank(("cg", u))
                        free(A(tok(SGB[:, :], T2), PS[:, b:b + 2, 0:HT], ACT.Sigmoid), ("cg", u))
                    if c + 2 < NC:
                        fr_load(g, c + 2)
            act.wait_ge(*freed(("yt", GROUPS - 1, NC - 1)))
            squares("ny", lambda k: YT[:, k, :])
            root("ny", (6, 7), GT[:, 1, :])

            def first_gate(m):
                got(act, ("g1", m))
                b = bank(("g1", m))
                free(A(tok(MG[:, m, :], T2), PS[:, b:b + 2, 0:HT], ACT.Sigmoid), ("g1", m))

            for m in range(4):
                first_gate(m)
            for k in range(DT):
                act.wait_ge(S("ln_centred"), k + 1)
                if k >= 2:
                    act.wait_ge(S("sq_used"), used_base["lnv"] + k - 1)
                A(SQ[:, k % 2, :], CACC[:, k, :], ACT.Square).then_inc(S("sq_ready"), 1)
            root("lnv", (6, 7))
            for m in (4, 5):
                first_gate(m)
            for k in range(DT):
                act.wait_ge(S("ln_scaled"), k + 1)
                A(CACC[:, k, :], CACC[:, k, :], ACT.Silu, bias=pcol("ln_b", k)).then_inc(S("conf_ready"), 1)
            for m in (6, 7):
                first_gate(m)
            for m in range(DT):
                got(act, ("g2", m))
                if m == 0:
                    act.wait_ge(S("y_ready"), 16)
                if m >= 2:
                    act.wait_ge(S("merged"), m - 1)
                else:
                    act.wait_ge(*freed(("co", DT - 1)))
                b = bank(("g2", m))
                free(A(tok(GT[:, m % 2, :], T2), PS[:, b:b + 2, 0:HT], ACT.Sigmoid), ("g2", m))
            for m in range(DT):
                act.wait_ge(*freed(("out", m)))
                if m >= 2:
                    act.wait_ge(S("sq_used"), used_base["n6"] + m - 1)
                A(SQ[:, m % 2, :], H[:, m, :], ACT.Square).then_inc(S("sq_ready"), 1)
            root("n6", (6, 7))
            for c, (t0, n) in enumerate(CHUNKS):
                act.wait_ge(S("lg_max"), NC)
                ins = A(AFF[0:n, c, :], PS[0:n, 0, c * EXPERTS:(c + 1) * EXPERTS], ACT.Exp,
                        bias=small[0:n, 48 + c:49 + c], accum_out=small[0:n, 56 + c:57 + c])
                if c < NC - 1:
                    ins.then_inc(S("aff_exp"), 1)
            free(ins, "lg")
            for c, (t0, n) in enumerate(CHUNKS):
                for hf in range(2):
                    got(act, ("xn", c, hf))
                    A(XNT[0:n, 0, c, 512 * hf:512 * hf + 512], PS[0:n, 2 + hf, :], ACT.Copy).then_inc(S("xnt_high"), 1)
                    if c > 0:
                        act.wait_ge(S("xnt_low"), 2 * c + hf - 1)
                    free(A(XGS[0:n, 512 * hf:512 * hf + 512], PS[0:n, 2 + hf, :], ACT.Copy), ("xn", c, hf))
            nc.scalar.preload_act_table_set("silu_and_others")

            def x_rows(e, hf):
                act.wait_ge(S("x_gathered"), e * 2 + hf + 1)
                A(XGS[0:CAP, 512 * hf:512 * hf + 512], PS[0:CAP, 6 + hf, :], ACT.Copy).then_inc(S("xgs_ready"), 1)

            def x_high(e, hf):
                act.wait_ge(S("x_turned"), e * 2 + hf + 1)
                A(XG[:, 0, 4 * hf:4 * hf + 4, :], PS[:, 6 + hf, 0:4 * CAP].rearrange("p (k n) -> p k n", k=4),
                  ACT.Copy).then_inc(S("xgh_ready"), 1)

            def y_high(e, hf):
                act.wait_ge(S("w_used"), e * PIECES + 44 + 4 * hf)
                act.wait_ge(S("sat_ready"), e * 3 + 3)
                A(YE[0:CAP, 0, 512 * hf:512 * hf + 512], PS[0:CAP, 4 + hf, :], ACT.Copy, scale=AFS[0:CAP])\
                    .then_inc(S("yeh_ready"), 1)

            def expert(e, first=False, last=False):
                for q in range(PIECES):
                    i, kk = q // 4, q % 4
                    if kk == 0:
                        landed_e(act, e, i)
                    if first and q < PBUF:
                        if q == 0:
                            act.wait_ge(S("sel_ready"), NC)
                    else:
                        act.wait_ge(S("w_used"), e * PIECES + q - PBUF + 1)
                    at = q - PBUF
                    if at == -1 and not first:
                        y_high(e - 1, 1)
                    if at >= 0 and at < 32 and at % 8 == 3:
                        b = at // 8
                        if not (first and b < 2):
                            act.wait_ge(S("hgs_ready"), e * 4 + b - 1)
                        A(SIL[0:CAP, b % 2, :], PS[0:CAP, 2 * (b % 2), :], ACT.Silu).then_inc(S("gate_act"), 1)
                    if at in TURN_H_AT:
                        b = TURN_H_AT.index(at)
                        act.wait_ge(S("h_turned"), e * 4 + b + 1)
                        A(HG[:, 0, 4 * b:4 * b + 4, :], PS[:, 6 + b % 2, 0:4 * CAP].rearrange("p (k n) -> p k n", k=4),
                          ACT.Copy).then_inc(S("hgh_ready"), 1)
                    if at in GATHER_AT and not last:
                        x_rows(e + 1, GATHER_AT.index(at))
                    if at in TURN_X_AT and not last:
                        x_high(e + 1, TURN_X_AT.index(at))
                    if at == 43:
                        y_high(e, 0)
                    A(WS[:, 0, q % PBUF, :], ring[:, (EXP0 + i) % RING, PIECE * kk:PIECE * (kk + 1)], ACT.Copy)\
                        .then_inc(S("wh_ready"), 1)

            for hf in range(2):
                x_rows(0, hf)
            for hf in range(2):
                x_high(0, hf)
            expert(0, first=True)
            with act.Fori(1, EXPERTS - 1) as e:
                expert(e)
            expert(EXPERTS - 1, last=True)
            y_high(EXPERTS - 1, 1)
            act.wait_ge(S("h_added"), EXPERTS * DT)
            squares("n7", lambda k: H[:, k, :])
            root("n7", (6, 7))

        @blk.vector
        def _(dve):
            V_ = nc.vector
            link = chain(dve, "dve_chain")
            MUL, ADD, SUB = ALU.mult, ALU.add, ALU.subtract

            def norm_apply(nm, src, dst, sem, R=RS):
                _, K, T, _, _, gain = NORM[nm]
                dve.wait_ge(*freed(nm))
                link(V_.reciprocal(R[:, 0:T], R[:, 0:T]))
                for k in range(K):
                    V_.scalar_tensor_tensor(dst(k), src(k), pcol(gain, k), R[:, 0:T], MUL, MUL).then_inc(S(sem), 1)

            dve.wait_ge(S("consts_in"), 48)
            l0 = PARAMS["lam"]
            V_.tensor_tensor(small[0:HD, 0:2], par[0:HD, l0:l0 + 4:2], par[0:HD, l0 + 1:l0 + 4:2], MUL).then_inc(S("lam_prod"), 1)

            def in_low(p):
                dve.wait_ge(S("iw_high"), p + 1)
                V_.tensor_tensor(in_split(1, p), in_raw(p), in_split(0, p).bitcast(F32), SUB).then_inc(S("iw_low"), 1)

            def norm_split(nm, base):
                gain = NORM[nm][5]
                dve.wait_ge(*freed(nm))
                link(V_.reciprocal(RS[:, 0:SEQ], RS[:, 0:SEQ]))
                for k in range(DT + 1):
                    if k < DT:
                        V_.scalar_tensor_tensor(SQ[:, k % 2, 0:SEQ], H[:, k, META:T2], pcol(gain, k), RS[:, 0:SEQ], MUL, MUL)\
                            .then_inc(S("x_normed"), 1)
                    if k >= 1:
                        dve.wait_ge(S("ux_high"), base + k)
                        V_.tensor_tensor(UX[:, 1, k - 1, :], SQ[:, (k - 1) % 2, 0:SEQ], UX[:, 0, k - 1, :].bitcast(F32), SUB)\
                            .then_inc(S("ux_low"), 1)
                        dve.wait_ge(S("ux_low"), base + k)

            norm_split("n1", 0)
            for p in range(IBUF):
                in_low(p)
            dve.wait_ge(*freed("lam"))
            link(V_.tensor_tensor(small[:, 4:5], small[:, 3:4], small[:, 2:3], SUB))
            link(V_.tensor_scalar(small[:, 4:5], small[:, 4:5], LAMBDA_INIT, None, SUB))
            link(V_.tensor_scalar(small[:, 5:6], pcol("subln_g"), 1.0 - LAMBDA_INIT, None, MUL))
            for p in range(24):
                if p + IBUF < 24:
                    in_low(p + IBUF)
                if p in (11, 23):
                    for m in range(4):
                        tag = ("in", p // 4, m)
                        got(dve, tag)
                        free(V_.tensor_copy(V[:, m, 512 * (p // 12):512 * (p // 12) + 512], PS[:, m, :]), tag)
            def rope_norm(j):
                dve.wait_ge(*freed(("rn", j)))
                R = MIX[:, j, :]
                link(V_.reciprocal(R, R))
                gain = pcol("q_g") if j < 4 else pcol("k_g")
                V_.scalar_tensor_tensor(QK[:, 8 + j, :], QK[:, 8 + j, :], gain, R, MUL, MUL).then_inc(S("rope_normed"), 1)

            def stick_out(h):
                r0 = HD * (h % 2)
                got(dve, ("o", h))
                free(V_.tensor_copy(MIX[r0:r0 + HD, h // 2, :], PS[r0:r0 + HD, 6, :]), ("o", h))

            def diff_out(h):
                got(dve, ("do", h))
                free(V_.tensor_copy(MIX[:, 4 + h, :], PS[:, bank(("do", h)), :]), ("do", h))

            rope_norm(0)
            for i in range(SB_HEADS + 1):
                if i < SB_HEADS:
                    dve.wait_ge(S("ln_ready"), i + 1)
                    V_.scalar_tensor_tensor(SP[:, i % 2, :], Z[:, i % 3, :], 0.0, SP[:, i % 2, :], ALU.max, ADD)\
                        .then_inc(S("sp_ready"), 1)
                    got(dve, ("rot", i))
                    dve.wait_ge(S("cos_part"), i + 1)
                    RB = U[:, i % 2, 0:SEQ]
                    if i >= 2:
                        dve.wait_ge(S("rope_done"), i - 1)
                    free(V_.tensor_tensor(RB, PS[:, 7, :], SIN, MUL), ("rot", i))
                    dve.wait_ge(*freed(("rot", i)))
                    V_.tensor_tensor(QK[:, 8 + i, :], RB, U[:, 2 + i % 2, 0:SEQ], ADD).then_inc(S("rope_done"), 1)
                if i >= 1:
                    h = i - 1
                    got(dve, ("c", h))
                    free(V_.tensor_tensor(Z[:, h % 3, :], Z[:, h % 3, :],
                                          PS[:, 3:6, :].rearrange("p a n -> p (a n)")[:, 0:1280], SUB), ("c", h))
                if i + 1 < SB_HEADS:
                    rope_norm(i + 1)
                if i >= 2:
                    stick_out(i - 2)
            stick_out(SB_HEADS - 1)
            dve.wait_ge(S("rope_done"), 8)
            for n in range(DIFF_HEADS * QB + 1):
                if n < DIFF_HEADS * QB:
                    qb, b0 = n % QB, 2 * (n % 2)
                    N = (qb + 1) * P
                    got(dve, ("s", n))
                    link(V_.tensor_tensor(PS[:, b0:b0 + 2, qb * P:N], PS[:, b0:b0 + 2, qb * P:N],
                                          causal.unsqueeze(1).to_broadcast([P, 2, P]), ADD))
                    link(V_.tensor_reduce(small[:, 8:10], PS[:, b0:b0 + 2, 0:N], AX_X, ALU.max))
                    V_.tensor_scalar(small[:, 16 + 2 * (n % 2):18 + 2 * (n % 2)], small[:, 8:10], -HD ** -0.5, None, MUL)\
                        .then_inc(S("diff_max"), 1)
                    dve.wait_ge(S("diff_max"), n + 1)
                if n >= 1:
                    m = n - 1
                    N = (m % QB + 1) * P
                    s0 = 24 + 2 * (m % 2)
                    dve.wait_ge(*freed(("s", m)))
                    dve.wait_ge(S("diff_exp0"), m + 1)
                    link(V_.reciprocal(small[:, s0:s0 + 2], small[:, s0:s0 + 2]))
                    link(V_.tensor_tensor(small[:, s0 + 1:s0 + 2], small[:, s0 + 1:s0 + 2], small[:, 4:5], MUL))
                    link(V_.tensor_scalar(DA2[:, m % 2, 0:N], PR[:, m % 2, 1, 0:N], small[:, s0 + 1:s0 + 2], None, MUL))
                    if m >= 2:
                        got(dve, ("at", m - 2))
                    V_.scalar_tensor_tensor(DA[:, m % 2, 0:N], PR[:, m % 2, 0, 0:N], small[:, s0:s0 + 1],
                                            DA2[:, m % 2, 0:N], MUL, ADD).then_inc(S("diff_map"), 1)
                    dve.wait_ge(S("diff_map"), m + 1)
                if n >= QB + 3 and (n - 3) % QB == 0:
                    diff_out((n - 3) // QB - 1)
            diff_out(DIFF_HEADS - 1)
            for h in range(DIFF_HEADS):
                dve.wait_ge(*freed(("sl", h)))
                R = QK[:, h, :]
                link(V_.reciprocal(R, R))
                V_.scalar_tensor_tensor(MIX[:, 4 + h, :], MIX[:, 4 + h, :], small[:, 5:6], R, MUL, MUL).then_inc(S("mix_ready"), 1)
            for m in range(DT):
                got(dve, ("wo", m))
                free(V_.tensor_tensor(H[:, m, META:T2], H[:, m, META:T2], PS[:, m % 4, :], ADD), ("wo", m))
            def ffn_low(p):
                dve.wait_ge(S("fw_high"), p + 1)
                V_.tensor_tensor(split(1, p), raw(p), split(0, p).bitcast(F32), SUB).then_inc(S("fw_low"), 1)

            def hidden_low(m):
                dve.wait_ge(S("gx_high"), m + 1)
                V_.tensor_tensor(GX[:, 1, m, :], RS[:, 0:SEQ], GX[:, 0, m, :].bitcast(F32), SUB).then_inc(S("gx_low"), 1)

            for p in range(FBUF):
                ffn_low(p)
            norm_split("n2", DT)
            for m in range(FFT):
                ffn_low(2 * m + 3)
                got(dve, ("up", m))
                dve.wait_ge(*freed(("ga", m)))
                if m >= 1:
                    dve.wait_ge(S("gx_low"), m)
                free(V_.tensor_tensor(RS[:, 0:SEQ], SQ[:, m % 2, 0:SEQ], PS[:, 2 * (m % 3) + 1, :], MUL), ("up", m))
                ffn_low(2 * m + 4)
                hidden_low(m)
            for m in range(DT):
                for p in range(2 * FFT + (3 if m == 0 else 4 * m + 8), min(2 * FFT + 4 * m + 12, len(pieces))):
                    ffn_low(p)
                got(dve, ("dn", m))
                b = 2 * ((m // 2) % 3) + m % 2
                free(V_.tensor_tensor(H[:, m, META:T2], H[:, m, META:T2], PS[:, b, :], ADD), ("dn", m))
            norm_apply("n3", lambda k: H[:, k, :], lambda k: U[:, k, :], "u_ready")
            for v in (XP[:, :, 0:3], XP[:, :, 3 + T2:6 + T2], CP[:, :, 0:15], CP[:, :, 15 + T2:30 + T2]):
                V_.memset(v, 0.0).then_inc(S("pads"), 1)
            dve.wait_ge(S("dt_parts"), 2)
            V_.scalar_tensor_tensor(DTF[0:64, 0, :], DTF[0:64, 1, :], 0.0, DTF[0:64, 2, :], ALU.max, ADD).then_inc(S("dt_done"), 1)
            dve.wait_ge(S("dt_done"), 1)
            V_.tensor_scalar(DTF[0:64, 5, :], DTF[0:64, 0, :], small[0:64, 32:33], -1.0, MUL, MUL).then_inc(S("dt_done"), 1)
            for part, dst in enumerate((DTT, AAT)):
                got(dve, ("dtT", part))
                link(V_.tensor_copy(dst[:, 0:4, :], PS[:, 4 + part, 0:256].rearrange("p (c n) -> p c n", c=4)))
                free(V_.tensor_copy(dst[0:META, 4, :], PS[0:META, 4 + part, 256:320]), ("dtT", part))
            dve.wait_ge(*freed(("dtT", 1)))
            got(dve, "F")
            got(dve, "TOT")
            free(V_.tensor_copy(ET[:, :, :], PS[:, 7, 0:320].rearrange("p (c n) -> p c n", c=NC)), "TOT")
            dve.wait_ge(*freed("TOT"))
            for n, cs in ((P, slice(0, 4)), (META, slice(4, 5))):
                lo, hi = cs.start * 64, cs.stop * 64
                k = cs.stop - cs.start
                ins = V_.tensor_copy(FT[0:n, cs, :], PS[0:n, 6, lo:hi].rearrange("p (c n) -> p c n", c=k))
                if n == P:
                    link(ins)
                else:
                    free(ins, "F")
                    dve.wait_ge(*freed("F"))
                ins = V_.tensor_tensor(W2[0:n, cs, :], ET[0:n, cs, :], FT[0:n, cs, :], SUB)
                ins.then_inc(S("w2_arg"), 1)
            dve.wait_ge(S("ssd_exp"), 5)
            link(V_.tensor_tensor(W2[:, 0:4, :], W2[:, 0:4, :], DTT[:, 0:4, :], MUL))
            V_.tensor_tensor(W2[0:META, 4, :], W2[0:META, 4, :], DTT[0:META, 4, :], MUL).then_inc(S("w2_ready"), 1)
            dve.wait_ge(S("w2_ready"), 1)
            dve.wait_ge(S("pads"), 4)

            def bc(ap, n, w):
                return ap.unsqueeze(2).to_broadcast([n, GH, w])

            def gate_y(g, c):
                t0, n = CHUNKS[c]
                got(dve, ("yt", g, c))
                if c == 0:
                    dve.wait_ge(*freed(("zt", 4 * g + 3)))
                yv = YT[:, 4 * g:4 * g + 4, t0:t0 + n]
                free(V_.tensor_tensor(yv, yv, PS[:, 5, :].rearrange("p (j n) -> p j n", j=4)[:, :, 0:n], MUL), ("yt", g, c))
                dve.wait_ge(*freed(("yt", g, c)))

            tap = [0]

            def conf_taps(upto):
                while tap[0] < upto:
                    pair, at = divmod(tap[0], 2 * CONF_TAPS)
                    u, j = 2 * pair + at % 2, at // 2
                    w0 = PARAMS["conf_w"] + u * CONF_TAPS
                    acc = CACC[:, u, :]
                    if tap[0] == 0:
                        dve.wait_ge(S("h_saved"), 16)
                    if j == 0:
                        dve.wait_ge(*freed(("ca", u)))
                        ins = V_.tensor_scalar(acc, CP[:, u % 2, 0:T2], par[:, w0:w0 + 1], pcol("conf_b", u), MUL, ADD)
                    else:
                        dve.wait_ge(S("conf_tap"), tap[0] - 1)
                        ins = V_.scalar_tensor_tensor(acc, CP[:, u % 2, j:j + T2], par[:, w0 + j:w0 + j + 1], acc, MUL, ADD)
                    ins.then_inc(S("conf_tap"), 1)
                    tap[0] += 1

            def some_taps(n, tiles):
                conf_taps(min(tap[0] + n, tiles * CONF_TAPS))

            for g in range(GROUPS):
                h8 = slice(GH * g, GH * g + GH)
                h8b = slice(32 + GH * g, 32 + GH * g + GH)
                for t in range(6):
                    i = 6 * g + t
                    dve.wait_ge(*freed(("xb", g, t)))
                    j = 16 + (0 if t == 2 else 4) + g if t in (2, 5) else 4 * g + (t if t < 2 else t - 1)
                    if i >= 2:
                        g2, t2 = divmod(i - 2, 6)
                        if t2 in (2, 5):
                            dve.wait_ge(S("conv_ready"), i - 1)
                        else:
                            got(dve, ("tr", g2, t2))
                    w0 = PARAMS["ssm_w"] + j * SSM_TAPS
                    co, xp = CO[:, i % 2, :], XP[:, i % 2, :]
                    for k in range(SSM_TAPS):
                        if k == 0:
                            ins = V_.tensor_scalar(co, xp[:, 0:T2], par[:, w0:w0 + 1], None, MUL)
                        else:
                            dve.wait_ge(S("conv_tap"), (SSM_TAPS - 1) * i + k)
                            ins = V_.scalar_tensor_tensor(co, xp[:, k:k + T2], par[:, w0 + k:w0 + k + 1], co, MUL, ADD)
                        ins.then_inc(S("conv_tap" if k < SSM_TAPS - 1 else "conv_done"), 1)
                        if k < 4:
                            some_taps(1, 2 * g)
                for s, c in enumerate(range(NC - 1, 0, -1)):
                    t0, n = CHUNKS[c]
                    got(dve, ("sb", g, c))
                    dst = SNAP[:, c - 1, :]
                    if g > 0 and s == 0:
                        got(dve, ("ob", g - 1, 3))
                    if c == NC - 1:
                        ins = V_.tensor_copy(dst, PS[:, 6, :])
                    else:
                        link(V_.tensor_tensor(dst.rearrange("p (h w) -> p h w", h=GH),
                                              SNAP[:, c, :].rearrange("p (h w) -> p h w", h=GH),
                                              bc(ET[:, c, h8b], P, HD), MUL))
                        ins = V_.tensor_tensor(dst, dst, PS[:, 6, :], ADD)
                    free(ins, ("sb", g, c))
                    dve.wait_ge(*freed(("sb", g, c)))
                    some_taps(10, 2 * g)
                for c, (t0, n) in enumerate(CHUNKS):
                    i = NC * g + c
                    F = FR[i % 2]
                    got(dve, ("cb", g, c))
                    link(V_.tensor_tensor(CBM[0:n, 0, 0:n], PS[0:n, 4, 0:n], upper[0:n, 0:n], MUL))
                    free(V_.tensor_tensor(CBM[0:n, 1, 0:n], PS[0:n, 4, 0:n], lower[0:n, 0:n], MUL), ("cb", g, c))
                    dve.wait_ge(S("fr_shifted"), 2 * i + 2)
                    V_.tensor_tensor(F[0][0:n, :, 0:n], F[0][0:n, :, 0:n], F[1][0:n, :, 0:n], ALU.min).then_inc(S("min_ready"), 1)
                    if i >= 1:
                        got(dve, ("yd", (i - 1) // NC, (i - 1) % NC))
                    link(V_.tensor_tensor(M1[0:n, :, 0:n], CBM[0:n, 0, 0:n].unsqueeze(1).to_broadcast([n, GH, n]),
                                          bc(DTT[0:n, c, h8], n, n), MUL))
                    dve.wait_ge(S("n1_ready"), i + 1)
                    V_.tensor_tensor(M1[0:n, :, 0:n], M1[0:n, :, 0:n], F[1][0:n, :, 0:n], ADD).then_inc(S("m_sum"), 1)
                    if c > 0:
                        gate_y(g, c - 1)
                    dve.wait_ge(S("xd_ready"), i + 1)
                    yc = YC[0:n, :]
                    yh = yc.rearrange("p (h w) -> p h w", h=GH)
                    if c > 0:
                        got(dve, ("of", g, c))
                        link(V_.tensor_tensor(yh, PS[0:n, 6, :].rearrange("p (h w) -> p h w", h=GH),
                                              bc(EF[0:n, c, h8], n, HD), MUL))
                        free(V_.tensor_tensor(yc, yc, XD[0:n, :], ADD), ("of", g, c))
                        dve.wait_ge(*freed(("of", g, c)))
                        base = yc
                    else:
                        base = XD[0:n, :]
                    if c < 4:
                        got(dve, ("ob", g, c))
                        tmp = YB[0:n, :]
                        free(V_.tensor_tensor(tmp.rearrange("p (h w) -> p h w", h=GH),
                                              PS[0:n, 7, :].rearrange("p (h w) -> p h w", h=GH),
                                              bc(EF[0:n, c, h8b], n, HD), MUL), ("ob", g, c))
                        dve.wait_ge(*freed(("ob", g, c)))
                        link(V_.tensor_tensor(yc, base, tmp, ADD))
                        base = yc
                    got(dve, ("yd", g, c))
                    free(V_.tensor_tensor(yc, base, PS[0:n, 5, :], ADD), ("yd", g, c))
                    if c < 4:
                        got(dve, ("sf", g, c))
                        st = ST[:, c % 2, :]
                        if c == 0:
                            ins = V_.tensor_copy(st, PS[:, 6, :])
                        else:
                            link(V_.tensor_tensor(st.rearrange("p (h w) -> p h w", h=GH),
                                                  ST[:, (c - 1) % 2, :].rearrange("p (h w) -> p h w", h=GH),
                                                  bc(ET[:, c, h8], P, HD), MUL))
                            ins = V_.tensor_tensor(st, st, PS[:, 6, :], ADD)
                        free(ins, ("sf", g, c))
                        dve.wait_ge(*freed(("sf", g, c)))
                    if c % 2 == 1:
                        u = 2 * g + c // 2
                        got(dve, ("ca", u))
                        dve.wait_ge(*freed(("cg", u)))
                        b = bank(("ca", u))
                        if u >= 2:
                            conf_taps((u // 2) * 2 * CONF_TAPS)
                            dve.wait_ge(S("conf_tap"), (u // 2) * 2 * CONF_TAPS)
                        free(V_.tensor_tensor(tok(CP[:, u % 2, 15:15 + T2], T2), tok(SGB[:, :], T2), PS[:, b:b + 2, 0:HT],
                                              MUL), ("ca", u))
                gate_y(g, NC - 1)
            conf_taps(DT * CONF_TAPS)
            got(dve, "lnm")
            mean = GT[:, 0, :]
            free(V_.tensor_scalar(tok(mean, T2), PS[:, 6:8, 0:HT], 1.0 / D, None, MUL), "lnm")
            dve.wait_ge(*freed("lnm"))
            for k in range(DT):
                V_.tensor_tensor(CACC[:, k, :], CACC[:, k, :], mean, SUB).then_inc(S("ln_centred"), 1)
            dve.wait_ge(S("ln_centred"), DT)
            norm_apply("lnv", lambda k: CACC[:, k, :], lambda k: CACC[:, k, :], "ln_scaled")
            norm_apply("ny", lambda k: YT[:, k, :], lambda k: YT[:, k, :], "y_ready", GT[:, 1, :])
            for m in range(DT):
                got(dve, ("co", m))
                dve.wait_ge(*freed(("g1", m)))
                b = bank(("co", m))
                free(V_.tensor_tensor(tok(MG[:, m, :], T2), tok(MG[:, m, :], T2), PS[:, b:b + 2, 0:HT], MUL), ("co", m))
            for m in range(DT):
                got(dve, ("so", m))
                dve.wait_ge(*freed(("g2", m)))
                b = bank(("so", m))
                free(V_.tensor_tensor(tok(GT[:, m % 2, :], T2), tok(GT[:, m % 2, :], T2), PS[:, b:b + 2, 0:HT], MUL),
                     ("so", m))
                dve.wait_ge(*freed(("so", m)))
                V_.tensor_tensor(MG[:, m, :], MG[:, m, :], GT[:, m % 2, :], ADD).then_inc(S("merged"), 1)
            dve.wait_ge(S("h_back"), 16)
            for m in range(DT):
                got(dve, ("out", m))
                b = bank(("out", m))
                free(V_.tensor_tensor(tok(H[:, m, :], T2), tok(H[:, m, :], T2), PS[:, b:b + 2, 0:HT], ADD), ("out", m))
            norm_apply("n6", lambda k: H[:, k, :], lambda k: U[:, k, :], "u_ready")
            got(dve, "lg")
            for c, (t0, n) in enumerate(CHUNKS):
                V_.tensor_reduce(small[0:n, 48 + c:49 + c], PS[0:n, 0, c * EXPERTS:(c + 1) * EXPERTS], AX_X, ALU.max,
                                 negate=True).then_inc(S("lg_max"), 1)
            dve.wait_ge(*freed("lg"))
            dve.wait_ge(S("aff_exp"), NC - 1)
            link(V_.reciprocal(small[:, 56:60], small[:, 56:60]))
            link(V_.reciprocal(small[0:META, 60:61], small[0:META, 60:61]))
            for n, cs in ((P, slice(0, 4)), (META, slice(4, 5))):
                k = cs.stop - cs.start
                V_.tensor_tensor(AFF[0:n, cs, :], AFF[0:n, cs, :],
                                 small[0:n, 56 + cs.start:56 + cs.stop].unsqueeze(2).to_broadcast([n, k, EXPERTS]),
                                 MUL).then_inc(S("aff_ready"), 1)
            E_ = EXPERTS
            TKR = [TK[0:E_, r, :] for r in range(8)]
            got(dve, "af")
            link(V_.tensor_copy(TKR[0][:, 0:512], PS[0:E_, 4, :]))
            free(V_.tensor_copy(TKR[0][:, 512:T2], PS[0:E_, 5, 0:META]), "af")
            dve.wait_ge(*freed("af"))
            src = TKR[0]
            for r in range(TOPK_ROUNDS):
                v8 = TV[0:E_, 8 * r:8 * r + 8]
                link(V_.max(v8, src))
                if r < TOPK_ROUNDS - 1:
                    link(V_.match_replace(TKR[1 + r % 2], v8, src, -1.0))
                    src = TKR[1 + r % 2]
            least = TV[0:E_, CAP - 1:CAP]
            link(V_.tensor_scalar(TKR[1], TKR[0], least, None, ALU.is_gt))
            link(V_.tensor_scalar(TKR[2], TKR[0], least, None, ALU.is_equal))
            link(V_.tensor_reduce(small[0:E_, 64:65], TKR[1], AX_X, ADD))
            link(V_.tensor_scalar(small[0:E_, 64:65], small[0:E_, 64:65], -1.0, float(CAP), MUL, ADD))
            link(V_.memset(TKR[5], 0.0))
            link(V_.tensor_tensor_scan(TKR[3], TKR[2], TKR[5], 0.0, ADD, ADD))
            link(V_.scalar_tensor_tensor(TKR[2], TKR[3], small[0:E_, 64:65], TKR[2], ALU.is_le, MUL))
            link(V_.tensor_tensor(TKR[1], TKR[1], TKR[2], ADD))
            link(V_.tensor_tensor_scan(TKR[3], TKR[1], TKR[5], 0.0, ADD, ADD))
            link(V_.tensor_tensor(TKR[3], TKR[3], TKR[1], MUL))
            V_.tensor_scalar(TKR[0], TKR[3], -1.0, None, ADD).then_inc(S("slots_ready"), 1)
            got(dve, "sl16")
            link(V_.tensor_copy(SLT[:, 0:4, :], PS[:, 0, 0:64].rearrange("p (c n) -> p c n", c=4)))
            free(V_.tensor_copy(SLT[0:META, 4, :], PS[0:META, 0, 64:80]), "sl16")
            dve.wait_ge(*freed("sl16"))
            def select(e):
                V_.tensor_copy(SLS[:, 0:4], SLT[:, 0:4, bass.ds(e, 1)].rearrange("p c n -> p (c n)")).then_inc(S("sel_cp"), 1)
                V_.tensor_copy(SLS[0:META, 4:5], SLT[0:META, 4, bass.ds(e, 1)]).then_inc(S("sel_cp"), 1)
                dve.wait_ge(S("sel_cp"), e * 2 + 2)
                for c, (t0, n) in enumerate(CHUNKS):
                    V_.tensor_scalar(SE[0:n, c, :], iota[0:n, :], SLS[0:n, c:c + 1], None, ALU.is_equal)\
                        .then_inc(S("sel_ready"), 1)
                V_.tensor_copy(small[:, 144:148], AFF[:, 0:4, bass.ds(e, 1)].rearrange("p c n -> p (c n)")).then_inc(S("aff_copied"), 1)
                V_.tensor_copy(small[0:META, 148:149], AFF[0:META, 4, bass.ds(e, 1)]).then_inc(S("aff_copied"), 1)

            def x_low(e, hf):
                dve.wait_ge(S("xgh_ready"), e * 2 + hf + 1)
                V_.tensor_tensor(XG[:, 1, 4 * hf:4 * hf + 4, :], PS[:, 6 + hf, 0:4 * CAP].rearrange("p (k n) -> p k n", k=4),
                                 XG[:, 0, 4 * hf:4 * hf + 4, :].bitcast(F32), SUB).then_inc(S("xgl_ready"), 1)

            def y_low(e, hf):
                dve.wait_ge(S("yeh_ready"), e * 2 + hf + 1)
                cols = slice(512 * hf, 512 * hf + 512)
                V_.scalar_tensor_tensor(YE[0:CAP, 1, cols], PS[0:CAP, 4 + hf, :], AFS[0:CAP], YE[0:CAP, 0, cols].bitcast(F32),
                                        MUL, SUB).then_inc(S("yel_ready"), 1)

            def add(e, m):
                dve.wait_ge(S("combined"), e * DT + m + 1)
                V_.tensor_tensor(tok(H[:, m, :], T2), tok(H[:, m, :], T2), PS[:, 4:6, 0:HT], ADD).then_inc(S("h_added"), 1)

            def expert(e, first=False, last=False):
                for q in range(PIECES):
                    i, kk = q // 4, q % 4
                    at = q - PBUF
                    if at == -1 and not first:
                        y_low(e - 1, 1)
                    if at - 1 in COMBINE_AT and not first:
                        add(e - 1, COMBINE_AT.index(at - 1))
                    if at >= 0 and at < 32 and at % 8 == 7:
                        b = at // 8
                        dve.wait_ge(S("w_used"), e * PIECES + at + 1)
                        dve.wait_ge(S("gate_act"), e * 4 + b + 1)
                        if not (first and b < 2):
                            dve.wait_ge(S("h_turned"), e * 4 + b - 1)
                        V_.tensor_tensor(HGS[0:CAP, b % 2, :], SIL[0:CAP, b % 2, :], PS[0:CAP, 2 * (b % 2) + 1, :], MUL)\
                            .then_inc(S("hgs_ready"), 1)
                    if at in TURN_H_AT:
                        b = TURN_H_AT.index(at)
                        dve.wait_ge(S("hgh_ready"), e * 4 + b + 1)
                        V_.tensor_tensor(HG[:, 1, 4 * b:4 * b + 4, :],
                                         PS[:, 6 + b % 2, 0:4 * CAP].rearrange("p (k n) -> p k n", k=4),
                                         HG[:, 0, 4 * b:4 * b + 4, :].bitcast(F32), SUB).then_inc(S("hgl_ready"), 1)
                    if at == SLOTS_AT:
                        dve.wait_ge(S("sat_turned"), e + 1)
                        if not first:
                            dve.wait_ge(S("yel_ready"), e * 2)
                        V_.tensor_copy(SAT[0:CAP, 0:512], PS[0:CAP, 6, :]).then_inc(S("sat_ready"), 1)
                        V_.tensor_copy(SAT[0:CAP, 512:T2], PS[0:CAP, 7, 0:META]).then_inc(S("sat_ready"), 1)
                        V_.tensor_copy(AFS[0:CAP], PS[0:CAP, 7, 256:257]).then_inc(S("sat_ready"), 1)
                        dve.wait_ge(S("sat_ready"), e * 3 + 3)
                    if at == SLOTS_AT + 1 and not last:
                        select(e + 1)
                    if at in TURN_X_AT and not last:
                        x_low(e + 1, TURN_X_AT.index(at))
                    if at == 43:
                        y_low(e, 0)
                    dve.wait_ge(S("wh_ready"), e * PIECES + q + 1)
                    V_.tensor_tensor(WS[:, 1, q % PBUF, :], ring[:, (EXP0 + i) % RING, PIECE * kk:PIECE * (kk + 1)],
                                     WS[:, 0, q % PBUF, :].bitcast(F32), SUB).then_inc(S("wl_ready"), 1)

            select(0)
            for hf in range(2):
                x_low(0, hf)
            expert(0, first=True)
            with dve.Fori(1, EXPERTS - 1) as e:
                expert(e)
            expert(EXPERTS - 1, last=True)
            y_low(EXPERTS - 1, 1)
            for m in range(DT):
                add(EXPERTS - 1, m)
            dve.wait_ge(S("h_added"), EXPERTS * DT)
            norm_apply("n7", lambda k: H[:, k, :], lambda k: H[:, k, :], "y_out")

        @blk.gpsimd
        def _(pool):
            G_ = nc.gpsimd
            MUL, SUB = ALU.mult, ALU.subtract

            def mask(buf, fill):
                for kb in range(QB):
                    v = buf[:, ZO[kb]:ZO[kb] + P]
                    last = G_.affine_select(out=v, in_=v, compare_op=ALU.is_gt, fill=fill, base=0,
                                            pattern=[[1, P]], channel_multiplier=-1)
                return last

            pool.wait_ge(S("consts_in"), 48)
            for i in range(SB_HEADS + 1):
                if i < SB_HEADS:
                    pool.wait_ge(S("rope_normed"), i + 1)
                    if i >= 2:
                        pool.wait_ge(S("rope_done"), i - 1)
                    G_.tensor_tensor(U[:, 2 + i % 2, 0:SEQ], QK[:, 8 + i, :], COS, MUL).then_inc(S("cos_part"), 1)
                    pool.wait_ge(S("sp_ready"), i + 1)
                    mask(SP[:, i % 2, :], 0.0).then_inc(S("sp_masked"), 1)
                if i >= 1:
                    pool.wait_ge(*freed(("c", i - 1)))
                    mask(Z[:, (i - 1) % 3, :], -BIG).then_inc(S("arg_masked"), 1)
            pool.wait_ge(*freed(("dn", DT - 1)))
            pool.dma_start(h_dram, H[:, :, :]).then_inc(S("h_saved"), 16)

            def bc(ap, n, w):
                return ap.unsqueeze(2).to_broadcast([n, GH, w])

            def scaled(dst, g, c, n, by, sem):
                G_.tensor_tensor(dst[0:n].rearrange("p (h w) -> p h w", h=GH),
                                 XS[0:n, c, :].rearrange("p (h w) -> p h w", h=GH), bc(by, n, HD), MUL)\
                    .then_inc(S(sem), 1)

            pool.wait_ge(S("h_saved"), 16)
            pool.wait_ge(S("w2_ready"), 1)
            for g in range(GROUPS):
                h8 = slice(GH * g, GH * g + GH)
                h8b = slice(32 + GH * g, 32 + GH * g + GH)
                pool.wait_ge(*freed(("tr", g, 4)))
                for s, c in enumerate(range(NC - 1, 0, -1)):
                    n = CHUNKS[c][1]
                    if s >= 2:
                        got(pool, ("sb", g, c + 2))
                    elif g > 0:
                        got(pool, ("sf", g - 1, 3))
                    scaled(XW[:, s % 2, :], g, c, n, W2[0:n, c, h8b], "xwb_ready")
                for c, (t0, n) in enumerate(CHUNKS):
                    i = NC * g + c
                    F = FR[i % 2]
                    pool.wait_ge(S(f"fr_in{i % 2}"), 32 * (i // 2 + 1))
                    G_.tensor_tensor(F[1][0:n, :, 0:n], F[1][0:n, :, 0:n], bc(FT[0:n, c, h8b], n, n), SUB)\
                        .then_inc(S("fr_shifted"), 1)
                    G_.tensor_tensor(F[0][0:n, :, 0:n], F[0][0:n, :, 0:n], bc(FT[0:n, c, h8], n, n), SUB)\
                        .then_inc(S("fr_shifted"), 1)
                    if i >= 1:
                        pool.wait_ge(*freed(("yd", (i - 1) // NC, (i - 1) % NC)))
                    scaled(XD, g, c, n, par[0:n, PARAMS["ssm_d"] + GH * g:PARAMS["ssm_d"] + GH * g + GH], "xd_ready")
                    if c < 4:
                        if c >= 2:
                            got(pool, ("sf", g, c - 2))
                        else:
                            got(pool, ("sb", g, 1))
                        scaled(XW[:, c % 2, :], g, c, n, W2[0:n, c, h8], "xwf_ready")
                    pool.wait_ge(S("min_ready"), i + 1)
                    pool.wait_ge(*freed(("cb", g, c)))
                    G_.tensor_tensor(F[1][0:n, :, 0:n], CBM[0:n, 1, 0:n].unsqueeze(1).to_broadcast([n, GH, n]),
                                     bc(DTT[0:n, c, h8b], n, n), MUL).then_inc(S("n1_ready"), 1)
                    pool.wait_ge(S("m_sum"), i + 1)
                    pool.wait_ge(S("e_ready"), i + 1)
                    G_.tensor_tensor(M1[0:n, :, 0:n], M1[0:n, :, 0:n], F[0][0:n, :, 0:n], MUL).then_inc(S("m_ready"), 1)
            got(pool, ("co", DT - 1))
            pool.wait_ge(S("h_saved"), 16)
            pool.dma_start(H[:, :, :], h_dram).then_inc(S("h_back"), 16)
            for c, (t0, n) in enumerate(CHUNKS):
                for hf in range(2):
                    pool.wait_ge(*freed(("xn", c, hf)))
                    pool.wait_ge(S("xnt_high"), 2 * c + hf + 1)
                    G_.tensor_tensor(XNT[0:n, 1, c, 512 * hf:512 * hf + 512], XGS[0:n, 512 * hf:512 * hf + 512],
                                     XNT[0:n, 0, c, 512 * hf:512 * hf + 512].bitcast(F32), SUB).then_inc(S("xnt_low"), 1)

        @blk.sync
        def _(sp):
            sp.dma_start(consts[:, :], inp["consts"]).then_inc(S("consts_in"), 16)
            sp.dma_start(par[:, :], inp["params"]).then_inc(S("consts_in"), 16)
            sp.dma_start(ROPE, inp["rope"].rearrange("p (a n) -> p a n", a=2)).then_inc(S("consts_in"), 16)

            def slot_free(n):
                tag = last_read[loads[n][0]]
                if tag[0] == "sem":
                    for sem, value in tag[1]:
                        sp.wait_ge(S(sem), value)
                else:
                    got(sp, tag)

            for n, (name, put) in enumerate(loads):
                if prev[n] is not None:
                    slot_free(prev[n])
                if name in AFTER_FFN:
                    got(sp, ("dn", DT - 1))
                if name == ("g1", 0):
                    sp.wait_ge(S("m_ready"), NC * GROUPS)
                for at, k, cols, src in put:
                    sp.dma_start(ring[:, slot_of[n], at:at + k * cols].rearrange("p (k n) -> p k n", k=k), src)\
                        .then_inc(S(f"ring{slot_of[n]}"), 16)

            def expert_load(e, i):
                s = (EXP0 + i) % RING
                if i < 8:
                    w = inp[("w_exp_gate_2", "w_exp_up_2")[i % 2]]
                    src = w[bass.ds(e, 1), :, (i // 2) * 512:(i // 2) * 512 + 512]
                else:
                    kh, ch = (i - 8) // 2, i % 2
                    src = inp["w_exp_down_2"][bass.ds(e, 1), kh * D:(kh + 1) * D, ch * 512:ch * 512 + 512]
                sp.dma_start(ring[:, s, :].rearrange("p (k n) -> p k n", k=DT),
                             src.rearrange("o (k p) n -> p (o k) n", p=P)).then_inc(S(f"ring{s}"), 16)

            def expert_read(e, i):
                sp.wait_ge(S("wh_ready"), e * PIECES + 4 * i + 4)
                sp.wait_ge(S("wl_ready"), e * PIECES + 4 * i + 4)
                sp.sem_inc(S("slots_turned"), 1)

            for i in range(RING):
                slot_free(max(j for j in range(N_DENSE) if slot_of[j] == (EXP0 + i) % RING))
                expert_load(0, i)
            with sp.Fori(0, EXPERTS - 1) as e:
                for i in range(RING, 12):
                    expert_read(e, i - RING)
                    expert_load(e, i)
                for i in range(RING):
                    expert_read(e, 12 - RING + i)
                    expert_load(e + 1, i)
            for i in range(RING, 12):
                expert_read(EXPERTS - 1, i - RING)
                expert_load(EXPERTS - 1, i)
            for k in range(DT):
                sp.wait_ge(S("y_out"), k + 1)
                sp.dma_start(out[k * P:(k + 1) * P, :], H[:, k, META:T2]).then_inc(S("stored"), 16)
            sp.wait_ge(S("stored"), 16 * DT)


WEIGHTS = ["w_in", "w_o", "w_gate", "w_up", "w_down", "w_in_2", "w_conf_out_2", "w_ssm_out_2", "w_out_2",
           "w_exp_gate_2", "w_exp_up_2", "w_exp_down_2"]


def shape_constants():
    i = np.arange(P)
    c = np.zeros((P, N_CONSTS), np.float32)
    put = lambda name, a: c.__setitem__((slice(None), slice(CONSTS[name], CONSTS[name] + a.shape[1])), a)
    put("ident", np.eye(P))
    put("ones", np.ones((P, P)))
    put("upper", (i[:, None] <= i[None, :]).astype(float))
    put("lower", (i[:, None] >= i[None, :]).astype(float))
    put("heads", (i[:, None] // HD == i[None, :] // HD).astype(float))
    rot = np.zeros((P, P))
    for h0 in (0, HD):
        for r in range(HD // 2):
            rot[h0 + HD // 2 + r, h0 + r] = -1.0
            rot[h0 + r, h0 + HD // 2 + r] = 1.0
    put("rot", rot)
    put("iota", np.broadcast_to(np.arange(CAP), (P, CAP)))
    put("causal", np.where(i[None, :] > i[:, None], -BIG, 0.0))
    freq = (np.float32(10000.0) ** (-np.arange(HD // 2, dtype=np.float32) / np.float32(HD // 2))).astype(np.float32)
    ang = (np.arange(SEQ, dtype=np.float32)[None, :] * freq[i % (HD // 2), None]).astype(np.float32).astype(np.float64)
    return c, np.concatenate([np.cos(ang), np.sin(ang)], axis=1).astype(np.float32)


def kernel(**inputs):
    import numpy as np
    import concourse.bacc as bacc
    from concourse.bass_utils import run_bass_kernel_spmd

    x = {k: np.asarray(v) for k, v in inputs.items()}
    par = np.zeros((P, N_PARAMS), np.float32)

    def put(name, a):
        a = a.reshape(a.shape[0], -1)
        par[:a.shape[1], PARAMS[name]:PARAMS[name] + a.shape[0]] = a.T

    tiles = lambda v: v.reshape(-1, P)
    put("attn_g", tiles(x["attn_norm_g"]))
    put("ffn_g", tiles(x["ffn_norm_g"]))
    put("mix_g", tiles(x["w_norm_mix_2"]))
    put("ffn2_g", tiles(x["w_norm_ffn_2"]))
    put("final_g", tiles(x["w_norm_final_2"]))
    put("subln_g", tiles(x["diff_subln_g"]))
    for name in ("q_g", "k_g"):
        g = x[f"diff_{name[0]}_norm_g"].reshape(-1)
        put(name, np.concatenate([g, g])[None])
    put("lam", np.stack([x[f"lambda_{n}"].reshape(-1) for n in ("q1", "k1", "q2", "k2")]))
    put("conf_w", x["w_conf_dw_2"][0].reshape(CONF_TAPS, DT, P).transpose(1, 0, 2).reshape(-1, P))
    put("conf_b", tiles(x["b_conf_dw_2"]))
    put("ln_g", tiles(x["conf_ln_g_2"]))
    put("ln_b", tiles(x["conf_ln_b_2"]))
    put("ssm_w", x["w_ssm_conv_2"][0].reshape(SSM_TAPS, 24, P).transpose(1, 0, 2).reshape(-1, P))
    put("ssm_b", tiles(x["b_ssm_conv_2"]))
    put("ssm_norm_g", tiles(x["w_ssm_norm_2"]))
    put("dt_bias", x["ssm_dt_bias_2"].reshape(1, 64))
    put("a_log", x["ssm_a_log_2"].reshape(1, 64))
    par[:, PARAMS["ssm_d"]:PARAMS["ssm_d"] + HEADS] = x["ssm_d_2"].reshape(1, HEADS)
    par[:, PARAMS["router"]:PARAMS["router"] + DT * EXPERTS] = \
        x["w_router_2"][0].reshape(DT, P, EXPERTS).transpose(1, 0, 2).reshape(P, -1)
    par[:, PARAMS["eps"]] = EPS
    par[:, PARAMS["subln_eps"]] = SUBLN_EPS
    par[:, PARAMS["one"]] = 1.0
    consts, rope = shape_constants()
    arrays = {"params": par, "consts": consts, "rope": rope,
              "h_t": np.ascontiguousarray(np.concatenate([x["meta_tokens_2"], x["x"][0]], axis=0).T)}
    for name in WEIGHTS:
        arrays[name] = np.ascontiguousarray(x[name][0])

    nc = bacc.Bacc("TRN2", target_bir_lowering=False, num_devices=1)
    inp = {k: nc.dram_tensor(k, a.shape, mybir.dt.from_np(a.dtype), kind="ExternalInput").ap() for k, a in arrays.items()}
    out = nc.dram_tensor("out_t", (D, SEQ), F32, kind="ExternalOutput").ap()
    program(nc, inp, out)
    r = run_bass_kernel_spmd(nc, [arrays], core_ids=[0])
    return np.ascontiguousarray(np.asarray(r.results[0]["out_t"]).T)[None]
```
